# Optimizing a Trainium2 kernel written in Bass

```python
import jax, jax.numpy as jnp
from jax import lax
import numpy as np

D_MODEL = 1024
BATCH = 1
SEQ = 256
DEPTH = 2
DEC_BATCH = 8
DEC_SEQ = 1
PAST_LEN = 2048
PAGE_SIZE = 128

PLE_DIM = 256
EPS = 1e-6
ROPE_BASE = 10000.0
CONV_DIM = 512
CONV_WIDTH = 31
CONV_STATE = CONV_WIDTH - 1
RET_HEADS = 4
RET_DK = 128
RET_DV = 256
RET_CHUNK = 128
MLA_HEADS = 8
MLA_Q_LORA = 384
MLA_KV_LORA = 256
MLA_NOPE = 64
MLA_ROPE = 32
MLA_V = 64
MLA_QK = MLA_NOPE + MLA_ROPE
MLA_QBLOCK = 128
D_FF = -(-8 * D_MODEL // (3 * 256)) * 256
IN_SIZES = (2 * CONV_DIM, RET_HEADS * RET_DK, RET_HEADS * RET_DK, RET_HEADS * RET_DV, RET_HEADS * RET_DV,
            MLA_Q_LORA, MLA_KV_LORA, MLA_ROPE, 3 * D_MODEL)
IN_DIM = sum(IN_SIZES)

kernel_name = 'hybrid_conv_retention_mla_decoder_step'

def rms_norm(x, g):
    xf = x.astype(jnp.float32)
    y = xf * lax.rsqrt(jnp.mean(xf * xf, axis=-1, keepdims=True) + EPS)
    return (y * g.astype(jnp.float32)).astype(x.dtype)

def layer_norm(x, g, b):
    xf = x.astype(jnp.float32)
    mu = jnp.mean(xf, axis=-1, keepdims=True)
    var = jnp.mean(jnp.square(xf - mu), axis=-1, keepdims=True)
    y = (xf - mu) * lax.rsqrt(var + EPS)
    return (y * g.astype(jnp.float32) + b.astype(jnp.float32)).astype(x.dtype)

def rope(x, pos):
    half = x.shape[-1] // 2
    inv = ROPE_BASE ** (-jnp.arange(half, dtype=jnp.float32) / half)
    ang = pos.astype(jnp.float32)[:, None] * inv[None, :]
    c = jnp.cos(ang)[:, None, :]
    s = jnp.sin(ang)[:, None, :]
    x1 = x[..., :half].astype(jnp.float32)
    x2 = x[..., half:].astype(jnp.float32)
    return jnp.concatenate([x1 * c - x2 * s, x1 * s + x2 * c], axis=-1).astype(x.dtype)

def causal_dwconv(u_ext, w, b):
    y = lax.conv_general_dilated(u_ext, w[:, None, :].astype(u_ext.dtype), window_strides=(1,), padding='VALID',
                                 dimension_numbers=('NWC', 'WIO', 'NWC'), feature_group_count=u_ext.shape[-1])
    return y + b.astype(y.dtype)

def conv_branch(glu_in, prefix, w_dw, b_dw, g_ln, b_ln, w_proj):
    a, gate = jnp.split(glu_in, 2, axis=-1)
    u = a * jax.nn.sigmoid(gate)
    u_ext = jnp.concatenate([prefix.astype(u.dtype), u], axis=1)
    y = jax.nn.silu(layer_norm(causal_dwconv(u_ext, w_dw, b_dw), g_ln, b_ln))
    return y @ w_proj, u_ext[:, -CONV_STATE:]

def retention_log_decay():
    return jnp.log(1.0 - 2.0 ** (-5.0 - jnp.arange(RET_HEADS, dtype=jnp.float32)))

def retention_chunk(S, q, k, v, log_gamma):
    C = q.shape[1]
    idx = jnp.arange(C, dtype=jnp.float32)
    diff = idx[:, None] - idx[None, :]
    decay = jnp.where(diff >= 0, jnp.exp(jnp.maximum(diff, 0.0)[None] * log_gamma[:, None, None]), 0.0)
    scores = jnp.einsum('bihd,bjhd->bhij', q, k) * decay[None]
    o = jnp.einsum('bhij,bjhe->bihe', scores, v)
    cross = jnp.exp((idx + 1.0)[:, None] * log_gamma[None, :])
    o = o + jnp.einsum('bihd,bhde->bihe', q, S) * cross[None, :, :, None]
    kdec = jnp.exp((C - 1.0 - idx)[:, None] * log_gamma[None, :])
    S_new = jnp.exp(C * log_gamma)[None, :, None, None] * S + jnp.einsum('bjhd,bjhe->bhde', k * kdec[None, :, :, None], v)
    return S_new, o

def retention_prompt(q, k, v, log_gamma):
    B, T, H, dk = q.shape
    dv = v.shape[-1]
    n = T // RET_CHUNK
    to_chunks = lambda a: jnp.moveaxis(a.reshape(B, n, RET_CHUNK, H, a.shape[-1]), 1, 0)
    S0 = jnp.zeros((B, H, dk, dv), jnp.float32)
    S, o = lax.scan(lambda s, c: retention_chunk(s, c[0], c[1], c[2], log_gamma), S0,
                    (to_chunks(q), to_chunks(k), to_chunks(v)))
    return S, jnp.moveaxis(o, 0, 1).reshape(B, T, H, dv)

def head_group_norm(o, g):
    of = o.astype(jnp.float32)
    mu = jnp.mean(of, axis=-1, keepdims=True)
    var = jnp.mean(jnp.square(of - mu), axis=-1, keepdims=True)
    y = ((of - mu) * lax.rsqrt(var + EPS)).reshape(o.shape[0], o.shape[1], -1)
    return y * g.astype(jnp.float32)

def mla_keys_values(c_kv, k_pe, w_uk, w_uv, g_kn):
    B, L, _ = c_kv.shape
    k_nope = (c_kv @ w_uk).reshape(B, L, MLA_HEADS, MLA_NOPE)
    k = jnp.concatenate([k_nope, jnp.broadcast_to(k_pe[:, :, None, :], (B, L, MLA_HEADS, MLA_ROPE)).astype(k_nope.dtype)], axis=-1)
    k = rms_norm(k, g_kn)
    v = (c_kv @ w_uv).reshape(B, L, MLA_HEADS, MLA_V)
    return k, v

def attend(q, k, v, q_pos, k_pos):
    s = jnp.einsum('bqhd,bkhd->bhqk', q, k, preferred_element_type=jnp.float32) * (MLA_QK ** -0.5)
    s = jnp.where(k_pos[None, None, None, :] <= q_pos[None, None, :, None], s, -1e30)
    p = jax.nn.softmax(s, axis=-1).astype(v.dtype)
    return jnp.einsum('bhqk,bkhd->bqhd', p, v)

def attend_blocked(q, k, v, pos):
    B, T, H, d = q.shape
    nb = T // MLA_QBLOCK
    qb = jnp.moveaxis(q.reshape(B, nb, MLA_QBLOCK, H, d), 1, 0)
    pb = pos.reshape(nb, MLA_QBLOCK)
    ob = lax.map(lambda a: attend(a[0], k, v, a[1], pos), (qb, pb))
    return jnp.moveaxis(ob, 0, 1).reshape(B, T, H, v.shape[-1])

def decoder_layer(x, p_l, pos, conv_prefix, ret_state, past_ckv, past_kpe, W, l, is_prompt):
    B, T, _ = x.shape
    h = rms_norm(x, W['g_mix'][l])
    z = h @ W['w_in'][l]
    split_idx = np.cumsum(IN_SIZES)[:-1].tolist()
    glu_in, rq, rk, rv, rg, q_a, kv_a, k_r, gates = jnp.split(z, split_idx, axis=-1)

    y_a, conv_new = conv_branch(glu_in, conv_prefix, W['w_dw'][l], W['b_dw'][l], W['g_cln'][l], W['b_cln'][l], W['w_conv_out'][l])

    log_gamma = retention_log_decay()
    q = rope(rq.reshape(B, T, RET_HEADS, RET_DK), pos)
    k = rope(rk.reshape(B, T, RET_HEADS, RET_DK), pos) * (RET_DK ** -0.5)
    v = rv.reshape(B, T, RET_HEADS, RET_DV)
    if is_prompt:
        S_new, o = retention_prompt(q, k, v, log_gamma)
    else:
        S_new, o = retention_chunk(ret_state.astype(jnp.float32), q, k, v, log_gamma)
    o = head_group_norm(o, W['g_rgn'][l]).astype(x.dtype)
    y_b = (o * jax.nn.silu(rg)) @ W['w_ret_out'][l]

    c_q = rms_norm(q_a, W['g_qa'][l])
    qm = (c_q @ W['w_uq'][l]).reshape(B, T, MLA_HEADS, MLA_QK)
    qm = jnp.concatenate([qm[..., :MLA_NOPE], rope(qm[..., MLA_NOPE:], pos)], axis=-1)
    qm = rms_norm(qm, W['g_qn'][l])
    c_kv = rms_norm(kv_a, W['g_kva'][l])
    k_pe = rope(k_r[:, :, None, :], pos)[:, :, 0, :]
    if is_prompt:
        km, vm = mla_keys_values(c_kv, k_pe, W['w_uk'][l], W['w_uv'][l], W['g_kn'][l])
        om = attend_blocked(qm, km, vm, pos)
    else:
        past_len = past_ckv.shape[1]
        all_ckv = jnp.concatenate([past_ckv.astype(c_kv.dtype), c_kv], axis=1)
        all_kpe = jnp.concatenate([past_kpe.astype(k_pe.dtype), k_pe], axis=1)
        k_pos = jnp.concatenate([jnp.arange(past_len, dtype=jnp.int32), pos])
        km, vm = mla_keys_values(all_ckv, all_kpe, W['w_uk'][l], W['w_uv'][l], W['g_kn'][l])
        om = attend(qm, km, vm, pos, k_pos)
    y_c = om.reshape(B, T, MLA_HEADS * MLA_V) @ W['w_mla_out'][l]

    g_a, g_b, g_c = jnp.split(jax.nn.sigmoid(gates), 3, axis=-1)
    x = x + (g_a * y_a + g_b * y_b + g_c * y_c) @ W['w_out'][l]

    hf = rms_norm(x, W['g_ffn'][l])
    x = x + (jax.nn.silu(hf @ W['w_gate'][l]) * (hf @ W['w_up'][l])) @ W['w_down'][l]

    pg = jax.nn.sigmoid(rms_norm(x, W['g_ple'][l]) @ W['w_ple_gate'][l])
    x = x + pg * (p_l @ W['w_ple_proj'][l])
    return x, c_kv, k_pe, S_new, conv_new

def setup_inputs(seed: int = 0) -> dict:
    key = jax.random.key(seed)
    ks = iter(jax.random.split(key, 48))
    f32 = jnp.float32

    def nrm(shape, scale):
        return scale * jax.random.normal(next(ks), shape, f32)

    def gain(n):
        return 1.0 + nrm((DEPTH, n), 0.02)

    n_pages = PAST_LEN // PAGE_SIZE
    n_used = DEC_BATCH * n_pages
    n_phys = n_used + max(1, n_used // 4)
    d = D_MODEL
    inp = {}
    inp['x_prompt'] = nrm((BATCH, SEQ, d), 1.0)
    inp['x_sample'] = nrm((DEC_BATCH, DEC_SEQ, d), 1.0)
    inp['p_prompt'] = nrm((DEPTH, BATCH, SEQ, PLE_DIM), 1.0)
    inp['p_sample'] = nrm((DEPTH, DEC_BATCH, DEC_SEQ, PLE_DIM), 1.0)
    inp['cache_ckv'] = nrm((DEPTH, n_phys, PAGE_SIZE, MLA_KV_LORA), 1.0)
    inp['cache_kpe'] = nrm((DEPTH, n_phys, PAGE_SIZE, MLA_ROPE), 1.0)
    inp['state_ret'] = nrm((DEPTH, DEC_BATCH, RET_HEADS, RET_DK, RET_DV), 0.5)
    inp['state_conv'] = nrm((DEPTH, DEC_BATCH, CONV_STATE, CONV_DIM), 0.5)
    inp['page_table'] = jax.random.permutation(next(ks), n_phys)[:n_used].reshape(DEC_BATCH, n_pages).astype(jnp.int32)
    inp['g_mix'] = gain(d)
    inp['w_in'] = nrm((DEPTH, d, IN_DIM), d ** -0.5)
    inp['w_dw'] = nrm((DEPTH, CONV_WIDTH, CONV_DIM), CONV_WIDTH ** -0.5)
    inp['b_dw'] = nrm((DEPTH, CONV_DIM), 0.02)
    inp['g_cln'] = gain(CONV_DIM)
    inp['b_cln'] = nrm((DEPTH, CONV_DIM), 0.02)
    inp['w_conv_out'] = nrm((DEPTH, CONV_DIM, d), CONV_DIM ** -0.5)
    inp['g_rgn'] = gain(RET_HEADS * RET_DV)
    inp['w_ret_out'] = nrm((DEPTH, RET_HEADS * RET_DV, d), (RET_HEADS * RET_DV) ** -0.5)
    inp['g_qa'] = gain(MLA_Q_LORA)
    inp['w_uq'] = nrm((DEPTH, MLA_Q_LORA, MLA_HEADS * MLA_QK), MLA_Q_LORA ** -0.5)
    inp['g_qn'] = gain(MLA_QK)
    inp['g_kva'] = gain(MLA_KV_LORA)
    inp['w_uk'] = nrm((DEPTH, MLA_KV_LORA, MLA_HEADS * MLA_NOPE), MLA_KV_LORA ** -0.5)
    inp['w_uv'] = nrm((DEPTH, MLA_KV_LORA, MLA_HEADS * MLA_V), MLA_KV_LORA ** -0.5)
    inp['g_kn'] = gain(MLA_QK)
    inp['w_mla_out'] = nrm((DEPTH, MLA_HEADS * MLA_V, d), (MLA_HEADS * MLA_V) ** -0.5)
    inp['w_out'] = nrm((DEPTH, d, d), d ** -0.5)
    inp['g_ffn'] = gain(d)
    inp['w_gate'] = nrm((DEPTH, d, D_FF), d ** -0.5)
    inp['w_up'] = nrm((DEPTH, d, D_FF), d ** -0.5)
    inp['w_down'] = nrm((DEPTH, D_FF, d), D_FF ** -0.5)
    inp['g_ple'] = gain(d)
    inp['w_ple_gate'] = nrm((DEPTH, d, d), d ** -0.5)
    inp['w_ple_proj'] = nrm((DEPTH, PLE_DIM, d), PLE_DIM ** -0.5)
    return inp

def reference(x_prompt, x_sample, p_prompt, p_sample, cache_ckv, cache_kpe, state_ret, state_conv, page_table,
              g_mix, w_in, w_dw, b_dw, g_cln, b_cln, w_conv_out, g_rgn, w_ret_out, g_qa, w_uq, g_qn, g_kva,
              w_uk, w_uv, g_kn, w_mla_out, w_out, g_ffn, w_gate, w_up, w_down, g_ple, w_ple_gate, w_ple_proj):
    W = dict(g_mix=g_mix, w_in=w_in, w_dw=w_dw, b_dw=b_dw, g_cln=g_cln, b_cln=b_cln, w_conv_out=w_conv_out,
             g_rgn=g_rgn, w_ret_out=w_ret_out, g_qa=g_qa, w_uq=w_uq, g_qn=g_qn, g_kva=g_kva, w_uk=w_uk,
             w_uv=w_uv, g_kn=g_kn, w_mla_out=w_mla_out, w_out=w_out, g_ffn=g_ffn, w_gate=w_gate, w_up=w_up,
             w_down=w_down, g_ple=g_ple, w_ple_gate=w_ple_gate, w_ple_proj=w_ple_proj)
    Bp, Tp, _ = x_prompt.shape
    Bs, Ts, _ = x_sample.shape
    past_len = page_table.shape[1] * cache_ckv.shape[2]
    pos_p = jnp.arange(Tp, dtype=jnp.int32)
    pos_s = past_len + jnp.arange(Ts, dtype=jnp.int32)
    conv_zero = jnp.zeros((Bp, CONV_STATE, CONV_DIM), x_prompt.dtype)

    xp, xs = x_prompt, x_sample
    ckv_p, kpe_p, ret_p, conv_p = [], [], [], []
    ckv_s, kpe_s, ret_s, conv_s = [], [], [], []
    for l in range(DEPTH):
        xp, a, b, c, e = decoder_layer(xp, p_prompt[l], pos_p, conv_zero, None, None, None, W, l, True)
        ckv_p.append(a); kpe_p.append(b); ret_p.append(c); conv_p.append(e)
        past_ckv = cache_ckv[l][page_table].reshape(Bs, past_len, MLA_KV_LORA)
        past_kpe = cache_kpe[l][page_table].reshape(Bs, past_len, MLA_ROPE)
        xs, a, b, c, e = decoder_layer(xs, p_sample[l], pos_s, state_conv[l], state_ret[l], past_ckv, past_kpe, W, l, False)
        ckv_s.append(a); kpe_s.append(b); ret_s.append(c); conv_s.append(e)

    return (xp, xs, jnp.stack(ckv_p), jnp.stack(kpe_p), jnp.stack(ckv_s), jnp.stack(kpe_s),
            jnp.stack(ret_p), jnp.stack(ret_s), jnp.stack(conv_p), jnp.stack(conv_s))


_drawn_inputs = setup_inputs


def setup_inputs(seed=0):
    import zlib

    import numpy as np

    out = dict(_drawn_inputs(seed))
    spreads = {}
    factors = {'cache_kpe': 4.495,
     'b_dw': 2.99,
     'g_cln': 5.572,
     'b_cln': 6.739,
     'g_rgn': 7.107,
     'g_qa': 8.0,
     'g_qn': 8.0,
     'g_kva': 2.929,
     'g_kn': 8.0,
     'g_ffn': 3.243,
     'g_ple': 8.0}
    for name, (base, spread) in spreads.items():
        noise = np.random.default_rng([zlib.crc32(name.encode()), seed]).standard_normal(out[name].shape)
        drawn = base * np.exp(spread * noise) if base else spread * noise
        out[name] = __import__('jax').numpy.asarray(drawn.astype(out[name].dtype))
    for name, factor in factors.items():
        out[name] = (out[name] * factor).astype(out[name].dtype)
    return out
```

```python
from contextlib import ExitStack

import numpy as np
import concourse.bass as bass
from concourse import mybir

F32 = mybir.dt.float32
F32R = mybir.dt.float32r
I32 = mybir.dt.int32
ALU = mybir.AluOpType
ACT = mybir.ActivationFunctionType
AX = mybir.AxisListType
ds = bass.ds

P = 128
DEPTH, D, TP, NB = 2, 1024, 256, 8
T = TP + NB
KT = D // P
EPS = 1e-6
CONV, TAPS = 512, 31
CT = CONV // P
HR, DK, DV = 4, 128, 256
HM, NOPE, ROPE, VD = 8, 64, 32, 64
QK = NOPE + ROPE
QL, KVL = 384, 256
PAST, PAGE = 2048, 128
NT = PAST // PAGE
FF = 2816
FT = FF // P
PLE = 256
ATT_SCALE = QK ** -0.5

STAGES = [("glu", 8, 8), ("qk", 8, 8), ("v", 8, 8), ("rg", 8, 8), ("gate_a", 8, 8), ("conv_out", 4, 8),
          ("gate_b", 8, 8), ("ret_out", 8, 8), ("kvq", 6, 6), ("uq", 3, 8), ("gate_c", 8, 8), ("mla_out", 4, 8),
          ("w_out", 8, 8), ("ffn_in", 2 * FT, 2 * FT), ("ffn_out", FT, 8), ("ple_gate", 8, 8), ("ple_proj", 2, 8)]
B0, C0 = {}, {}
NBLK = NCHUNK = 0
for _name, _b, _c in STAGES:
    B0[_name], C0[_name] = NBLK, NCHUNK
    NBLK += _b
    NCHUNK += _c
RING = 4
UQ_HEADS = (3, 3, 2)

TAB = {}
_n = 0
for _name, _w in (("rope_c", 2 * T), ("rope_s", 2 * T), ("decay", HR * 384), ("mask", 384), ("mla_c", T), ("mla_s", T),
                  ("ident", P), ("ones", P), ("rot", QK), ("kdec", 2 * HR)):
    TAB[_name] = _n
    _n += _w
NTAB = _n
VEC = {}
_n = 0
for _name, _w in (("g_mix", KT), ("g_ffn", KT), ("g_ple", KT), ("w_dw", CT * 32), ("b_dw", CT), ("g_cln", CT),
                  ("b_cln", CT), ("g_rgn", KT), ("g_qa", 3), ("g_kva", 2), ("g_qn", 1), ("g_kn", 1)):
    VEC[_name] = _n
    _n += _w
NVEC = _n

GAMMA = [1.0 - 2.0 ** (-5.0 - h) for h in range(HR)]


def build(nc, x_in, p_in, stream, uk_in, uv_in, ukt_in, vec_in, tab_in, ckv_in, kpe_in, pages_in, state_in, conv_in,
          y_out, ckv_out, kpe_out, ret_prompt_out, ret_sample_out, conv_prompt_out, conv_sample_out):
    ctx = ExitStack()
    with ctx:
        base = -(-nc.sbuf_base // 32) * 32
        top = [0]
        names = {}

        def at_offset(name, cols, offset, dt=F32, shape=None):
            names[name] = (offset, cols * 4)
            return nc.alloc_sbuf_tensor_at(name, [P] + (shape or [cols]), dt, offset=base + offset)

        def place(name, shape, dt=F32):
            cols = int(np.prod(shape))
            off = top[0]
            top[0] += -(-cols * 4 // 32) * 32
            return at_offset(name, cols, off, dt, list(shape))

        xT = place("xT", [KT, T])
        h_hi = place("h_hi", [KT, T], F32R)
        h_lo = place("h_lo", [KT, T], F32R)
        w_raw = [place(f"w_raw{r}", [8 * P]) for r in range(RING)]
        w_hi = [place(f"w_hi{r}", [8 * P], F32R) for r in range(RING)]
        w_lo = [place(f"w_lo{r}", [8 * P], F32R) for r in range(RING)]
        tab = place("tab", [NTAB])
        vecs = place("vecs", [DEPTH, NVEC])
        vec = place("vec", [NVEC])
        pages = place("pages", [NB * NT], I32)
        uk = place("uk", [2, 512])
        uv = place("uv", [2, 512])
        off_ukh = top[0]
        uk_hi = place("uk_hi", [2, 512], F32R)
        uk_lo = place("uk_lo", [2, 512], F32R)
        off_ukt = top[0]
        uk_t = place("uk_t", [HM, 256])
        zt = place("zt", [4, T])
        et = place("et", [4, T])
        rstd = place("rstd", [T])
        rsb = place("rsb", [2, T])
        p_raw = place("p_raw", [2, T])
        kpe_own = place("kpe_own", [T])
        ckv_own = place("ckv_own", [2, NB])
        own = place("own", [HM, NB])
        qt_hi = place("qt_hi", [NB, 2, HM], F32R)
        qt_lo = place("qt_lo", [NB, 2, HM], F32R)
        qpe4 = place("qpe4", [NB, HM])
        lat = place("lat", [2, HM, NB])
        small = place("small", [96])
        q_hi = [place(f"q_hi{i}", [2, HM], F32R) for i in range(2)]
        q_lo = [place(f"q_lo{i}", [2, HM], F32R) for i in range(2)]
        q_pe = [place(f"q_pe{i}", [4, HM]) for i in range(2)]
        off_mix = top[0]
        mix = place("mix", [KT, T])
        off_g = top[0]
        gate = place("gate", [KT, T])
        off_s = top[0]
        s_hi = place("s_hi", [KT, T], F32R)
        s_lo = place("s_lo", [KT, T], F32R)
        off_u = top[0]
        a_hi = at_offset("a_hi", FT * T, off_g, F32R, [FT, T])
        a_lo = at_offset("a_lo", FT * T, off_g + FT * T * 4, F32R, [FT, T])
        p_hi = at_offset("p_hi", 2 * T, off_s, F32R, [2, T])
        p_lo = at_offset("p_lo", 2 * T, off_s + 2 * T * 4, F32R, [2, T])
        yconv = at_offset("yconv", CT * T, off_mix, F32, [CT, T])
        o = off_u
        u_ext = at_offset("u_ext", CT * 288, o, F32, [CT, 288])
        u_smp = at_offset("u_smp", CT * NB * 31, o + CT * 288 * 4, F32, [CT, NB, 31])
        oT = at_offset("oT", KT * T, o, F32, [KT, T])
        o += CT * 288 * 4 + CT * NB * 31 * 4
        qk = at_offset("qk", KT * T, o, F32, [KT, T]); o += KT * T * 4
        v_nat = at_offset("v_nat", 2 * 1024, o, F32, [2, 1024]); o += 8192
        v_smp = at_offset("v_smp", 1024, o, F32, [1024])
        conv_stage = at_offset("conv_stage", CT * NB * 30, o, F32, [CT, NB, 30]); o += 4096
        k_nat = at_offset("k_nat", 2 * 512, o, F32, [2, 512]); o += 4096
        k_smp = at_offset("k_smp", 512, o, F32, [512]); o += 2048
        rgs = at_offset("rgs", KT * T, o, F32, [KT, T])
        conv_prod = at_offset("conv_prod", CT * NB * 31, o, F32, [CT, NB, 31])
        conv_new = at_offset("conv_new", CT * NB * 30, o + CT * NB * 31 * 4, F32, [CT, NB, 30]); o += KT * T * 4
        end1 = o
        state = [at_offset(f"state{i}", 1024, off_ukt + 4096 * i, F32, [HR, DV]) for i in range(2)]
        sT = [at_offset(f"sT{i}", 384, off_ukh + 1536 * i, F32, [384]) for i in range(2)]
        k_mask = [at_offset(f"k_mask{i}", 512, off_ukh + 3072 + 2048 * i, F32, [512]) for i in range(2)]
        ret_stage = at_offset("ret_stage", 1024, names["zt"][0], F32, [HR, DV])
        ckv = [at_offset(f"ckv{i}", NT * KVL, off_u + 16384 * i, F32, [NT, KVL]) for i in range(2)]
        kpe = [at_offset(f"kpe{i}", NT * ROPE, off_u + 32768 + 2048 * i, F32, [NT, ROPE]) for i in range(2)]
        o = off_u + 36864
        vm = at_offset("vm", 2 * 512, o, F32, [2, 512])
        sq = [at_offset(f"sq{i}", 512, o + 2048 * i, F32, [HM, 64]) for i in range(2)]
        end2 = o + 4096
        qm = at_offset("qm", HM * T, off_g, F32, [HM, T])
        sqg = at_offset("sqg", 5 * T, off_g, F32, [5, T])
        qa_hi = at_offset("qa_hi", 3 * T, off_s, F32R, [3, T])
        qa_lo = at_offset("qa_lo", 3 * T, off_s + 3 * T * 4, F32R, [3, T])
        ckvT = at_offset("ckvT", 2 * T, off_s + 6 * T * 4, F32, [2, T])
        km = at_offset("km", HM * T, off_s + 8 * T * 4, F32, [HM, T])
        ap_s = [at_offset(f"ap_s{i}", 384, off_ukh + 1536 * i, F32, [384]) for i in range(2)]
        ap_t = [at_offset(f"ap_t{i}", 384, off_ukh + 3072 + 1536 * i, F32, [384]) for i in range(2)]
        oM = at_offset("oM", 4 * T, names["zt"][0], F32, [4, T])
        ct_hi = [at_offset(f"ct_hi{i}", 512, off_s + 4096 * i, F32R, [4, P]) for i in range(2)]
        ct_lo = [at_offset(f"ct_lo{i}", 512, off_s + 4096 * i + 2048, F32R, [4, P]) for i in range(2)]
        kpeT = at_offset("kpeT", 512, off_s + 8192, F32, [4, P])
        o = off_g
        ssq = [at_offset(f"ssq{i}", NT * HM, o + 512 * i, F32, [NT, HM]) for i in range(2)]
        sspe = [at_offset(f"sspe{i}", NT, o + 1024 + 64 * i, F32, [NT]) for i in range(2)]
        kn_r = at_offset("kn_r", NT * HM, o + 1152, F32, [NT, HM])
        sc = at_offset("sc", NT * HM, o + 1664, F32, [NT, HM])
        pr = at_offset("pr", NT * HM, o + 2176, F32, [NT, HM])
        cv_hi, cv_lo = s_hi, s_lo
        a_end = off_g + 2 * FT * T * 4
        total = max(end1, end2, a_end)
        assert base + total <= nc.sbuf_usable_end, (base, total, end1, end2, a_end, nc.sbuf_usable_end)
        ctx.enter_context(nc.sbuf_tensor("arena", [P, (base + total - nc.sbuf_base) // 4 + 1], F32))

        bank = [ctx.enter_context(nc.psum_tensor(f"bank{i}", [P, 512], F32)) for i in range(8)]

        DMA = 16

        class Sem:

            def __init__(self, name, per=1, credit=0):
                self.s = ctx.enter_context(nc.semaphore(name))
                self.per, self.credit = per, credit

            def at(self, l, n):
                return l * self.per + (n + self.credit)

        settled = {e: Sem(f"settled_{i}") for i, e in enumerate((nc.sync.engine, nc.gpsimd.engine, nc.tensor.engine, nc.vector.engine))}

        def settle(eng):
            eng.sem_inc(settled[eng.engine].s, 1)

        class Steps:

            def __init__(self):
                self.n = 0

            def one(self):
                self.n += 1
                return 1

        def col(name, k=0):
            return vec[:, VEC[name] + k:VEC[name] + k + 1]

        def tb(name, w, a=0, rows=slice(0, P)):
            return tab[rows, TAB[name] + a:TAB[name] + a + w]

        ident = tb("ident", P)
        ones = tb("ones", P)

        tables_loaded = Sem("tables_loaded")
        w_loaded = [Sem(f"w_loaded{r}", 16 * ((NBLK - r + RING - 1) // RING)) for r in range(RING)]
        w_split = Sem("w_split", NBLK, 1)
        w_high = Sem("w_high", NBLK)
        w_begun = Sem("w_begun", NBLK)
        chunk_ready = Sem("chunk_ready", NCHUNK)
        chunk_free = Sem("chunk_free", NCHUNK, 4)
        h_high = Sem("h_high", 3 * KT)
        h_low = Sem("h_low", 3 * KT)
        x_sq = Sem("x_sq", 3 * KT)
        x_sum = Sem("x_sum", 3 * KT)
        x_root = Sem("x_root", 3)
        rstd_ready = Sem("rstd_ready", 3)
        NEXP = 4 + 8 + 24 + FT + 8
        exp_ready = Sem("exp_ready", NEXP)
        E0 = {"glu": 0, "rg": 4, "gate_a": 12, "gate_b": 20, "gate_c": 28, "ffn_in": 36, "ple_gate": 36 + FT}
        vec_ready = Sem("vec_ready")
        conv_state_loaded = Sem("conv_state_loaded", 16)
        conv_state_placed = Sem("conv_state_placed")
        conv_biased = Sem("conv_biased")
        u_ready = Sem("u_ready")
        conv_new_ready = Sem("conv_new_ready")
        conv_stored = Sem("conv_stored", 32)
        rope_ready = Sem("rope_ready", 2)
        k_turned = Sem("k_turned")
        k_copied = Sem("k_copied")
        v_turned = Sem("v_turned", 2)
        v_copied = Sem("v_copied", 2, 1)
        conv_done = Sem("conv_done")
        cln_sum = Sem("cln_sum", 2)
        cln_centred = Sem("cln_centred")
        cln_sq = Sem("cln_sq")
        cln_root = Sem("cln_root")
        cln_y = Sem("cln_y")
        cln_exp = Sem("cln_exp")
        conv_act = Sem("conv_act")
        conv_high = Sem("conv_high")
        conv_split = Sem("conv_split")
        ret_s = Sem("ret_s", HR)
        ret_sd = Sem("ret_sd", HR)
        ret_o = Sem("ret_o", HR)
        ret_oc = Sem("ret_oc", HR)
        ret_st = Sem("ret_st", HR)
        ret_stc = Sem("ret_stc", HR)
        ret_stored = Sem("ret_stored", 16)
        st_loaded = [Sem(f"st_loaded{i}", 64) for i in range(2)]
        st_stored = [Sem(f"st_stored{i}", 64) for i in range(2)]
        st_mask = Sem("st_mask", NB)
        st_outer = Sem("st_outer", NB)
        st_new = Sem("st_new", NB)
        st_o = Sem("st_o", NB)
        st_oc = Sem("st_oc", NB)
        gn_sum = Sem("gn_sum", HR)
        gn_c = Sem("gn_c", HR)
        gn_sq = Sem("gn_sq", HR)
        gn_var = Sem("gn_var", HR)
        gn_root = Sem("gn_root", HR)
        gn_y = Sem("gn_y", HR)
        gn_high = Sem("gn_high", HR)
        gn_low = Sem("gn_low", HR)
        mla_w_loaded = Sem("mla_w_loaded", 48)
        ukt_loaded = Sem("ukt_loaded", 16)
        kvq_act = Sem("kvq_act", 5)
        qa_low = Sem("qa_low")
        kvq_sum = Sem("kvq_sum", 2)
        kvq_root = Sem("kvq_root", 2)
        kvq_r = Sem("kvq_r", 2)
        ckv_ready = Sem("ckv_ready")
        kr_rot = Sem("kr_rot")
        kpe_ready = Sem("kpe_ready")
        own_stored = Sem("own_stored", 32)
        uq_rot = Sem("uq_rot", HM)
        q_roped = Sem("q_roped", HM)
        hn_sq = Sem("hn_sq", 2 * HM)
        hn_sum = Sem("hn_sum", 2 * HM)
        hn_root = Sem("hn_root", 2 * HM)
        hn_done = Sem("hn_done", 2 * HM)
        kn_ready = Sem("kn_ready", HM)
        kn_copied = Sem("kn_copied", HM)
        vm_ready = Sem("vm_ready")
        vm_copied = Sem("vm_copied")
        own_prod = Sem("own_prod")
        qg_ready = Sem("qg_ready")
        own_sum = Sem("own_sum")
        own_copied = Sem("own_copied")
        qt_ready = Sem("qt_ready")
        qt_high = Sem("qt_high")
        qt_low = Sem("qt_low")
        at_s = Sem("at_s", HM)
        at_m = Sem("at_m", HM)
        at_p = Sem("at_p", HM)
        at_n = Sem("at_n", HM)
        at_t = Sem("at_t", HM)
        at_tc = Sem("at_tc", HM)
        at_o = Sem("at_o", HM)
        at_oc = Sem("at_oc", HM)
        uk_high = Sem("uk_high")
        uk_low = Sem("uk_low")
        ck_loaded = [Sem(f"ck_loaded{i}", 4 * 32 * NT) for i in range(2)]
        c_kt = Sem("c_kt", NB)
        c_ktc = Sem("c_ktc", NB)
        c_ksq = Sem("c_ksq", NB)
        c_kss = Sem("c_kss", NB)
        c_q = Sem("c_q", NB)
        q_pe_zeroed = Sem("q_pe_zeroed")
        c_tr = Sem("c_tr", NB * 8)
        c_hi = Sem("c_hi", NB * 8)
        c_lo = Sem("c_lo", NB * 8)
        c_kn = Sem("c_kn", NB * NT)
        c_sq = Sem("c_sq", NB * NT)
        c_ss = Sem("c_ss", NB * NT)
        c_sc = Sem("c_sc", NB)
        t_tot = Sem("t_tot", NB)
        t_root = Sem("t_root", NB)
        t_s = Sem("t_s", NB)
        t_mx = Sem("t_mx", NB)
        t_mt = Sem("t_mt", NB)
        t_dg = Sem("t_dg", NB)
        t_bc = Sem("t_bc", NB)
        t_shift = Sem("t_shift", NB)
        t_p = Sem("t_p", NB)
        t_l = Sem("t_l", NB)
        t_lat = Sem("t_lat", NB)
        t_fin = Sem("t_fin", NB)
        uvs_ready = Sem("uvs_ready")
        uvs_copied = Sem("uvs_copied")
        mla_high = Sem("mla_high")
        mla_split = Sem("mla_split")
        mix_done = Sem("mix_done", KT)
        mix_high = Sem("mix_high", KT)
        mix_low = Sem("mix_low", KT)
        ffn_a = Sem("ffn_a", FT)
        ffn_high = Sem("ffn_high", FT)
        ffn_low = Sem("ffn_low", FT)
        p_high = Sem("p_high")
        p_low = Sem("p_low")
        x_final = Sem("x_final")
        dve_step = Sem("dve_step")
        y_stored = Sem("y_stored", 16)

        block = ctx.enter_context(nc.Block())
        CUT_RET = (B0["conv_out"] + RING) // RING * RING
        CUT_CACHE = (B0["gate_c"] + RING) // RING * RING

        @block.sync
        def _(sp):
            sp.dma_start(tab[:, :], tab_in).then_inc(tables_loaded.s, DMA)
            sp.dma_start(xT[:, :, :], x_in).then_inc(tables_loaded.s, DMA)
            sp.dma_start(vecs[:, :, :], vec_in).then_inc(tables_loaded.s, DMA)
            sp.dma_start(pages[0:1, :], pages_in).then_inc(tables_loaded.s, DMA)
            sp.wait_ge(tables_loaded.s, 4 * DMA)

            with sp.Fori(0, DEPTH) as l:
                def load_block(n, r, reuse):
                    sp.wait_ge(w_split.s, w_split.at(l, reuse))
                    sp.dma_start(w_raw[r][:, :], stream[ds(l * NBLK + n, 1)].rearrange("o p c -> (o p) c"))\
                        .then_inc(w_loaded[r].s, DMA)

                def load_blocks(a, b):
                    whole = (b - a) // RING
                    if whole > 0:
                        with sp.Fori(0, whole) as j:
                            for r in range(RING):
                                load_block(j * RING + (a + r), r, j * RING + (a + r - RING + 1))
                    for n in range(a + whole * RING, b):
                        load_block(n, n % RING, n - RING + 1)

                sp.wait_ge(w_split.s, w_split.at(l, 0))
                sp.dma_start(conv_stage[:, :, :, :], conv_in[ds(l, 1)].rearrange("o p c b w -> (o p) c b w"))\
                    .then_inc(conv_state_loaded.s, DMA)
                for r in range(RING):
                    load_block(r, r, 0)
                load_blocks(RING, CUT_RET)
                sp.dma_start(uk[:, :, :], uk_in[ds(l, 1)].rearrange("o p c n -> (o p) c n")).then_inc(mla_w_loaded.s, DMA)
                sp.dma_start(uv[:, :, :], uv_in[ds(l, 1)].rearrange("o p c n -> (o p) c n")).then_inc(mla_w_loaded.s, DMA)
                sp.dma_start(p_raw[:, :, :], p_in[ds(l, 1)].rearrange("o p c n -> (o p) c n")).then_inc(mla_w_loaded.s, DMA)

                def load_state(b, i):
                    sp.dma_start(state[i][:, :, :], state_in[ds(l * NB + b, 1)].rearrange("o h d e -> d (o h) e"))\
                        .then_inc(st_loaded[i].s, DMA)

                def store_state(b, i):
                    sp.wait_ge(st_new.s, st_new.at(l, b + 1))
                    sp.dma_start(ret_sample_out[ds(l * NB + b, 1)].rearrange("o h d e -> d (o h) e"), state[i][:, :, :])\
                        .then_inc(st_stored[i].s, DMA)

                for i in range(2):
                    load_state(i, i)
                with sp.Fori(0, NB // 2 - 1) as j:
                    for i in range(2):
                        store_state(j * 2 + i, i)
                        st = st_stored[i]
                        sp.wait_ge(st.s, st.at(l, DMA) + j * DMA)
                        sp.wait_ge(st_o.s, st_o.at(l, j * 2 + (i + 1)))
                        load_state(j * 2 + (i + 2), i)
                for i in range(2):
                    store_state(NB - 2 + i, i)
                for i in range(2):
                    sp.wait_ge(st_stored[i].s, st_stored[i].at(l, 64))
                sp.wait_ge(st_o.s, st_o.at(l, NB))
                sp.dma_start(uk_t[0:NOPE, :, :], ukt_in[ds(l, 1)].rearrange("o p c n -> (o p) c n")).then_inc(ukt_loaded.s, DMA)
                load_blocks(CUT_RET, CUT_CACHE)

                def load_cache(b, i):
                    for t in range(NT):
                        page = sp.value_load(pages[0:1, ds(b * NT + t, 1)], min_val=0, max_val=ckv_in.shape[0] // DEPTH - 1)
                        src = page + l * (ckv_in.shape[0] // DEPTH)
                        sp.dma_start(ckv[i][:, t, :], ckv_in[ds(src, 1)].rearrange("o p c -> (o p) c")).then_inc(ck_loaded[i].s, DMA)
                        sp.dma_start(kpe[i][:, t, :], kpe_in[ds(src, 1)].rearrange("o p c -> (o p) c")).then_inc(ck_loaded[i].s, DMA)

                sp.wait_ge(gn_low.s, gn_low.at(l, HR))
                sp.wait_ge(gn_high.s, gn_high.at(l, HR))
                sp.wait_ge(ret_stored.s, ret_stored.at(l, DMA))
                settle(sp)
                for i in range(2):
                    load_cache(i, i)
                with sp.Fori(0, NB // 2 - 1) as j:
                    for i in range(2):
                        sp.wait_ge(t_lat.s, t_lat.at(l, j * 2 + (i + 1)))
                        sp.wait_ge(c_ksq.s, c_ksq.at(l, j * 2 + (i + 1)))
                        settle(sp)
                        load_cache(j * 2 + (i + 2), i)
                load_blocks(CUT_CACHE, NBLK)

            sp.wait_ge(conv_stored.s, DEPTH * 32)
            sp.wait_ge(ret_stored.s, DEPTH * DMA)
            sp.wait_ge(own_stored.s, DEPTH * 32)
            for i in range(2):
                sp.wait_ge(st_stored[i].s, DEPTH * 64)
            sp.wait_ge(x_final.s, 1)
            sp.dma_start(y_out, xT[:, :, :]).then_inc(y_stored.s, DMA)
            sp.wait_ge(y_stored.s, DMA)

        @block.gpsimd
        def _(pool):
            pool.sem_inc(w_split.s, 1)
            with pool.Fori(0, DEPTH) as l:
                def cut(n, turn, r):
                    ld = w_loaded[r]
                    pool.wait_ge(ld.s, turn * DMA + ld.at(l, DMA))
                    settle(pool)
                    pool.tensor_copy(w_hi[r][:, :], w_raw[r][:, :]).then_inc(w_high.s, 1)
                    pool.wait_ge(w_high.s, w_high.at(l, n + 1))
                    pool.tensor_tensor(w_lo[r][:, :], w_raw[r][:, :], w_hi[r][:, :].bitcast(F32), ALU.subtract)\
                        .then_inc(w_split.s, 1)

                pool.wait_ge(chunk_free.s, chunk_free.at(l, 0))
                for r in range(RING):
                    cut(r, 0, r)
                with pool.Fori(1, NBLK // RING) as j:
                    for r in range(RING):
                        pool.wait_ge(w_begun.s, w_begun.at(l, j * RING + (r - RING + 2)))
                        cut(j * RING + r, j, r)
                for n in range(NBLK // RING * RING, NBLK):
                    pool.wait_ge(w_begun.s, w_begun.at(l, n - RING + 2))
                    cut(n, n // RING, n % RING)

        @block.tensor
        def _(pe):
            mm = pe.matmul
            pe.wait_ge(tables_loaded.s, 4 * DMA)
            rot = tb("rot", QK, 0, slice(0, QK))

            def three(out, w, rhs, first, last):
                a = mm(out, w[0], rhs[0], start=first, stop=False)
                mm(out, w[0], rhs[1], start=False, stop=False)
                return a, mm(out, w[1], rhs[0], start=False, stop=last)

            with pe.Fori(0, DEPTH) as l:
                def chunk(c, c_static, run, rhs, M=P, wait_k=None):
                    pe.wait_ge(chunk_free.s, chunk_free.at(l, c - 3))
                    out = bank[c_static % 4][0:M, 0:T]
                    for k, (n, n_static, a) in enumerate(run):
                        s = n_static % RING
                        if a == 0:
                            pe.wait_ge(w_split.s, w_split.at(l, n + 1))
                        if wait_k is not None:
                            wait_k(k)
                        first, last = three(out, (w_hi[s][:, a:a + M], w_lo[s][:, a:a + M]),
                                            (rhs[0][:, k, :], rhs[1][:, k, :]), k == 0, k == len(run) - 1)
                        if a == 0:
                            first.then_inc(w_begun.s, 1)
                    last.then_inc(chunk_ready.s, 1)

                def group(stage, i, rhs, wait_k=None):
                    for r in range(4):
                        n, c = B0[stage] + r, C0[stage] + r
                        chunk(i * 4 + c, c, [(i * 4 + n, n, k * P) for k in range(KT)], rhs, wait_k=wait_k if r == 0 else None)

                def stream_chunk(stage, m, kt, rhs, wait_k=None):
                    t0 = m * kt
                    chunk(C0[stage] + m, C0[stage] + m,
                          [(B0[stage] + (t0 + k) // 8, B0[stage] + (t0 + k) // 8, (t0 + k) % 8 * P) for k in range(kt)],
                          rhs, wait_k=wait_k)

                h = (h_hi, h_lo)
                s_ = (s_hi, s_lo)

                def token_sums(w):
                    for k in range(KT):
                        pe.wait_ge(x_sq.s, x_sq.at(l, w * KT + k + 1))
                        mm(bank[4][:, 0:T], ones, et[:, k % 4, :], start=k == 0, stop=k == KT - 1).then_inc(x_sum.s, 1)

                def h_there(w):
                    return lambda k: pe.wait_ge(h_low.s, h_low.at(l, w * KT + k + 1))

                pe.wait_ge(chunk_free.s, chunk_free.at(l, 0))
                token_sums(0)
                with pe.Fori(0, 2) as i:
                    group("glu", i, h, h_there(0))
                with pe.Fori(0, 2) as i:
                    group("qk", i, h)
                pe.wait_ge(rope_ready.s, rope_ready.at(l, 2))
                pe.wait_ge(x_root.s, x_root.at(l, 1))
                for hd in range(HR):
                    for c in range(2):
                        pe.transpose(bank[4 + c][:, hd * P:hd * P + P], qk[:, HR + hd, c * P:c * P + P], ident)
                    ins = pe.transpose(bank[6][0:NB, hd * P:hd * P + P], qk[:, HR + hd, TP:T], ident)
                ins.then_inc(k_turned.s, 1)
                pe.wait_ge(k_copied.s, k_copied.at(l, 1))
                settle(pe)
                with pe.Fori(0, 2) as i:
                    group("v", i, h)
                    pe.wait_ge(v_copied.s, v_copied.at(l, i))
                    pe.wait_ge(chunk_free.s, chunk_free.at(l, i * 4 + (C0["v"] + 4)))
                    for r in range(4):
                        for c in range(2):
                            pe.transpose(bank[4 + c][:, r * P:r * P + P], zt[:, r, c * P:c * P + P], ident)
                        ins = pe.transpose(bank[6][0:NB, r * P:r * P + P], zt[:, r, TP:T], ident)
                    ins.then_inc(v_turned.s, 1)
                with pe.Fori(0, 2) as i:
                    group("rg", i, h)
                with pe.Fori(0, 2) as i:
                    group("gate_a", i, h)

                pe.wait_ge(conv_done.s, conv_done.at(l, 1))
                pe.wait_ge(v_copied.s, v_copied.at(l, 2))
                for c in range(CT):
                    ins = mm(bank[4][:, 0:T], ones, yconv[:, c, :], start=c == 0, stop=c == CT - 1)
                ins.then_inc(cln_sum.s, 1)
                pe.wait_ge(cln_sq.s, cln_sq.at(l, 1))
                for c in range(CT):
                    ins = mm(bank[5][:, 0:T], ones, et[:, c, :], start=c == 0, stop=c == CT - 1)
                ins.then_inc(cln_sum.s, 1)

                def ret_scores(hd):
                    b = bank[4 + hd % 2]
                    if hd >= 2:
                        pe.wait_ge(ret_sd.s, ret_sd.at(l, hd - 1))
                    mm(b[:, 0:TP], qk[:, HR + hd, 0:P], qk[:, hd, 0:TP], start=True, stop=True)
                    mm(b[:, TP:TP + P], qk[:, HR + hd, P:TP], qk[:, hd, P:TP], start=True, stop=True).then_inc(ret_s.s, 1)

                pe.wait_ge(cln_root.s, cln_root.at(l, 1))
                ret_scores(0)
                ret_scores(1)
                for hd in range(HR):
                    pe.wait_ge(ret_sd.s, ret_sd.at(l, hd + 1))
                    if hd:
                        pe.wait_ge(ret_oc.s, ret_oc.at(l, hd))
                    for e in range(2):
                        o = bank[6][:, e * TP:e * TP + TP]
                        v0 = hd * DV + e * P
                        mm(o, v_nat[:, 0, v0:v0 + P], sT[hd % 2][:, 0:TP], start=True, stop=False)
                        ins = mm(o[:, P:TP], v_nat[:, 1, v0:v0 + P], sT[hd % 2][:, TP:TP + P], start=False, stop=True)
                    ins.then_inc(ret_o.s, 1)
                    if hd:
                        pe.wait_ge(ret_stc.s, ret_stc.at(l, hd))
                    for c in range(2):
                        ins = mm(bank[7][:, 0:DV], k_nat[:, c, hd * P:hd * P + P], v_nat[:, c, hd * DV:hd * DV + DV],
                                 start=c == 0, stop=c == 1)
                    ins.then_inc(ret_st.s, 1)
                    if hd + 2 < HR:
                        ret_scores(hd + 2)

                pe.wait_ge(ret_oc.s, ret_oc.at(l, HR))
                settle(pe)
                with pe.Fori(0, NB // 2) as j:
                    for i in range(2):
                        b = j * 2 + i
                        pe.wait_ge(st_mask.s, st_mask.at(l, b + 1))
                        for hd in range(HR):
                            ins = mm(bank[4 + hd // 2][:, hd % 2 * DV:hd % 2 * DV + DV], k_mask[i][0:NB, hd * P:hd * P + P],
                                     v_smp[0:NB, hd * DV:hd * DV + DV], start=True, stop=True)
                        ins.then_inc(st_outer.s, 1)
                        pe.wait_ge(st_new.s, st_new.at(l, b + 1))
                        for hd in range(HR):
                            for e in range(2):
                                m = 2 * hd + e
                                ins = mm(bank[6][:, m:m + 1], state[i][:, hd, e * P:e * P + P],
                                         qk[:, hd, ds(b + TP, 1)], start=True, stop=True)
                        ins.then_inc(st_o.s, 1)

                pe.wait_ge(conv_split.s, conv_split.at(l, 1))
                for m in range(KT):
                    stream_chunk("conv_out", m, CT, (cv_hi, cv_lo))

                pe.wait_ge(st_oc.s, st_oc.at(l, NB))
                pe.wait_ge(ret_stc.s, ret_stc.at(l, HR))
                for hd in range(HR):
                    for e in range(2):
                        ins = mm(bank[4 + hd][:, 0:T], ones, oT[:, 2 * hd + e, :], start=e == 0, stop=e == 1)
                    ins.then_inc(gn_sum.s, 1)
                for hd in range(HR):
                    pe.wait_ge(gn_sq.s, gn_sq.at(l, hd + 1))
                    for e in range(2):
                        ins = mm(bank[4 + hd][:, 0:T], ones, et[:, 2 * (hd % 2) + e, :], start=e == 0, stop=e == 1)
                    ins.then_inc(gn_var.s, 1)

                with pe.Fori(0, 2) as i:
                    group("gate_b", i, h)
                pe.wait_ge(gn_low.s, gn_low.at(l, HR))
                settle(pe)
                with pe.Fori(0, 2) as i:
                    group("ret_out", i, s_)

                for m in range(6):
                    n, c = B0["kvq"] + m, C0["kvq"] + m
                    chunk(c, c, [(n, n, k * P) for k in range(KT)], h)
                pe.wait_ge(kvq_act.s, kvq_act.at(l, 3))
                pe.wait_ge(gn_root.s, gn_root.at(l, HR))
                for k in range(3):
                    ins = mm(bank[4][:, 0:T], ones, sqg[:, k, :], start=k == 0, stop=k == 2)
                ins.then_inc(kvq_sum.s, 1)
                pe.wait_ge(kvq_act.s, kvq_act.at(l, 5))
                for k in range(2):
                    ins = mm(bank[5][:, 0:T], ones, sqg[:, 3 + k, :], start=k == 0, stop=k == 1)
                ins.then_inc(kvq_sum.s, 1)
                pe.wait_ge(chunk_free.s, chunk_free.at(l, C0["kvq"] + 6))
                mm(bank[6][0:QK, 0:T], rot, zt[0:QK, 1, :], start=True, stop=True).then_inc(kr_rot.s, 1)

                def head_sum(k, buf_bank):
                    pe.wait_ge(hn_sq.s, hn_sq.at(l, k + 1))
                    if k >= 2:
                        pe.wait_ge(hn_root.s, hn_root.at(l, k - 1))
                    mm(buf_bank[0:QK, 0:T], ones[0:QK, 0:QK], et[0:QK, k % 4, :], start=True, stop=True).then_inc(hn_sum.s, 1)

                pe.wait_ge(qa_low.s, qa_low.at(l, 1))
                pe.wait_ge(kvq_root.s, kvq_root.at(l, 2))
                pe.wait_ge(kpe_ready.s, kpe_ready.at(l, 1))
                for step in range(HM + 3):
                    if step < HM:
                        g = min(step // 3, 2)
                        n, c = B0["uq"] + g, C0["uq"] + step
                        chunk(c, c, [(n, n, ((step - 3 * g) * 3 + k) * QK) for k in range(3)], (qa_hi, qa_lo), M=QK)
                    hd = step - 1
                    if 0 <= hd < HM:
                        pe.wait_ge(chunk_free.s, chunk_free.at(l, C0["uq"] + hd + 1))
                        if hd >= 2:
                            pe.wait_ge(q_roped.s, q_roped.at(l, hd - 1))
                        mm(bank[4 + hd % 2][0:QK, 0:T], rot, qm[0:QK, hd, :], start=True, stop=True).then_inc(uq_rot.s, 1)
                    hd = step - 3
                    if hd >= 0:
                        head_sum(hd, bank[6 + hd % 2])
                pe.wait_ge(mla_w_loaded.s, mla_w_loaded.at(l, 48))
                pe.wait_ge(q_roped.s, q_roped.at(l, HM))
                pe.wait_ge(ckv_ready.s, ckv_ready.at(l, 1))
                for step in range(HM + 2):
                    if step < HM:
                        if step >= 2:
                            pe.wait_ge(kn_copied.s, kn_copied.at(l, step - 1))
                        for c in range(2):
                            ins = mm(bank[4 + step % 2][0:NOPE, 0:T], uk[:, c, step * NOPE:step * NOPE + NOPE], ckvT[:, c, :],
                                     start=c == 0, stop=c == 1)
                        ins.then_inc(kn_ready.s, 1)
                    if step >= 2:
                        head_sum(HM + step - 2, bank[6 + step % 2])
                pe.wait_ge(kn_copied.s, kn_copied.at(l, HM))
                for c in range(2):
                    for k in range(2):
                        ins = mm(bank[4 + c][:, :], ckvT[:, k, c * P:c * P + P], uv[:, k, :], start=k == 0, stop=k == 1)
                ins.then_inc(vm_ready.s, 1)
                pe.wait_ge(hn_root.s, hn_root.at(l, 2 * HM))
                pe.wait_ge(own_prod.s, own_prod.at(l, 1))
                mm(bank[6][:, 0:HM * NB], ones[0:QK, :], et[0:QK, 0, 0:HM * NB], start=True, stop=True).then_inc(own_sum.s, 1)
                pe.wait_ge(qg_ready.s, qg_ready.at(l, 1))
                pe.wait_ge(ukt_loaded.s, ukt_loaded.at(l, DMA))
                for hd in range(HM):
                    for c in range(2):
                        o = (c * HM + hd) * NB
                        ins = mm(bank[7][:, o:o + NB], uk_t[0:NOPE, hd, c * P:c * P + P], et[0:NOPE, 1, hd * NB:hd * NB + NB],
                                 start=True, stop=True)
                ins.then_inc(qt_ready.s, 1)

                def att_scores(hd):
                    b = bank[4 + hd % 2]
                    if hd >= 2:
                        pe.wait_ge(at_m.s, at_m.at(l, hd - 1))
                    mm(b[:, 0:P], qm[0:QK, hd, 0:P], km[0:QK, hd, 0:P], start=True, stop=True)
                    mm(b[:, P:3 * P], qm[0:QK, hd, P:TP], km[0:QK, hd, 0:TP], start=True, stop=True).then_inc(at_s.s, 1)

                pe.wait_ge(vm_copied.s, vm_copied.at(l, 1))
                pe.wait_ge(hn_done.s, hn_done.at(l, 2 * HM))
                att_scores(0)
                att_scores(1)
                pe.wait_ge(own_copied.s, own_copied.at(l, 1))
                pe.wait_ge(qt_low.s, qt_low.at(l, 1))
                for hd in range(HM):
                    pe.wait_ge(at_n.s, at_n.at(l, hd + 1))
                    if hd:
                        pe.wait_ge(at_tc.s, at_tc.at(l, hd))
                    for c in range(3):
                        ins = pe.transpose(bank[6][:, c * P:c * P + P], ap_s[hd % 2][:, c * P:c * P + P], ident)
                    ins.then_inc(at_t.s, 1)
                    if hd + 2 < HM:
                        att_scores(hd + 2)
                    pe.wait_ge(at_tc.s, at_tc.at(l, hd + 1))
                    if hd:
                        pe.wait_ge(at_oc.s, at_oc.at(l, hd))
                    r = slice(hd % 2 * VD, hd % 2 * VD + VD)
                    mm(bank[7][r, 0:TP], vm[:, 0, hd * VD:hd * VD + VD], ap_t[hd % 2][:, 0:TP], start=True, stop=False)
                    mm(bank[7][r, P:TP], vm[:, 1, hd * VD:hd * VD + VD], ap_t[hd % 2][:, TP:TP + P], start=False, stop=True)\
                        .then_inc(at_o.s, 1)

                def front(b, i, tail):
                    ck = ck_loaded[i]
                    turn = b // 2 if isinstance(b, int) else tail[2]
                    pe.wait_ge(ck.s, turn * (32 * NT) + ck.at(l, 32 * NT))
                    if tail is not None:
                        pe.wait_ge(c_lo.s, c_lo.at(l, b * 8))
                    for g in range(4):
                        ins = pe.transpose(bank[5][:, g * P:g * P + P], kpe[i][:, 4 * g:4 * g + 4, :].rearrange("p t r -> p (t r)"), ident)
                    ins.then_inc(c_kt.s, 1)

                    def turn_pair(tp):
                        if tp == 1:
                            pe.wait_ge(c_ktc.s, c_ktc.at(l, b + 1))
                        elif tp >= 2:
                            pe.wait_ge(c_lo.s, c_lo.at(l, b * 8 + (tp - 1)))
                        for u in range(2):
                            for c in range(2):
                                q = 2 * u + c
                                ins = pe.transpose(bank[4 + tp % 2][:, q * P:q * P + P], ckv[i][:, 2 * tp + u, c * P:c * P + P], ident)
                        ins.then_inc(c_tr.s, 1)

                    turn_pair(0)
                    pe.wait_ge(c_q.s, c_q.at(l, b + 1))
                    for tp in range(NT // 2):
                        if tp + 1 < NT // 2:
                            turn_pair(tp + 1)
                        pe.wait_ge(c_lo.s, c_lo.at(l, b * 8 + (tp + 1)))
                        if tp == 0:
                            pe.wait_ge(c_ktc.s, c_ktc.at(l, b + 1))
                        for u in range(2):
                            t = 2 * tp + u
                            o = bank[6 + i][:, t * HM:t * HM + HM]
                            for c in range(2):
                                q = 2 * u + c
                                three(o, (ct_hi[tp % 2][:, q, :], ct_lo[tp % 2][:, q, :]), (q_hi[i][:, c, :], q_lo[i][:, c, :]), c == 0, False)
                            ins = mm(o, kpeT[:, t // 4, :], q_pe[i][:, t % 4, :], start=False, stop=True)
                            if t == NT - 1:
                                ins.then_inc(c_sc.s, 1)
                            if tail is not None or t >= 2:
                                pe.wait_ge(c_sq.s, c_sq.at(l, b * NT + (t - 1)))
                            for c in range(2):
                                q = 2 * u + c
                                _, ins = three(bank[u][:, :], (ct_hi[tp % 2][:, q, :], ct_lo[tp % 2][:, q, :]),
                                               (uk_hi[:, c, :], uk_lo[:, c, :]), c == 0, c == 1)
                            ins.then_inc(c_kn.s, 1)
                        if tail is not None and tp in (2, 4, 7):
                            tail_step(tail, (2, 4, 7).index(tp))

                def tail_step(tail, step):
                    b, i = tail[0], tail[1]
                    if step == 0:
                        pe.wait_ge(t_mx.s, t_mx.at(l, b + 1))
                        pe.transpose(bank[2][0:HM, 0:P], small[:, 0:8], ident).then_inc(t_mt.s, 1)
                    elif step == 1:
                        pe.wait_ge(t_dg.s, t_dg.at(l, b + 1))
                        mm(bank[2][:, P:P + HM], ones[0:HM, :], small[0:HM, 16:24], start=True, stop=True).then_inc(t_bc.s, 1)
                    else:
                        pe.wait_ge(t_p.s, t_p.at(l, b + 1))
                        pe.wait_ge(t_l.s, t_l.at(l, b + 1))
                        mm(bank[2][:, P + 8:P + 16], ones, small[:, 48:56], start=True, stop=True)
                        for c in range(2):
                            for t in range(NT):
                                ins = mm(bank[3][:, c * HM:c * HM + HM], ckv[i][:, t, c * P:c * P + P], pr[:, t, :],
                                         start=t == 0, stop=t == NT - 1)
                        ins.then_inc(t_lat.s, 1)

                pe.wait_ge(chunk_free.s, chunk_free.at(l, C0["gate_c"]))
                pe.wait_ge(at_tc.s, at_tc.at(l, HM))
                pe.wait_ge(at_oc.s, at_oc.at(l, HM))
                pe.wait_ge(uk_low.s, uk_low.at(l, 1))
                front(0, 0, None)
                with pe.Fori(0, NB // 2 - 1) as j:
                    front(j * 2 + 1, 1, (j * 2, 0, j))
                    front(j * 2 + 2, 0, (j * 2 + 1, 1, j + 1))
                front(NB - 1, 1, (NB - 2, 0, NB // 2 - 1))
                for step in range(3):
                    tail_step((NB - 1, 1), step)

                pe.wait_ge(t_fin.s, t_fin.at(l, NB))
                for hd in range(HM):
                    r = slice(hd % 2 * VD, hd % 2 * VD + VD)
                    o = hd // 2 * NB
                    for c in range(2):
                        ins = mm(bank[4][r, o:o + NB], uv[:, c, hd * VD:hd * VD + VD], lat[:, c, hd, :], start=c == 0, stop=c == 1)
                ins.then_inc(uvs_ready.s, 1)

                with pe.Fori(0, 2) as i:
                    group("gate_c", i, h)
                pe.wait_ge(mla_split.s, mla_split.at(l, 1))
                for m in range(KT):
                    stream_chunk("mla_out", m, 4, (cv_hi, cv_lo))
                with pe.Fori(0, 2) as i:
                    group("w_out", i, s_, lambda k: pe.wait_ge(mix_low.s, mix_low.at(l, k + 1)))

                token_sums(1)
                with pe.Fori(0, 2 * FT // 4) as i:
                    group("ffn_in", i, h, h_there(1))
                for m in range(KT):
                    stream_chunk("ffn_out", m, FT, (a_hi, a_lo), (lambda k: pe.wait_ge(ffn_low.s, ffn_low.at(l, k + 1))) if m == 0 else None)

                token_sums(2)
                with pe.Fori(0, 2) as i:
                    group("ple_gate", i, h, h_there(2))
                pe.wait_ge(p_low.s, p_low.at(l, 1))
                for m in range(KT):
                    stream_chunk("ple_proj", m, 2, (p_hi, p_lo))

        @block.scalar
        def _(act):
            A = act.activation

            def copy(out, in_, **kw):
                return A(out, in_, ACT.Copy, **kw)

            act.sem_inc(v_copied.s, 1)
            act.wait_ge(tables_loaded.s, 4 * DMA)
            act.wait_ge(q_pe_zeroed.s, 1)
            with act.Fori(0, DEPTH) as l:
                def split_x(w, gain, there):
                    for k in range(KT):
                        there(k)
                        copy(h_hi[:, k, :], xT[:, k, :], scale=col(gain, k)).then_inc(h_high.s, 1)
                        if k >= 4:
                            act.wait_ge(x_sum.s, x_sum.at(l, w * KT + k - 3))
                        A(et[:, k % 4, :], xT[:, k, :], ACT.Square).then_inc(x_sq.s, 1)
                    act.wait_ge(x_sum.s, x_sum.at(l, (w + 1) * KT))
                    A(rstd[:, :], bank[4][:, 0:T], ACT.Sqrt, scale=1.0 / D, bias=EPS).then_inc(x_root.s, 1)

                def exps(stage, i, slots):
                    for r in slots:
                        act.wait_ge(chunk_free.s, chunk_free.at(l, i * 4 + (C0[stage] + r + 1)))
                        A(et[:, r, :], zt[:, r, :], ACT.Exp, scale=-1.0).then_inc(exp_ready.s, 1)

                act.wait_ge(vec_ready.s, vec_ready.at(l, 1))
                split_x(0, "g_mix", lambda k: None)
                act.wait_ge(conv_state_loaded.s, conv_state_loaded.at(l, DMA))
                copy(u_smp[:, :, :, 0:30], conv_stage[:, :, :, :]).then_inc(conv_state_placed.s, 1)
                for c in range(CT):
                    ins = A(yconv[:, c, :], tb("rope_c", T), ACT.Identity, scale=0.0, bias=col("b_dw", c))
                ins.then_inc(conv_biased.s, 1)
                with act.Fori(0, 2) as i:
                    exps("glu", i, (1, 3))
                act.wait_ge(u_ready.s, u_ready.at(l, 1))
                copy(conv_new[:, :, :, :], u_smp[:, :, :, 1:31]).then_inc(conv_new_ready.s, 1)
                act.wait_ge(conv_new_ready.s, conv_new_ready.at(l, 1))
                act.dma_start(conv_sample_out[ds(l, 1)].rearrange("o p c b w -> (o p) c b w"), conv_new[:, :, :, :]).then_inc(conv_stored.s, DMA)
                act.dma_start(conv_prompt_out[ds(l, 1)].rearrange("o p c w -> (o p) c w"), u_ext[:, :, TP:TP + 30]).then_inc(conv_stored.s, DMA)

                act.wait_ge(k_turned.s, k_turned.at(l, 1))
                for hd in range(HR):
                    for c in range(2):
                        copy(k_nat[:, c, hd * P:hd * P + P], bank[4 + c][:, hd * P:hd * P + P], scale=tb("kdec", 1, c * HR + hd))
                copy(k_smp[0:NB, :], bank[6][0:NB, :]).then_inc(k_copied.s, 1)
                with act.Fori(0, 2) as i:
                    act.wait_ge(v_turned.s, v_turned.at(l, i + 1))
                    for c in range(2):
                        copy(v_nat[:, c, ds(i * 512, 512)], bank[4 + c][:, :])
                    copy(v_smp[0:NB, ds(i * 512, 512)], bank[6][0:NB, :]).then_inc(v_copied.s, 1)
                with act.Fori(0, 2) as i:
                    exps("rg", i, range(4))
                with act.Fori(0, 2) as i:
                    exps("gate_a", i, range(4))

                act.wait_ge(cln_centred.s, cln_centred.at(l, 1))
                A(et[:, :, :], yconv[:, :, :], ACT.Square).then_inc(cln_sq.s, 1)
                act.wait_ge(cln_sum.s, cln_sum.at(l, 2))
                A(rsb[:, 0, :], bank[5][:, 0:T], ACT.Sqrt, scale=1.0 / CONV, bias=EPS).then_inc(cln_root.s, 1)
                act.wait_ge(cln_y.s, cln_y.at(l, 1))
                A(et[:, :, :], yconv[:, :, :], ACT.Exp, scale=-1.0).then_inc(cln_exp.s, 1)
                act.wait_ge(conv_act.s, conv_act.at(l, 1))
                copy(cv_hi[:, 0:CT, :], yconv[:, :, :]).then_inc(conv_high.s, 1)

                act.wait_ge(conv_stored.s, conv_stored.at(l, 32))
                for hd in range(HR):
                    act.wait_ge(ret_o.s, ret_o.at(l, hd + 1))
                    copy(oT[:, 2 * hd:2 * hd + 2, 0:TP], bank[6][:, :].rearrange("p (e t) -> p e t", e=2)).then_inc(ret_oc.s, 1)
                    act.wait_ge(ret_st.s, ret_st.at(l, hd + 1))
                    copy(ret_stage[:, hd, :], bank[7][:, 0:DV]).then_inc(ret_stc.s, 1)
                act.wait_ge(ret_stc.s, ret_stc.at(l, HR))
                act.dma_start(ret_prompt_out[ds(l, 1)].rearrange("o h d e -> d (o h) e"), ret_stage[:, :, :]).then_inc(ret_stored.s, DMA)

                def gn_square(hd):
                    act.wait_ge(gn_c.s, gn_c.at(l, hd + 1))
                    if hd >= 2:
                        act.wait_ge(gn_var.s, gn_var.at(l, hd - 1))
                    e = 2 * (hd % 2)
                    A(et[:, e:e + 2, :], oT[:, 2 * hd:2 * hd + 2, :], ACT.Square).then_inc(gn_sq.s, 1)

                def gn_rt(hd):
                    act.wait_ge(gn_var.s, gn_var.at(l, hd + 1))
                    if hd >= 2:
                        act.wait_ge(gn_y.s, gn_y.at(l, hd - 1))
                    A(rsb[:, hd % 2, :], bank[4 + hd][:, 0:T], ACT.Sqrt, scale=1.0 / DV, bias=EPS).then_inc(gn_root.s, 1)

                def gn_hi(hd):
                    act.wait_ge(gn_y.s, gn_y.at(l, hd + 1))
                    copy(s_hi[:, 2 * hd:2 * hd + 2, :], oT[:, 2 * hd:2 * hd + 2, :]).then_inc(gn_high.s, 1)

                gn_square(0)
                gn_square(1)
                gn_rt(0)
                gn_square(2)
                gn_rt(1)
                gn_hi(0)
                gn_square(3)
                gn_rt(2)
                gn_hi(1)
                gn_rt(3)
                gn_hi(2)
                gn_hi(3)
                with act.Fori(0, 2) as i:
                    exps("gate_b", i, range(4))

                for m in range(5):
                    act.wait_ge(chunk_free.s, chunk_free.at(l, C0["kvq"] + m + 1))
                    z = zt[:, (0, 1, 2, 3, 0)[m], :]
                    ins = A(sqg[:, m, :], z, ACT.Square)
                    if m < 3:
                        ins = copy(qa_hi[:, m, :], z, scale=col("g_qa", m))
                    ins.then_inc(kvq_act.s, 1)
                for n, width in enumerate((QL, KVL)):
                    act.wait_ge(kvq_sum.s, kvq_sum.at(l, n + 1))
                    A(rsb[:, n, :], bank[4 + n][:, 0:T], ACT.Sqrt, scale=1.0 / width, bias=EPS).then_inc(kvq_root.s, 1)

                def head_square(k, buf):
                    if k >= 4:
                        act.wait_ge(hn_done.s, hn_done.at(l, k - 3))
                    A(et[0:QK, k % 4, :], buf, ACT.Square).then_inc(hn_sq.s, 1)

                def head_root(k):
                    act.wait_ge(hn_sum.s, hn_sum.at(l, k + 1))
                    A(et[0:QK, k % 4, :], bank[6 + k % 2][0:QK, 0:T], ACT.Sqrt, scale=1.0 / QK, bias=EPS).then_inc(hn_root.s, 1)

                for step in range(HM + 2):
                    if step < HM:
                        act.wait_ge(q_roped.s, q_roped.at(l, step + 1))
                        head_square(step, qm[0:QK, step, :])
                    if step >= 2:
                        head_root(step - 2)
                act.wait_ge(ckv_ready.s, ckv_ready.at(l, 1))
                act.dma_start(ckv_out[ds(l, 1)].rearrange("o p c t -> (o p) c t"), ckvT[:, :, :]).then_inc(own_stored.s, DMA)
                act.dma_start(kpe_out[ds(l, 1)].rearrange("o p t -> (o p) t"), kpe_own[NOPE:QK, :]).then_inc(own_stored.s, DMA)
                for step in range(HM + 2):
                    if step < HM:
                        copy(km[NOPE:QK, step, :], kpe_own[NOPE:QK, :])
                        act.wait_ge(kn_ready.s, kn_ready.at(l, step + 1))
                        copy(km[0:NOPE, step, :], bank[4 + step % 2][0:NOPE, 0:T]).then_inc(kn_copied.s, 1)
                        act.wait_ge(kn_copied.s, kn_copied.at(l, step + 1))
                        head_square(HM + step, km[0:QK, step, :])
                    if step >= 2:
                        head_root(HM + step - 2)
                act.wait_ge(vm_ready.s, vm_ready.at(l, 1))
                for c in range(2):
                    ins = copy(vm[:, c, :], bank[4 + c][:, :])
                ins.then_inc(vm_copied.s, 1)
                act.wait_ge(own_sum.s, own_sum.at(l, 1))
                copy(own[:, :, :].rearrange("p b h -> p (b h)"), bank[6][:, 0:HM * NB]).then_inc(own_copied.s, 1)
                act.wait_ge(qt_ready.s, qt_ready.at(l, 1))
                for c in range(2):
                    ins = copy(qt_hi[:, :, c, :], bank[7][:, c * 64:c * 64 + 64].rearrange("p (h b) -> p b h", h=HM))
                ins.then_inc(qt_high.s, 1)

                def att_exp(hd):
                    i = hd % 2
                    act.wait_ge(at_m.s, at_m.at(l, hd + 1))
                    A(ap_s[i][:, 0:P], ap_s[i][:, 0:P], ACT.Exp, scale=ATT_SCALE, bias=small[:, 4 + 2 * i:5 + 2 * i],
                      accum_out=small[:, 8 + 2 * i:9 + 2 * i])
                    A(ap_s[i][:, P:3 * P], ap_s[i][:, P:3 * P], ACT.Exp, scale=ATT_SCALE, bias=small[:, 5 + 2 * i:6 + 2 * i],
                      accum_out=small[:, 9 + 2 * i:10 + 2 * i]).then_inc(at_p.s, 1)

                att_exp(0)
                for hd in range(HM):
                    if hd + 1 < HM:
                        att_exp(hd + 1)
                    act.wait_ge(at_t.s, at_t.at(l, hd + 1))
                    copy(ap_t[hd % 2][:, :], bank[6][:, 0:3 * P]).then_inc(at_tc.s, 1)
                    act.wait_ge(at_o.s, at_o.at(l, hd + 1))
                    r = slice(hd % 2 * VD, hd % 2 * VD + VD)
                    copy(oM[r, hd // 2, 0:TP], bank[7][r, 0:TP]).then_inc(at_oc.s, 1)
                act.wait_ge(own_stored.s, own_stored.at(l, 32))
                copy(uk_hi[:, :, :], uk[:, :, :]).then_inc(uk_high.s, 1)

                def front(b, i, tail, turn):
                    copy(q_hi[i][:, :, :], qt_hi[:, ds(b, 1)].rearrange("p o c h -> p (o c) h").bitcast(F32))
                    copy(q_lo[i][:, :, :], qt_lo[:, ds(b, 1)].rearrange("p o c h -> p (o c) h").bitcast(F32))
                    for r in range(4):
                        rows = slice(r * ROPE, r * ROPE + ROPE)
                        ins = copy(q_pe[i][rows, r, :], qpe4[rows, ds(b, 1), :].rearrange("p o h -> p (o h)"))
                    ins.then_inc(c_q.s, 1)
                    ck = ck_loaded[i]
                    act.wait_ge(ck.s, turn * (32 * NT) + ck.at(l, 32 * NT))
                    if tail is not None:
                        act.wait_ge(c_ss.s, c_ss.at(l, b * NT))
                    A(sq[0][:, :, :].rearrange("p h n -> p (h n)"), kpe[i][:, :, :].rearrange("p t r -> p (t r)"), ACT.Square).then_inc(c_ksq.s, 1)
                    act.wait_ge(c_kt.s, c_kt.at(l, b + 1))
                    copy(kpeT[:, :, :], bank[5][:, :].rearrange("p (g k) -> p g k", g=4)).then_inc(c_ktc.s, 1)

                    def high(tp):
                        act.wait_ge(c_tr.s, c_tr.at(l, b * 8 + (tp + 1)))
                        copy(ct_hi[tp % 2][:, :, :], bank[4 + tp % 2][:, :].rearrange("p (q k) -> p q k", q=4)).then_inc(c_hi.s, 1)

                    high(0)
                    for tp in range(NT // 2):
                        if tp + 1 < NT // 2:
                            high(tp + 1)
                        for u in range(2):
                            t = 2 * tp + u
                            act.wait_ge(c_kn.s, c_kn.at(l, b * NT + (t + 1)))
                            if t == 0:
                                act.wait_ge(c_kss.s, c_kss.at(l, b + 1))
                            elif t >= 2 or tail is not None:
                                act.wait_ge(c_ss.s, c_ss.at(l, b * NT + (t - 1)))
                            A(sq[u][:, :, :], bank[u][:, :].rearrange("p (h n) -> p h n", h=HM), ACT.Square).then_inc(c_sq.s, 1)
                        if tail is not None and tp == 0:
                            tail_root(tail)
                        if tail is not None and tp == 5:
                            tail_exp(tail)

                def tail_root(b):
                    act.wait_ge(t_tot.s, t_tot.at(l, b + 1))
                    A(kn_r[:, :, :], kn_r[:, :, :], ACT.Sqrt, scale=1.0 / QK, bias=EPS).then_inc(t_root.s, 1)

                def tail_exp(b):
                    act.wait_ge(t_shift.s, t_shift.at(l, b + 1))
                    A(pr[:, :, :], sc[:, :, :], ACT.Exp, scale=ATT_SCALE)
                    A(small[:, 40:48], small[:, 32:40], ACT.Exp, scale=ATT_SCALE).then_inc(t_p.s, 1)

                act.wait_ge(qt_low.s, qt_low.at(l, 1))
                front(0, 0, None, 0)
                with act.Fori(0, NB // 2 - 1) as j:
                    front(j * 2 + 1, 1, j * 2, j)
                    front(j * 2 + 2, 0, j * 2 + 1, j + 1)
                front(NB - 1, 1, NB - 2, NB // 2 - 1)
                tail_root(NB - 1)
                tail_exp(NB - 1)

                act.wait_ge(uvs_ready.s, uvs_ready.at(l, 1))
                copy(oM[:, :, TP:T], bank[4][:, 0:4 * NB].rearrange("p (q b) -> p q b", q=4)).then_inc(uvs_copied.s, 1)
                act.wait_ge(uvs_copied.s, uvs_copied.at(l, 1))
                copy(cv_hi[:, 0:4, :], oM[:, :, :]).then_inc(mla_high.s, 1)
                with act.Fori(0, 2) as i:
                    exps("gate_c", i, range(4))
                act.wait_ge(mix_done.s, mix_done.at(l, KT))
                for k in range(KT):
                    copy(s_hi[:, k, :], mix[:, k, :]).then_inc(mix_high.s, 1)

                split_x(1, "g_ffn", lambda k: act.wait_ge(chunk_free.s, chunk_free.at(l, C0["w_out"] + k + 1)))
                with act.Fori(0, 2 * FT // 4) as i:
                    exps("ffn_in", i, (0,))
                    for u in range(2):
                        act.wait_ge(ffn_a.s, ffn_a.at(l, i * 2 + (u + 1)))
                        copy(a_hi[:, ds(i * 2 + u, 1), :].rearrange("p o t -> p (o t)"), zt[:, 2 * u, :]).then_inc(ffn_high.s, 1)
                        if u == 0:
                            exps("ffn_in", i, (2,))
                split_x(2, "g_ple", lambda k: act.wait_ge(chunk_free.s, chunk_free.at(l, C0["ffn_out"] + k + 1)))
                act.wait_ge(mla_w_loaded.s, mla_w_loaded.at(l, 48))
                copy(p_hi[:, :, :], p_raw[:, :, :]).then_inc(p_high.s, 1)
                with act.Fori(0, 2) as i:
                    exps("ple_gate", i, range(4))

        @block.vector
        def _(v):
            steps = Steps()

            def steps_restart():
                if steps.n:
                    v.wait_ge(dve_step.s, steps.n)
                    v.sem_clear(dve_step.s)
                    steps.n = 0

            tt, stt = v.tensor_tensor, v.scalar_tensor_tensor

            def flat(ap):
                return ap.rearrange("p o t -> p (o t)")

            v.wait_ge(tables_loaded.s, 4 * DMA)
            v.sem_inc(chunk_free.s, 4)
            for i in range(2):
                ins = v.memset(q_pe[i][:, :, :], 0.0)
            ins.then_inc(q_pe_zeroed.s, 1)
            with v.Fori(0, DEPTH) as l:
                def split_x(w, gain):
                    for k in range(KT):
                        v.wait_ge(h_high.s, h_high.at(l, w * KT + k + 1))
                        stt(h_lo[:, k, :], xT[:, k, :], col(gain, k), h_hi[:, k, :].bitcast(F32), ALU.mult, ALU.subtract)\
                            .then_inc(h_low.s, 1)
                    v.wait_ge(x_root.s, x_root.at(l, w + 1))
                    v.reciprocal(rstd[:, :], rstd[:, :]).then_inc(rstd_ready.s, 1)
                    v.wait_ge(rstd_ready.s, rstd_ready.at(l, w + 1))

                def take(stage, i, r, out=None, rows=P, rs=rstd[:, :], s=None):
                    c = C0[stage] + r
                    v.wait_ge(chunk_ready.s, chunk_ready.at(l, i * 4 + (c + 1)))
                    out = zt[:, r % 4, :] if out is None else out
                    tt(out, bank[c % 4][0:rows, 0:T], rs[0:rows, :], ALU.mult).then_inc(chunk_free.s, 1)

                def taken(stage, i, r):
                    v.wait_ge(chunk_free.s, chunk_free.at(l, i * 4 + (C0[stage] + r + 1)))

                def one_plus_inv(n, r, out):
                    v.wait_ge(exp_ready.s, exp_ready.at(l, n + 1))
                    v.tensor_scalar(et[:, r, :], et[:, r, :], 1.0, None, ALU.add).then_inc(dve_step.s, steps.one())
                    v.wait_ge(dve_step.s, steps.n)
                    v.reciprocal(out, et[:, r, :]).then_inc(dve_step.s, steps.one())
                    v.wait_ge(dve_step.s, steps.n)

                def taps(ct, i, r):
                    for j in range(4):
                        w = 4 * r + j
                        stt(yconv[:, ct, 0:TP], u_ext[:, ct, ds(i * 16 + w, TP)],
                               vec[:, ds(i * 16 + (VEC["w_dw"] + ct * 32 + w), 1)], yconv[:, ct, 0:TP], ALU.mult, ALU.add).then_inc(dve_step.s, steps.one())
                        v.wait_ge(dve_step.s, steps.n)

                def gates(stage, ct=None):
                    with v.Fori(0, 2) as i:
                        for r in range(5):
                            if r < 4:
                                take(stage, i, r)
                            if r:
                                q = r - 1
                                one_plus_inv(i * 4 + (E0[stage] + q), q, flat(gate[:, ds(i * 4 + q, 1), :]))
                                if ct is not None:
                                    taps(ct, i, q)
                        steps_restart()

                def gated_sum(stage, done=None, first=False):
                    with v.Fori(0, 2) as i:
                        for r in range(4):
                            c = C0[stage] + r
                            m = i * 4 + r
                            v.wait_ge(chunk_ready.s, chunk_ready.at(l, i * 4 + (c + 1)))
                            g, x = flat(gate[:, ds(m, 1), :]), flat(mix[:, ds(m, 1), :])
                            if first:
                                tt(x, bank[c % 4][:, 0:T], g, ALU.mult).then_inc(chunk_free.s, 1)
                                continue
                            tt(zt[:, r, :], bank[c % 4][:, 0:T], g, ALU.mult).then_inc(chunk_free.s, 1)
                            taken(stage, i, r)
                            ins = tt(x, x, zt[:, r, :], ALU.add)
                            if done is not None:
                                ins.then_inc(done.s, 1)
                            else:
                                ins.then_inc(dve_step.s, steps.one())
                        steps_restart()

                def add_to_x(stage):
                    with v.Fori(0, 2) as i:
                        for r in range(4):
                            c = C0[stage] + r
                            x = flat(xT[:, ds(i * 4 + r, 1), :])
                            v.wait_ge(chunk_ready.s, chunk_ready.at(l, i * 4 + (c + 1)))
                            tt(x, bank[c % 4][:, 0:T], x, ALU.add).then_inc(chunk_free.s, 1)

                v.tensor_copy(vec[:, :], flat(vecs[:, ds(l, 1), :])).then_inc(vec_ready.s, 1)
                v.wait_ge(vec_ready.s, vec_ready.at(l, 1))
                split_x(0, "g_mix")
                v.memset(u_ext[:, :, 0:30], 0.0).then_inc(dve_step.s, steps.one())
                v.memset(u_ext[:, :, 30 + TP:288], 0.0).then_inc(dve_step.s, steps.one())
                steps_restart()
                with v.Fori(0, 2) as i:
                    for r in range(4):
                        take("glu", i, r)
                        if r % 2:
                            one_plus_inv(i * 2 + r // 2, r, et[:, r, :])
                            taken("glu", i, r - 1)
                            m = i * 2 + r // 2
                            tt(flat(u_ext[:, ds(m, 1), 30:30 + TP]), zt[:, r - 1, 0:TP], et[:, r, 0:TP], ALU.mult).then_inc(dve_step.s, steps.one())
                            tt(u_smp[:, ds(m, 1), :, 30:31].rearrange("p o b w -> p (o b w)"), zt[:, r - 1, TP:T], et[:, r, TP:T], ALU.mult).then_inc(dve_step.s, steps.one())
                    steps_restart()
                v.wait_ge(conv_state_placed.s, conv_state_placed.at(l, 1))
                v.wait_ge(conv_biased.s, conv_biased.at(l, 1))
                taps_w = vec[:, VEC["w_dw"]:VEC["w_dw"] + CT * 32].rearrange("p (c w) -> p c w", c=CT)[:, :, 0:31]
                tt(conv_prod[:, :, :, :], u_smp[:, :, :, :], taps_w.unsqueeze(2).broadcast_to([P, CT, NB, 31]), ALU.mult)\
                    .then_inc(u_ready.s, 1)
                v.wait_ge(u_ready.s, u_ready.at(l, 1))
                v.tensor_reduce(small[:, 0:CT * NB], conv_prod[:, :, :, :].rearrange("p c b w -> p (c b) w"), AX.X, ALU.add).then_inc(dve_step.s, steps.one())
                v.wait_ge(dve_step.s, steps.n)
                steps_restart()

                with v.Fori(0, 2) as i:
                    for r in range(4):
                        take("qk", i, r)
                        taken("qk", i, r)
                        cos = tab[:, ds(i * T + TAB["rope_c"], T)]
                        o = flat(qk[:, ds(i * 4 + r, 1), :])
                        lo, hi = (slice(0, 64), slice(64, P))
                        tt(et[:, r, :], zt[:, r, :], cos, ALU.mult).then_inc(dve_step.s, steps.one())
                        tt(qk[lo, ds(i * 4 + r, 1), :].rearrange("p o t -> p (o t)"), zt[hi, r, :], tab[hi, ds(i * T + TAB["rope_s"], T)], ALU.mult).then_inc(dve_step.s, steps.one())
                        tt(qk[hi, ds(i * 4 + r, 1), :].rearrange("p o t -> p (o t)"), zt[lo, r, :], tab[lo, ds(i * T + TAB["rope_s"], T)], ALU.mult).then_inc(dve_step.s, steps.one())
                        v.wait_ge(dve_step.s, steps.n)
                        ins = tt(o, o, et[:, r, :], ALU.add)
                        if r == 3:
                            ins.then_inc(rope_ready.s, 1)
                        else:
                            ins.then_inc(dve_step.s, steps.one())
                        taps(0, i, r)
                    steps_restart()
                with v.Fori(0, 2) as i:
                    v.wait_ge(v_copied.s, v_copied.at(l, i))
                    for r in range(4):
                        take("v", i, r)
                        taps(1, i, r)
                    steps_restart()
                v.wait_ge(conv_stored.s, conv_stored.at(l, 32))
                v.wait_ge(v_copied.s, v_copied.at(l, 2))
                settle(v)
                with v.Fori(0, 2) as i:
                    for r in range(5):
                        if r < 4:
                            take("rg", i, r)
                        if r:
                            q = r - 1
                            one_plus_inv(i * 4 + (E0["rg"] + q), q, et[:, q, :])
                            tt(flat(rgs[:, ds(i * 4 + q, 1), :]), zt[:, q, :], et[:, q, :], ALU.mult).then_inc(dve_step.s, steps.one())
                            taps(2, i, q)
                    steps_restart()
                gates("gate_a", 3)
                ys = yconv[:, :, TP:T]
                tt(ys, ys, small[:, 0:CT * NB].rearrange("p (c b) -> p c b", c=CT), ALU.add).then_inc(conv_done.s, 1)

                v.wait_ge(cln_sum.s, cln_sum.at(l, 1))
                for c in range(CT):
                    ins = stt(yconv[:, c, :], bank[4][:, 0:T], -1.0 / CONV, yconv[:, c, :], ALU.mult, ALU.add)
                ins.then_inc(cln_centred.s, 1)
                v.wait_ge(cln_root.s, cln_root.at(l, 1))
                v.reciprocal(rsb[:, 0, :], rsb[:, 0, :]).then_inc(dve_step.s, steps.one())
                v.wait_ge(dve_step.s, steps.n)
                for c in range(CT):
                    stt(yconv[:, c, :], yconv[:, c, :], col("g_cln", c), rsb[:, 0, :], ALU.mult, ALU.mult).then_inc(dve_step.s, steps.one())
                v.wait_ge(dve_step.s, steps.n)
                for c in range(CT):
                    ins = v.tensor_scalar(yconv[:, c, :], yconv[:, c, :], col("b_cln", c), None, ALU.add)
                ins.then_inc(cln_y.s, 1)
                v.wait_ge(cln_exp.s, cln_exp.at(l, 1))
                v.tensor_scalar(et[:, :, :], et[:, :, :], 1.0, None, ALU.add).then_inc(dve_step.s, steps.one())
                v.wait_ge(dve_step.s, steps.n)
                v.reciprocal(et[:, :, :], et[:, :, :]).then_inc(dve_step.s, steps.one())
                v.wait_ge(dve_step.s, steps.n)
                tt(yconv[:, :, :], yconv[:, :, :], et[:, :, :], ALU.mult).then_inc(conv_act.s, 1)
                v.wait_ge(conv_high.s, conv_high.at(l, 1))
                tt(cv_lo[:, 0:CT, :], yconv[:, :, :], cv_hi[:, 0:CT, :].bitcast(F32), ALU.subtract).then_inc(conv_split.s, 1)

                for hd in range(HR):
                    v.wait_ge(ret_s.s, ret_s.at(l, hd + 1))
                    tt(sT[hd % 2][:, :], bank[4 + hd % 2][:, 0:384], tb("decay", 384, 384 * hd), ALU.mult).then_inc(ret_sd.s, 1)
                steps_restart()
                with v.Fori(0, NB // 2) as j:
                    for i in range(2):
                        b = j * 2 + i
                        v.tensor_scalar(k_mask[i][0:NB, :], k_smp[0:NB, :], tab[0:NB, ds(b + TAB["ident"], 1)], None, ALU.mult)\
                            .then_inc(st_mask.s, 1)
                        v.wait_ge(st_outer.s, st_outer.at(l, b + 1))
                        sl = st_loaded[i]
                        v.wait_ge(sl.s, j * DMA + sl.at(l, DMA))
                        for hd in range(HR):
                            s = state[i][:, hd, :]
                            ins = stt(s, s, GAMMA[hd], bank[4 + hd // 2][:, hd % 2 * DV:hd % 2 * DV + DV], ALU.mult, ALU.add)
                        ins.then_inc(st_new.s, 1)
                        v.wait_ge(st_o.s, st_o.at(l, b + 1))
                        v.tensor_copy(oT[:, :, ds(b + TP, 1)].rearrange("p m o -> p (m o)"), bank[6][:, 0:KT]).then_inc(st_oc.s, 1)
                gated_sum("conv_out", first=True)

                for hd in range(HR):
                    v.wait_ge(gn_sum.s, gn_sum.at(l, hd + 1))
                    o = oT[:, 2 * hd:2 * hd + 2, :]
                    stt(o, bank[4 + hd][:, 0:T].unsqueeze(1).broadcast_to([P, 2, T]), -1.0 / DV, o, ALU.mult, ALU.add).then_inc(gn_c.s, 1)
                for hd in range(HR):
                    v.wait_ge(gn_root.s, gn_root.at(l, hd + 1))
                    r = rsb[:, hd % 2, :]
                    o = oT[:, 2 * hd:2 * hd + 2, :]
                    v.reciprocal(r, r).then_inc(dve_step.s, steps.one())
                    v.wait_ge(dve_step.s, steps.n)
                    tt(o, o, r.unsqueeze(1).broadcast_to([P, 2, T]), ALU.mult).then_inc(dve_step.s, steps.one())
                    v.wait_ge(dve_step.s, steps.n)
                    for m in (2 * hd, 2 * hd + 1):
                        ins = stt(oT[:, m, :], oT[:, m, :], col("g_rgn", m), rgs[:, m, :], ALU.mult, ALU.mult)
                    ins.then_inc(gn_y.s, 1)
                    v.wait_ge(gn_high.s, gn_high.at(l, hd + 1))
                    tt(s_lo[:, 2 * hd:2 * hd + 2, :], o, s_hi[:, 2 * hd:2 * hd + 2, :].bitcast(F32), ALU.subtract).then_inc(gn_low.s, 1)
                steps_restart()
                v.wait_ge(ret_stored.s, ret_stored.at(l, DMA))
                settle(v)
                gates("gate_b")
                gated_sum("ret_out")

                def kvq(m):
                    v.wait_ge(chunk_ready.s, chunk_ready.at(l, C0["kvq"] + m + 1))
                    tt(zt[:, m % 4, :], bank[(C0["kvq"] + m) % 4][:, 0:T], rstd[:, :], ALU.mult).then_inc(chunk_free.s, 1)

                for m in range(4):
                    kvq(m)
                for m in range(3):
                    v.wait_ge(kvq_act.s, kvq_act.at(l, m + 1))
                    ins = stt(qa_lo[:, m, :], zt[:, m, :], col("g_qa", m), qa_hi[:, m, :].bitcast(F32), ALU.mult, ALU.subtract)
                ins.then_inc(qa_low.s, 1)
                v.wait_ge(qa_low.s, qa_low.at(l, 1))
                kvq(4)
                kvq(5)
                for n in range(2):
                    v.wait_ge(kvq_root.s, kvq_root.at(l, n + 1))
                    v.reciprocal(rsb[:, n, :], rsb[:, n, :]).then_inc(dve_step.s, steps.one())
                v.wait_ge(dve_step.s, steps.n)
                for c in range(2):
                    ins = stt(ckvT[:, c, :], zt[:, 3 if c == 0 else 0, :], col("g_kva", c), rsb[:, 1, :], ALU.mult, ALU.mult)
                ins.then_inc(ckv_ready.s, 1)
                pe_rows = slice(NOPE, QK)
                m_cos, m_sin = tb("mla_c", T, 0, pe_rows), tb("mla_s", T, 0, pe_rows)
                v.wait_ge(kr_rot.s, kr_rot.at(l, 1))
                tt(kpe_own[pe_rows, :], bank[6][pe_rows, 0:T], m_sin, ALU.mult).then_inc(dve_step.s, steps.one())
                tt(zt[pe_rows, 1, :], zt[pe_rows, 1, :], m_cos, ALU.mult).then_inc(dve_step.s, steps.one())
                v.wait_ge(dve_step.s, steps.n)
                tt(kpe_own[pe_rows, :], kpe_own[pe_rows, :], zt[pe_rows, 1, :], ALU.add).then_inc(kpe_ready.s, 1)

                def head_norm(k, buf, gain):
                    v.wait_ge(hn_root.s, hn_root.at(l, k + 1))
                    r = et[0:QK, k % 4, :]
                    v.reciprocal(r, r).then_inc(dve_step.s, steps.one())
                    v.wait_ge(dve_step.s, steps.n)
                    stt(buf, buf, col(gain)[0:QK, :], r, ALU.mult, ALU.mult).then_inc(hn_done.s, 1)

                for step in range(HM + 4):
                    if step < HM:
                        c = C0["uq"] + step
                        v.wait_ge(chunk_ready.s, chunk_ready.at(l, c + 1))
                        tt(qm[0:QK, step, :], bank[c % 4][0:QK, 0:T], rsb[0:QK, 0, :], ALU.mult).then_inc(chunk_free.s, 1)
                    hd = step - 1
                    if 0 <= hd < HM:
                        v.wait_ge(uq_rot.s, uq_rot.at(l, hd + 1))
                        q = qm[pe_rows, hd, :]
                        tt(zt[pe_rows, hd % 4, :], bank[4 + hd % 2][pe_rows, 0:T], m_sin, ALU.mult).then_inc(dve_step.s, steps.one())
                        tt(q, q, m_cos, ALU.mult).then_inc(dve_step.s, steps.one())
                        v.wait_ge(dve_step.s, steps.n)
                        tt(q, q, zt[pe_rows, hd % 4, :], ALU.add).then_inc(q_roped.s, 1)
                    if step >= 4:
                        head_norm(step - 4, qm[0:QK, step - 4, :], "g_qn")
                for hd in range(HM):
                    head_norm(HM + hd, km[0:QK, hd, :], "g_kn")
                v.wait_ge(hn_done.s, hn_done.at(l, 2 * HM))
                qs = qm[0:QK, :, TP:T]
                tt(et[0:QK, 0, 0:64].rearrange("p (b h) -> p b h", b=NB), qs.rearrange("p h b -> p b h"),
                   km[0:QK, :, TP:T].rearrange("p h b -> p b h"), ALU.mult).then_inc(own_prod.s, 1)
                v.tensor_scalar(et[0:QK, 1, 0:64].rearrange("p (h b) -> p h b", h=HM), qs, col("g_kn")[0:QK, :], None, ALU.mult)\
                    .then_inc(qg_ready.s, 1)
                v.wait_ge(qg_ready.s, qg_ready.at(l, 1))
                for q in range(4):
                    v.tensor_copy(qpe4[32 * q:32 * q + 32, :, :], et[pe_rows, 1, 0:64].rearrange("p (h b) -> p b h", h=HM)).then_inc(dve_step.s, steps.one())
                v.tensor_copy(ckv_own[:, :, :], ckvT[:, :, TP:T]).then_inc(dve_step.s, steps.one())
                v.wait_ge(dve_step.s, steps.n)
                v.wait_ge(qt_high.s, qt_high.at(l, 1))
                for c in range(2):
                    ins = tt(qt_lo[:, :, c, :], bank[7][:, c * 64:c * 64 + 64].rearrange("p (h b) -> p b h", h=HM),
                             qt_hi[:, :, c, :].bitcast(F32), ALU.subtract)
                ins.then_inc(qt_low.s, 1)

                def att_max(hd):
                    i = hd % 2
                    v.wait_ge(at_s.s, at_s.at(l, hd + 1))
                    tt(ap_s[i][:, :], bank[4 + i][:, 0:384], tb("mask", 384), ALU.add).then_inc(dve_step.s, steps.one())
                    v.wait_ge(dve_step.s, steps.n)
                    v.tensor_reduce(small[:, 0:1], ap_s[i][:, 0:P], AX.X, ALU.max).then_inc(dve_step.s, steps.one())
                    v.tensor_reduce(small[:, 1:2], ap_s[i][:, P:3 * P], AX.X, ALU.max).then_inc(dve_step.s, steps.one())
                    v.wait_ge(dve_step.s, steps.n)
                    v.tensor_scalar(small[:, 4 + 2 * i:6 + 2 * i], small[:, 0:2], -ATT_SCALE, None, ALU.mult).then_inc(at_m.s, 1)

                def att_div(hd):
                    i = hd % 2
                    v.wait_ge(at_p.s, at_p.at(l, hd + 1))
                    v.reciprocal(small[:, 8 + 2 * i:10 + 2 * i], small[:, 8 + 2 * i:10 + 2 * i]).then_inc(dve_step.s, steps.one())
                    v.wait_ge(dve_step.s, steps.n)
                    v.tensor_scalar(ap_s[i][:, 0:P], ap_s[i][:, 0:P], small[:, 8 + 2 * i:9 + 2 * i], None, ALU.mult)
                    v.tensor_scalar(ap_s[i][:, P:3 * P], ap_s[i][:, P:3 * P], small[:, 9 + 2 * i:10 + 2 * i], None, ALU.mult)\
                        .then_inc(at_n.s, 1)

                att_max(0)
                for hd in range(HM):
                    if hd + 1 < HM:
                        att_max(hd + 1)
                    att_div(hd)
                v.wait_ge(uk_high.s, uk_high.at(l, 1))
                tt(uk_lo[:, :, :], uk[:, :, :], uk_hi[:, :, :].bitcast(F32), ALU.subtract).then_inc(uk_low.s, 1)

                def front(b, i, tail):
                    v.wait_ge(c_ksq.s, c_ksq.at(l, b + 1))
                    v.tensor_reduce(sspe[i][:, :], sq[0][:, :, :].rearrange("p h (a r) -> p (h a) r", r=ROPE), AX.X, ALU.add).then_inc(c_kss.s, 1)

                    def low(tp):
                        v.wait_ge(c_hi.s, c_hi.at(l, b * 8 + (tp + 1)))
                        tt(ct_lo[tp % 2][:, :, :], bank[4 + tp % 2][:, :].rearrange("p (q k) -> p q k", q=4),
                           ct_hi[tp % 2][:, :, :].bitcast(F32), ALU.subtract).then_inc(c_lo.s, 1)

                    low(0)
                    for tp in range(NT // 2):
                        if tp + 1 < NT // 2:
                            low(tp + 1)
                        for u in range(2):
                            t = 2 * tp + u
                            v.wait_ge(c_sq.s, c_sq.at(l, b * NT + (t + 1)))
                            v.tensor_reduce(ssq[i][:, t, :], sq[u][:, :, :], AX.X, ALU.add).then_inc(c_ss.s, 1)
                        if tail is not None and tp in (0, 1, 3, 5, 6, 7):
                            tail_step(tail, (0, 1, 3, 5, 6, 7).index(tp))

                def tail_step(tail, step):
                    b, i = tail
                    if step == 0:
                        v.wait_ge(c_ss.s, c_ss.at(l, b * NT + NT))
                        v.wait_ge(c_kss.s, c_kss.at(l, b + 1))
                        tt(kn_r[:, :, :], ssq[i][:, :, :], sspe[i][:, :].unsqueeze(2).broadcast_to([P, NT, HM]), ALU.add)\
                            .then_inc(t_tot.s, 1)
                    elif step == 1:
                        v.wait_ge(t_root.s, t_root.at(l, b + 1))
                        v.reciprocal(kn_r[:, :, :], kn_r[:, :, :]).then_inc(dve_step.s, steps.one())
                        v.wait_ge(dve_step.s, steps.n)
                        v.wait_ge(c_sc.s, c_sc.at(l, b + 1))
                        tt(sc[:, :, :], bank[6 + i][:, 0:NT * HM].rearrange("p (t h) -> p t h", t=NT), kn_r[:, :, :], ALU.mult).then_inc(dve_step.s, steps.one())
                        v.wait_ge(dve_step.s, steps.n)
                        v.tensor_reduce(small[:, 0:8], sc[:, :, :].rearrange("p t h -> p h t"), AX.X, ALU.max).then_inc(t_mx.s, 1)
                    elif step == 2:
                        v.wait_ge(t_mt.s, t_mt.at(l, b + 1))
                        v.tensor_reduce(small[0:HM, 8:9], bank[2][0:HM, 0:P], AX.X, ALU.max).then_inc(dve_step.s, steps.one())
                        v.wait_ge(dve_step.s, steps.n)
                        v.tensor_scalar(small[0:HM, 16:24], ident[0:HM, 0:HM], small[0:HM, 8:9], None, ALU.mult).then_inc(t_dg.s, 1)
                    elif step == 3:
                        v.wait_ge(t_bc.s, t_bc.at(l, b + 1))
                        o = flat(own[:, ds(b, 1), :])
                        m = small[:, 24:32]
                        tt(m, bank[2][:, P:P + HM], o, ALU.max).then_inc(dve_step.s, steps.one())
                        v.wait_ge(dve_step.s, steps.n)
                        tt(sc[:, :, :], sc[:, :, :], m.unsqueeze(1).broadcast_to([P, NT, HM]), ALU.subtract).then_inc(dve_step.s, steps.one())
                        tt(small[:, 32:40], o, m, ALU.subtract).then_inc(t_shift.s, 1)
                    elif step == 4:
                        v.wait_ge(t_p.s, t_p.at(l, b + 1))
                        v.tensor_reduce(small[:, 48:56], pr[:, :, :].rearrange("p t h -> p h t"), AX.X, ALU.add).then_inc(t_l.s, 1)
                    else:
                        v.wait_ge(t_lat.s, t_lat.at(l, b + 1))
                        tt(small[:, 56:64], bank[2][:, P + 8:P + 16], small[:, 40:48], ALU.add).then_inc(dve_step.s, steps.one())
                        v.wait_ge(dve_step.s, steps.n)
                        v.reciprocal(small[:, 56:64], small[:, 56:64]).then_inc(dve_step.s, steps.one())
                        v.wait_ge(dve_step.s, steps.n)
                        for c in range(2):
                            stt(small[:, 64 + 8 * c:72 + 8 * c], small[:, 40:48], ckv_own[:, c, ds(b, 1)], bank[3][:, c * HM:c * HM + HM],
                                      ALU.mult, ALU.add).then_inc(dve_step.s, steps.one())
                        v.wait_ge(dve_step.s, steps.n)
                        for c in range(2):
                            ins = tt(lat[:, c, :, ds(b, 1)].rearrange("p h o -> p (h o)"), small[:, 64 + 8 * c:72 + 8 * c], small[:, 56:64], ALU.mult)
                        ins.then_inc(t_fin.s, 1)

                steps_restart()
                front(0, 0, None)
                steps_restart()
                with v.Fori(0, NB // 2 - 1) as j:
                    front(j * 2 + 1, 1, (j * 2, 0))
                    front(j * 2 + 2, 0, (j * 2 + 1, 1))
                    steps_restart()
                front(NB - 1, 1, (NB - 2, 0))
                for step in range(6):
                    tail_step((NB - 1, 1), step)
                v.wait_ge(mla_high.s, mla_high.at(l, 1))
                tt(cv_lo[:, 0:4, :], oM[:, :, :], cv_hi[:, 0:4, :].bitcast(F32), ALU.subtract).then_inc(mla_split.s, 1)
                steps_restart()
                v.wait_ge(mla_split.s, mla_split.at(l, 1))
                settle(v)
                gates("gate_c")
                gated_sum("mla_out", mix_done)
                for k in range(KT):
                    v.wait_ge(mix_high.s, mix_high.at(l, k + 1))
                    tt(s_lo[:, k, :], mix[:, k, :], s_hi[:, k, :].bitcast(F32), ALU.subtract).then_inc(mix_low.s, 1)
                add_to_x("w_out")

                split_x(1, "g_ffn")
                settle(v)
                steps_restart()
                with v.Fori(0, 2 * FT // 4) as i:
                    def low(u):
                        v.wait_ge(ffn_high.s, ffn_high.at(l, i * 2 + (u + 1)))
                        tt(flat(a_lo[:, ds(i * 2 + u, 1), :]), zt[:, 2 * u, :], flat(a_hi[:, ds(i * 2 + u, 1), :]).bitcast(F32), ALU.subtract)\
                            .then_inc(ffn_low.s, 1)

                    for u in range(2):
                        g, up = 2 * u, 2 * u + 1
                        take("ffn_in", i, g)
                        take("ffn_in", i, up)
                        if u:
                            low(0)
                        one_plus_inv(i * 2 + (E0["ffn_in"] + u), g, et[:, g, :])
                        tt(zt[:, g, :], zt[:, g, :], et[:, g, :], ALU.mult).then_inc(dve_step.s, steps.one())
                        v.wait_ge(dve_step.s, steps.n)
                        taken("ffn_in", i, up)
                        tt(zt[:, g, :], zt[:, g, :], zt[:, up, :], ALU.mult).then_inc(ffn_a.s, 1)
                    low(1)
                    steps_restart()
                add_to_x("ffn_out")

                split_x(2, "g_ple")
                v.wait_ge(p_high.s, p_high.at(l, 1))
                tt(p_lo[:, :, :], p_raw[:, :, :], p_hi[:, :, :].bitcast(F32), ALU.subtract).then_inc(p_low.s, 1)
                gates("ple_gate")
                with v.Fori(0, 2) as i:
                    for r in range(4):
                        c = C0["ple_proj"] + r
                        x = flat(xT[:, ds(i * 4 + r, 1), :])
                        v.wait_ge(chunk_ready.s, chunk_ready.at(l, i * 4 + (c + 1)))
                        tt(zt[:, r, :], bank[c % 4][:, 0:T], flat(gate[:, ds(i * 4 + r, 1), :]), ALU.mult).then_inc(chunk_free.s, 1)
                        taken("ple_proj", i, r)
                        tt(x, x, zt[:, r, :], ALU.add).then_inc(dve_step.s, steps.one())
                    steps_restart()
            v.sem_inc(x_final.s, 1)


def constants():
    f = np.float32
    tab = np.zeros((P, NTAB), f)
    pos = np.concatenate([np.arange(TP), np.full(NB, PAST)]).astype(f)

    def angles(half):
        inv = np.power(f(10000.0), -np.arange(half, dtype=f) / f(half)).astype(f)
        ang = (inv[:, None] * pos[None, :]).astype(f)
        return np.cos(ang.astype(np.float64)), np.sin(ang.astype(np.float64))

    def put(name, a, rows=slice(0, P), off=0):
        tab[rows, TAB[name] + off:TAB[name] + off + a.shape[1]] = a

    c, s = angles(DK // 2)
    for i, factor in enumerate((1.0, DK ** -0.5)):
        put("rope_c", np.concatenate([c, c]) * factor, off=i * T)
        put("rope_s", np.concatenate([s, -s]) * factor, off=i * T)
    lg = np.log(1.0 - 2.0 ** (-5.0 - np.arange(HR, dtype=np.float64)))
    j, i = np.arange(P)[:, None], np.arange(P)[None, :]
    for h in range(HR):
        diag = np.where(i >= j, np.exp((i - j) * lg[h]), 0.0)
        put("decay", np.concatenate([diag, np.exp((i + P - j) * lg[h]), diag], 1), off=384 * h)
        for ch in range(2):
            put("kdec", np.exp((TP - 1 - (ch * P + np.arange(P))) * lg[h])[:, None], off=ch * HR + h)
    q, k = np.arange(P)[:, None], np.arange(P)[None, :]
    causal = np.where(k <= q, 0.0, -1e30)
    put("mask", np.concatenate([causal, np.zeros((P, P)), causal], 1))
    c, s = angles(ROPE // 2)
    put("mla_c", np.concatenate([np.ones((NOPE, T)), c, c]), slice(0, QK))
    put("mla_s", np.concatenate([np.zeros((NOPE, T)), s, s]), slice(0, QK))
    put("ident", np.eye(P))
    put("ones", np.ones((P, P)))
    rot = np.zeros((QK, QK))
    half = ROPE // 2
    for a in range(half):
        rot[NOPE + half + a, NOPE + a] = -1.0
        rot[NOPE + a, NOPE + half + a] = 1.0
    put("rot", rot, slice(0, QK))
    return tab


def kernel(x_prompt, x_sample, p_prompt, p_sample, cache_ckv, cache_kpe, state_ret, state_conv, page_table,
           g_mix, w_in, w_dw, b_dw, g_cln, b_cln, w_conv_out, g_rgn, w_ret_out, g_qa, w_uq, g_qn, g_kva,
           w_uk, w_uv, g_kn, w_mla_out, w_out, g_ffn, w_gate, w_up, w_down, g_ple, w_ple_gate, w_ple_proj):
    import concourse.bacc as bacc
    from concourse.bass_utils import run_bass_kernel_spmd

    A = np.asarray

    def tiles(w):
        w = A(w)
        k, m = w.shape
        return w.reshape(k // P, P, m // P, P).transpose(2, 0, 1, 3)

    def blocks(t):
        t = t.reshape(-1, 8, P, P)
        return t.transpose(0, 2, 1, 3).reshape(-1, P, 8 * P)

    def paired(a, b):
        return np.stack([tiles(a), tiles(b)], 1).reshape(-1, KT, P, P)

    def layer_stream(l):
        w = A(w_in[l])
        c = np.cumsum([0, CONV, CONV, HR * DK, HR * DK, HR * DV, HR * DV, QL, KVL, ROPE, D, D, D])
        part = [w[:, c[i]:c[i + 1]] for i in range(len(c) - 1)]
        glu_a, glu_g, rq, rk, rv, rg, q_a, kv_a, _, ga, gb, gc = part
        kr = w[:, c[8] - NOPE:c[8] - NOPE + P]
        uq = A(w_uq[l]).reshape(3, P, HM, QK).transpose(1, 2, 0, 3).reshape(P, HM, 3 * QK)
        uq_blocks = []
        h = 0
        for n in UQ_HEADS:
            b = uq[:, h:h + n].reshape(P, n * 3 * QK)
            uq_blocks.append(np.concatenate([b, np.zeros((P, 8 * P - b.shape[1]), b.dtype)], 1))
            h += n
        return np.concatenate([
            blocks(paired(glu_a, glu_g)), blocks(tiles(rq)), blocks(tiles(rk)), blocks(tiles(rv)), blocks(tiles(rg)),
            blocks(tiles(ga)), blocks(tiles(w_conv_out[l])), blocks(tiles(gb)), blocks(tiles(w_ret_out[l])),
            blocks(tiles(q_a)), blocks(tiles(kv_a)), blocks(tiles(kr)), np.stack(uq_blocks),
            blocks(tiles(gc)), blocks(tiles(w_mla_out[l])), blocks(tiles(w_out[l])),
            blocks(paired(w_gate[l], w_up[l])), blocks(tiles(w_down[l])), blocks(tiles(w_ple_gate[l])), blocks(tiles(w_ple_proj[l])),
        ])

    def channel_major(prompt, sample, width):
        x = np.concatenate([A(prompt).reshape(TP, width), A(sample).reshape(NB, width)])
        return x.T.reshape(width // P, P, T).transpose(1, 0, 2)

    def vectors(l):
        def cols(g, n):
            g = A(g)
            if g.shape[0] < P:
                return np.concatenate([g, np.zeros(P - g.shape[0], g.dtype)]).reshape(P, 1)
            return g.reshape(n, P).T

        taps = A(w_dw[l]).T.reshape(CT, P, TAPS)
        taps = np.concatenate([taps, np.zeros((CT, P, 1), taps.dtype)], 2).transpose(1, 0, 2).reshape(P, CT * 32)
        return np.concatenate([cols(g_mix[l], KT), cols(g_ffn[l], KT), cols(g_ple[l], KT), taps, cols(b_dw[l], CT),
                               cols(g_cln[l], CT), cols(b_cln[l], CT), cols(g_rgn[l], KT), cols(g_qa[l], 3),
                               cols(g_kva[l], 2), cols(g_qn[l], 1), cols(g_kn[l], 1)], 1)

    L = range(DEPTH)
    n_phys = cache_ckv.shape[1]
    arrays = {
        "x": channel_major(x_prompt, x_sample, D),
        "p": np.stack([channel_major(p_prompt[l], p_sample[l], PLE) for l in L]),
        "stream": np.concatenate([layer_stream(l) for l in L]),
        "uk": np.stack([A(w_uk[l]).reshape(2, P, 512).transpose(1, 0, 2) for l in L]),
        "uv": np.stack([A(w_uv[l]).reshape(2, P, 512).transpose(1, 0, 2) for l in L]),
        "ukt": np.stack([A(w_uk[l]).reshape(KVL, HM, NOPE).transpose(2, 1, 0) for l in L]),
        "vec": np.stack([vectors(l) for l in L]).transpose(1, 0, 2),
        "tab": constants(),
        "ckv": A(cache_ckv).reshape(DEPTH * n_phys, PAGE, KVL),
        "kpe": A(cache_kpe).reshape(DEPTH * n_phys, PAGE, ROPE),
        "pages": A(page_table).reshape(1, NB * NT),
        "state": A(state_ret).reshape(DEPTH * NB, HR, DK, DV),
        "conv": A(state_conv).reshape(DEPTH, NB, TAPS - 1, CT, P).transpose(0, 4, 3, 1, 2),
    }
    outs = {"y": (P, KT, T), "ckv_o": (DEPTH, P, 2, T), "kpe_o": (DEPTH, ROPE, T), "ret_p": (DEPTH, HR, DK, DV),
            "ret_s": (DEPTH * NB, HR, DK, DV), "conv_p": (DEPTH, P, CT, TAPS - 1), "conv_s": (DEPTH, P, CT, NB, TAPS - 1)}
    nc = bacc.Bacc("TRN2", target_bir_lowering=False, num_devices=1)
    arrays = {f"in_{k}": np.ascontiguousarray(a) for k, a in arrays.items()}
    args = [nc.dram_tensor(n, a.shape, mybir.dt.from_np(a.dtype), kind="ExternalInput").ap() for n, a in arrays.items()]
    args += [nc.dram_tensor(f"out_{n}", s, F32, kind="ExternalOutput").ap() for n, s in outs.items()]
    build(nc, *args)
    r = run_bass_kernel_spmd(nc, [arrays], core_ids=[0]).results[0]

    y = r["out_y"].transpose(2, 1, 0).reshape(T, D)
    ckv_o = r["out_ckv_o"].transpose(0, 3, 2, 1).reshape(DEPTH, T, KVL)
    kpe_o = r["out_kpe_o"].transpose(0, 2, 1)
    conv_p = r["out_conv_p"].transpose(0, 3, 2, 1).reshape(DEPTH, 1, TAPS - 1, CONV)
    conv_s = r["out_conv_s"].transpose(0, 3, 4, 2, 1).reshape(DEPTH, NB, TAPS - 1, CONV)
    return (y[:TP].reshape(1, TP, D), y[TP:].reshape(NB, 1, D),
            ckv_o[:, :TP].reshape(DEPTH, 1, TP, KVL), kpe_o[:, :TP].reshape(DEPTH, 1, TP, ROPE),
            ckv_o[:, TP:].reshape(DEPTH, NB, 1, KVL), kpe_o[:, TP:].reshape(DEPTH, NB, 1, ROPE),
            r["out_ret_p"].reshape(DEPTH, 1, HR, DK, DV), r["out_ret_s"].reshape(DEPTH, NB, HR, DK, DV), conv_p, conv_s)
```

```python
from contextlib import ExitStack

import numpy as np
import concourse.bass as bass
from concourse import mybir

F32 = mybir.dt.float32
F32R = mybir.dt.float32r
I32 = mybir.dt.int32
ALU = mybir.AluOpType
ACT = mybir.ActivationFunctionType
AX = mybir.AxisListType
ds = bass.ds

P = 128
DEPTH, D, TP, NB = 2, 1024, 256, 8
T = TP + NB
KT = D // P
EPS = 1e-6
CONV, TAPS = 512, 31
CT = CONV // P
HR, DK, DV = 4, 128, 256
HM, NOPE, ROPE, VD = 8, 64, 32, 64
QK = NOPE + ROPE
QL, KVL = 384, 256
PAST, PAGE = 2048, 128
NT = PAST // PAGE
FF = 2816
FT = FF // P
PLE = 256
ATT_SCALE = QK ** -0.5

STAGES = [("glu", 8, 8), ("qk", 8, 8), ("v", 8, 8), ("rg", 8, 8), ("gate_a", 8, 8), ("conv_out", 4, 8),
          ("gate_b", 8, 8), ("ret_out", 8, 8), ("kvq", 6, 6), ("uq", 3, 8), ("gate_c", 8, 8), ("mla_out", 4, 8),
          ("w_out", 8, 8), ("ffn_in", 2 * FT, 2 * FT), ("ffn_out", FT, 8), ("ple_gate", 8, 8), ("ple_proj", 2, 8)]
B0, C0 = {}, {}
NBLK = NCHUNK = 0
for _name, _b, _c in STAGES:
    B0[_name], C0[_name] = NBLK, NCHUNK
    NBLK += _b
    NCHUNK += _c
RING = 4
UQ_HEADS = (3, 3, 2)

TAB = {}
_n = 0
for _name, _w in (("rope_c", 2 * T), ("rope_s", 2 * T), ("decay", HR * 384), ("mask", 384), ("mla_c", T), ("mla_s", T),
                  ("ident", P), ("ones", P), ("rot", QK), ("kdec", 2 * HR)):
    TAB[_name] = _n
    _n += _w
NTAB = _n
VEC = {}
_n = 0
for _name, _w in (("g_mix", KT), ("g_ffn", KT), ("g_ple", KT), ("w_dw", CT * 32), ("b_dw", CT), ("g_cln", CT),
                  ("b_cln", CT), ("g_rgn", KT), ("g_qa", 3), ("g_kva", 2), ("g_qn", 1), ("g_kn", 1)):
    VEC[_name] = _n
    _n += _w
NVEC = _n

GAMMA = [1.0 - 2.0 ** (-5.0 - h) for h in range(HR)]


def build(nc, x_in, p_in, stream, uk_in, uv_in, ukt_in, vec_in, tab_in, cache_in, pages_in, state_in, conv_in,
          y_out, ckv_out, kpe_out, ret_prompt_out, ret_sample_out, conv_prompt_out, conv_sample_out):
    ctx = ExitStack()
    with ctx:
        base = -(-nc.sbuf_base // 32) * 32
        top = [0]
        names = {}

        def at_offset(name, cols, offset, dt=F32, shape=None):
            names[name] = (offset, cols * 4)
            return nc.alloc_sbuf_tensor_at(name, [P] + (shape or [cols]), dt, offset=base + offset)

        def place(name, shape, dt=F32):
            cols = int(np.prod(shape))
            off = top[0]
            top[0] += -(-cols * 4 // 32) * 32
            return at_offset(name, cols, off, dt, list(shape))

        xT = place("xT", [KT, T])
        h_hi = place("h_hi", [KT, T], F32R)
        h_lo = place("h_lo", [KT, T], F32R)
        w_raw = [place(f"w_raw{r}", [8 * P]) for r in range(RING)]
        w_hi = [place(f"w_hi{r}", [8 * P], F32R) for r in range(RING)]
        w_lo = [place(f"w_lo{r}", [8 * P], F32R) for r in range(RING)]
        tab = place("tab", [NTAB])
        vecs = place("vecs", [DEPTH, NVEC])
        vec = place("vec", [NVEC])
        pages = place("pages", [NB * NT], I32)
        uk = place("uk", [2, 512])
        uv = place("uv", [2, 512])
        off_ukh = top[0]
        UKW = 512 + HM
        UKA, UKB = slice(0, 256 + HM), slice(256 + HM, UKW)
        uk_hi = place("uk_hi", [2, UKW], F32R)
        uk_lo = place("uk_lo", [2, UKW], F32R)
        off_ukt = top[0]
        uk_t = place("uk_t", [HM, 256])
        zt = place("zt", [4, T])
        et = place("et", [4, T])
        rstd = place("rstd", [T])
        rsb = place("rsb", [2, T])

        kpe_own = place("kpe_own", [T])
        ckv_own = place("ckv_own", [2, NB])
        own = place("own", [HM, NB])
        qt_hi = place("qt_hi", [NB, 2, HM], F32R)
        qt_lo = place("qt_lo", [NB, 2, HM], F32R)
        qpe4 = place("qpe4", [NB, HM])
        lat = place("lat", [2, HM, NB])
        small = place("small", [96])
        q_pe = [place(f"q_pe{i}", [4, HM]) for i in range(3)]
        off_mix = top[0]
        mix = place("mix", [KT, T])
        off_g = top[0]
        gate = place("gate", [KT, T])
        off_s = top[0]
        s_hi = place("s_hi", [KT, T], F32R)
        s_lo = place("s_lo", [KT, T], F32R)
        off_u = top[0]
        a_hi = at_offset("a_hi", FT * T, off_g, F32R, [FT, T])
        a_lo = at_offset("a_lo", FT * T, off_g + FT * T * 4, F32R, [FT, T])
        p_raw = at_offset("p_raw", 2 * T, -(-(off_g + 2 * FT * T * 4) // 32) * 32, F32, [2, T])
        p_hi = at_offset("p_hi", 2 * T, off_s, F32R, [2, T])
        p_lo = at_offset("p_lo", 2 * T, off_s + 2 * T * 4, F32R, [2, T])
        yconv = at_offset("yconv", CT * T, off_mix, F32, [CT, T])
        o = off_u
        u_ext = at_offset("u_ext", CT * 288, o, F32, [CT, 288])
        u_smp = at_offset("u_smp", CT * NB * 31, o + CT * 288 * 4, F32, [CT, NB, 31])
        oT = at_offset("oT", KT * T, o, F32, [KT, T])
        o += CT * 288 * 4 + CT * NB * 31 * 4
        qk = at_offset("qk", KT * T, o, F32, [KT, T]); o += KT * T * 4
        v_nat = at_offset("v_nat", 2 * 1024, o, F32, [2, 1024]); o += 8192
        v_smp = at_offset("v_smp", 1024, o, F32, [1024])
        conv_stage = at_offset("conv_stage", CT * NB * 30, o, F32, [CT, NB, 30]); o += 4096
        k_nat = at_offset("k_nat", 2 * 512, o, F32, [2, 512]); o += 4096
        k_smp = at_offset("k_smp", 512, o, F32, [512]); o += 2048
        rgs = at_offset("rgs", KT * T, o, F32, [KT, T])
        conv_prod = at_offset("conv_prod", CT * NB * 31, o, F32, [CT, NB, 31])
        conv_new = at_offset("conv_new", CT * NB * 30, o + CT * NB * 31 * 4, F32, [CT, NB, 30]); o += KT * T * 4
        end1 = o
        state = [at_offset(f"state{i}", 1024, off_ukt + 4096 * i, F32, [HR, DV]) for i in range(2)]
        sT = [at_offset(f"sT{i}", 384, off_ukh + 1536 * i, F32, [384]) for i in range(2)]
        k_mask = [at_offset(f"k_mask{i}", 512, off_ukh + 3072 + 2048 * i, F32, [512]) for i in range(2)]
        ret_stage = at_offset("ret_stage", 1024, names["zt"][0], F32, [HR, DV])
        KV = KVL + ROPE
        cache = [at_offset(f"cache{i}", NT * KV, (off_u, off_u + NT * KV * 4, off_g)[i], F32, [NT, KV]) for i in range(3)]
        o = off_u + 2 * NT * KV * 4
        vm = at_offset("vm", 2 * 512, o, F32, [2, 512])
        sq = [at_offset(f"sq{i}", 512, names["et"][0] + 2048 * i, F32, [HM, 64]) for i in range(2)]
        o += 4096
        ssq = [at_offset(f"ssq{i}", NT * HM, o + 512 * i, F32, [NT, HM]) for i in range(3)]
        sspe = [at_offset(f"sspe{i}", NT, o + 1536 + 64 * i, F32, [NT]) for i in range(3)]
        kn_r = at_offset("kn_r", NT * HM, o + 1728, F32, [NT, HM])
        sc = at_offset("sc", NT * HM, o + 2240, F32, [NT, HM])
        pr = at_offset("pr", NT * HM, o + 2752, F32, [NT, HM])
        scores = [at_offset(f"scores{i}", NT * HM, o + 3264 + 512 * i, F32, [NT, HM]) for i in range(3)]
        scores_pe = [at_offset(f"scores_pe{i}", NT * HM, off_g + NT * KV * 4 + 512 * i, F32, [NT, HM]) for i in range(3)]
        latn = at_offset("latn", KVL, names["rsb"][0])
        kpeT = at_offset("kpeT", 512, o - 4096, F32, [4, P])
        kpe_n = at_offset("kpe_n", 512, o - 2048, F32, [NT, ROPE])
        end2 = o + 4800
        qm = at_offset("qm", HM * T, off_g, F32, [HM, T])
        sqg = at_offset("sqg", 5 * T, off_g, F32, [5, T])
        qa_hi = at_offset("qa_hi", 3 * T, off_s, F32R, [3, T])
        qa_lo = at_offset("qa_lo", 3 * T, off_s + 3 * T * 4, F32R, [3, T])
        ckvT = at_offset("ckvT", 2 * T, off_s + 6 * T * 4, F32, [2, T])
        km = at_offset("km", HM * T, off_s + 8 * T * 4, F32, [HM, T])
        ap_s = [at_offset(f"ap_s{i}", 384, off_ukh + 1536 * i, F32, [384]) for i in range(2)]
        ap_t = [at_offset(f"ap_t{i}", 384, off_ukh + 3072 + 1536 * i, F32, [384]) for i in range(2)]
        oM = at_offset("oM", 4 * T, names["zt"][0], F32, [4, T])
        ct_hi = [at_offset(f"ct_hi{i}", 512, off_ukt + 4096 * i, F32R, [4, P]) for i in range(2)]
        ct_lo = [at_offset(f"ct_lo{i}", 512, off_ukt + 4096 * i + 2048, F32R, [4, P]) for i in range(2)]
        cv_hi, cv_lo = s_hi, s_lo
        a_end = off_g + 2 * FT * T * 4
        total = max(end1, end2, a_end)
        assert base + total <= nc.sbuf_usable_end, (base, total, end1, end2, a_end, nc.sbuf_usable_end)
        ctx.enter_context(nc.sbuf_tensor("arena", [P, (base + total - nc.sbuf_base) // 4 + 1], F32))

        bank = [ctx.enter_context(nc.psum_tensor(f"bank{i}", [P, 512], F32)) for i in range(8)]

        DMA = 16

        class Sem:

            def __init__(self, name, per=1, credit=0):
                self.s = ctx.enter_context(nc.semaphore(name))
                self.per, self.credit = per, credit

            def at(self, l, n):
                return l * self.per + (n + self.credit)

        settled = {e: Sem(f"settled_{i}") for i, e in enumerate((nc.sync.engine, nc.gpsimd.engine, nc.tensor.engine, nc.vector.engine))}

        def settle(eng):
            eng.sem_inc(settled[eng.engine].s, 1)

        class Steps:

            def __init__(self):
                self.n = 0

            def one(self):
                self.n += 1
                return 1

        def col(name, k=0):
            return vec[:, VEC[name] + k:VEC[name] + k + 1]

        def tb(name, w, a=0, rows=slice(0, P)):
            return tab[rows, TAB[name] + a:TAB[name] + a + w]

        ident = tb("ident", P)
        ones = tb("ones", P)

        tables_loaded = Sem("tables_loaded")
        w_loaded = [Sem(f"w_loaded{r}", 16 * ((NBLK - r + RING - 1) // RING)) for r in range(RING)]
        w_split = Sem("w_split", NBLK, 1)
        w_high = Sem("w_high", NBLK)
        w_begun = Sem("w_begun", NBLK)
        chunk_ready = Sem("chunk_ready", NCHUNK)
        chunk_free = Sem("chunk_free", NCHUNK, 4)
        h_high = Sem("h_high", 3 * KT)
        h_low = Sem("h_low", 3 * KT)
        x_sq = Sem("x_sq", 3 * KT)
        x_sum = Sem("x_sum", 3 * KT)
        x_root = Sem("x_root", 3)

        NEXP = 4 + 8 + 24 + FT + 8
        exp_ready = Sem("exp_ready", NEXP)
        E0 = {"glu": 0, "rg": 4, "gate_a": 12, "gate_b": 20, "gate_c": 28, "ffn_in": 36, "ple_gate": 36 + FT}
        vec_ready = Sem("vec_ready")
        conv_state_loaded = Sem("conv_state_loaded", 16)
        conv_state_placed = Sem("conv_state_placed")
        conv_biased = Sem("conv_biased")
        u_ready = Sem("u_ready")
        conv_new_ready = Sem("conv_new_ready")
        conv_stored = Sem("conv_stored", 32)
        rope_ready = Sem("rope_ready", 2)
        k_turned = Sem("k_turned")
        k_copied = Sem("k_copied")
        v_turned = Sem("v_turned", 2)
        v_copied = Sem("v_copied", 2, 1)
        conv_done = Sem("conv_done")
        cln_sum = Sem("cln_sum", 2)
        cln_centred = Sem("cln_centred")
        cln_sq = Sem("cln_sq")
        cln_root = Sem("cln_root")
        cln_y = Sem("cln_y")
        cln_exp = Sem("cln_exp")
        conv_act = Sem("conv_act")
        conv_high = Sem("conv_high")
        conv_split = Sem("conv_split")
        ret_s = Sem("ret_s", HR)
        ret_sd = Sem("ret_sd", HR)
        ret_o = Sem("ret_o", HR)
        ret_oc = Sem("ret_oc", HR)
        ret_st = Sem("ret_st", HR)
        ret_stc = Sem("ret_stc", HR)
        ret_stored = Sem("ret_stored", 16)
        st_loaded = [Sem(f"st_loaded{i}", 64) for i in range(2)]
        st_stored = [Sem(f"st_stored{i}", 64) for i in range(2)]
        st_mask = Sem("st_mask", NB)
        st_outer = Sem("st_outer", NB)
        st_new = Sem("st_new", NB)
        st_o = Sem("st_o", NB)
        st_oc = Sem("st_oc", NB)
        gn_sum = Sem("gn_sum", HR)
        gn_c = Sem("gn_c", HR)
        gn_sq = Sem("gn_sq", HR)
        gn_var = Sem("gn_var", HR)
        gn_root = Sem("gn_root", HR)
        gn_y = Sem("gn_y", HR)
        gn_high = Sem("gn_high", HR)
        gn_low = Sem("gn_low", HR)
        mla_w_loaded = Sem("mla_w_loaded", 32)
        p_loaded = Sem("p_loaded", 16)
        ukt_loaded = Sem("ukt_loaded", 16)
        kvq_act = Sem("kvq_act", 5)
        qa_low = Sem("qa_low")
        kvq_sum = Sem("kvq_sum", 2)
        kvq_root = Sem("kvq_root", 2)
        kvq_r = Sem("kvq_r", 2)
        ckv_ready = Sem("ckv_ready")
        kr_rot = Sem("kr_rot")
        kpe_ready = Sem("kpe_ready")
        own_stored = Sem("own_stored", 32)
        uq_rot = Sem("uq_rot", HM)
        q_roped = Sem("q_roped", HM)
        hn_sq = Sem("hn_sq", 2 * HM)
        hn_sum = Sem("hn_sum", 2 * HM)
        hn_root = Sem("hn_root", 2 * HM)
        hn_done = Sem("hn_done", 2 * HM)
        kn_ready = Sem("kn_ready", HM)
        kn_copied = Sem("kn_copied", HM)
        vm_ready = Sem("vm_ready")
        vm_copied = Sem("vm_copied")
        own_prod = Sem("own_prod")
        qg_ready = Sem("qg_ready")
        own_sum = Sem("own_sum")
        own_copied = Sem("own_copied")
        qt_ready = Sem("qt_ready")
        qt_high = Sem("qt_high")
        qt_low = Sem("qt_low")
        at_s = Sem("at_s", HM)
        at_m = Sem("at_m", HM)
        at_p = Sem("at_p", HM)
        at_n = Sem("at_n", HM)
        at_t = Sem("at_t", HM)
        at_tc = Sem("at_tc", HM)
        at_o = Sem("at_o", HM)
        at_oc = Sem("at_oc", HM)
        uk_high = Sem("uk_high")
        uk_low = Sem("uk_low")
        ck_loaded = [Sem(f"ck_loaded{i}", 16 * NT * ((NB - i + 2) // 3)) for i in range(3)]
        c_kst = Sem("c_kst", NB)
        c_kt = Sem("c_kt", NB)
        c_ktc = Sem("c_ktc", NB)
        c_ksq = Sem("c_ksq", NB)
        c_kss = Sem("c_kss", NB)
        c_q = Sem("c_q", NB)
        q_pe_zeroed = Sem("q_pe_zeroed")
        c_tr = Sem("c_tr", NB * 8)
        c_hi = Sem("c_hi", NB * 8)
        c_lo = Sem("c_lo", NB * 8)
        c_kn = Sem("c_kn", NB * NT)
        c_sq = Sem("c_sq", NB * NT)
        c_ss = Sem("c_ss", NB * NT)
        c_sr = Sem("c_sr", NB * NT)
        c_pe = Sem("c_pe", NB)
        c_pec = Sem("c_pec", NB)
        t_cp = Sem("t_cp", NB)
        t_tr = Sem("t_tr", NB)
        t_tot = Sem("t_tot", NB)
        t_root = Sem("t_root", NB)
        t_s = Sem("t_s", NB)
        t_mx = Sem("t_mx", NB)
        t_mt = Sem("t_mt", NB)
        t_dg = Sem("t_dg", NB)
        t_bc = Sem("t_bc", NB)
        t_shift = Sem("t_shift", NB)
        t_p = Sem("t_p", NB)
        t_l = Sem("t_l", NB)
        t_lat = Sem("t_lat", NB)
        t_fin = Sem("t_fin", NB)
        uvs_ready = Sem("uvs_ready")
        uvs_copied = Sem("uvs_copied")
        mla_high = Sem("mla_high")
        mla_split = Sem("mla_split")
        mix_done = Sem("mix_done", KT)
        mix_high = Sem("mix_high", KT)
        mix_low = Sem("mix_low", KT)
        ffn_a = Sem("ffn_a", FT)
        ffn_high = Sem("ffn_high", FT)
        ffn_low = Sem("ffn_low", FT)
        p_high = Sem("p_high")
        p_low = Sem("p_low")
        x_final = Sem("x_final")
        act_step = Sem("act_step")
        dve_step = Sem("dve_step")
        y_stored = Sem("y_stored", 16)

        GATES = ("gate_a", "gate_b", "gate_c", "ple_gate")
        GATE_OF = {"conv_out": "gate_a", "ret_out": "gate_b", "mla_out": "gate_c"}
        block = ctx.enter_context(nc.Block())
        CUT_RET = (B0["conv_out"] + RING) // RING * RING
        CUT_CACHE = (B0["gate_c"] + RING) // RING * RING

        CUT_P = B0["ffn_in"] // RING * RING + RING

        @block.sync
        def _(sp):
            sp.dma_start(tab[:, :], tab_in).then_inc(tables_loaded.s, DMA)
            sp.dma_start(xT[:, :, :], x_in).then_inc(tables_loaded.s, DMA)
            sp.dma_start(vecs[:, :, :], vec_in).then_inc(tables_loaded.s, DMA)
            sp.dma_start(pages[0:1, :], pages_in).then_inc(tables_loaded.s, DMA)
            sp.wait_ge(tables_loaded.s, 4 * DMA)

            with sp.Fori(0, DEPTH) as l:
                def load_block(n, r, reuse):
                    sp.wait_ge(w_split.s, w_split.at(l, reuse))
                    sp.dma_start(w_raw[r][:, :], stream[ds(l * NBLK + n, 1)].rearrange("o p c -> (o p) c"))\
                        .then_inc(w_loaded[r].s, DMA)

                def load_blocks(a, b):
                    whole = (b - a) // RING
                    if whole > 0:
                        with sp.Fori(0, whole) as j:
                            for r in range(RING):
                                load_block(j * RING + (a + r), r, j * RING + (a + r - RING + 1))
                    for n in range(a + whole * RING, b):
                        load_block(n, n % RING, n - RING + 1)

                sp.wait_ge(w_split.s, w_split.at(l, 0))
                sp.dma_start(conv_stage[:, :, :, :], conv_in[ds(l, 1)].rearrange("o p c b w -> (o p) c b w"))\
                    .then_inc(conv_state_loaded.s, DMA)
                for r in range(RING):
                    load_block(r, r, 0)
                load_blocks(RING, CUT_RET)
                sp.dma_start(uk[:, :, :], uk_in[ds(l, 1)].rearrange("o p c n -> (o p) c n")).then_inc(mla_w_loaded.s, DMA)
                sp.dma_start(uv[:, :, :], uv_in[ds(l, 1)].rearrange("o p c n -> (o p) c n")).then_inc(mla_w_loaded.s, DMA)

                def load_state(b, i):
                    sp.dma_start(state[i][:, :, :], state_in[ds(l * NB + b, 1)].rearrange("o h d e -> d (o h) e"))\
                        .then_inc(st_loaded[i].s, DMA)

                def store_state(b, i):
                    sp.wait_ge(st_new.s, st_new.at(l, b + 1))
                    sp.dma_start(ret_sample_out[ds(l * NB + b, 1)].rearrange("o h d e -> d (o h) e"), state[i][:, :, :])\
                        .then_inc(st_stored[i].s, DMA)

                for i in range(2):
                    load_state(i, i)
                with sp.Fori(0, NB // 2 - 1) as j:
                    for i in range(2):
                        store_state(j * 2 + i, i)
                        st = st_stored[i]
                        sp.wait_ge(st.s, st.at(l, DMA) + j * DMA)
                        sp.wait_ge(st_o.s, st_o.at(l, j * 2 + (i + 1)))
                        load_state(j * 2 + (i + 2), i)
                for i in range(2):
                    store_state(NB - 2 + i, i)
                for i in range(2):
                    sp.wait_ge(st_stored[i].s, st_stored[i].at(l, 64))
                sp.wait_ge(st_o.s, st_o.at(l, NB))
                sp.dma_start(uk_t[0:NOPE, :, :], ukt_in[ds(l, 1)].rearrange("o p c n -> (o p) c n")).then_inc(ukt_loaded.s, DMA)
                load_blocks(CUT_RET, CUT_CACHE)

                n_phys = cache_in.shape[0] // DEPTH
                def load_cache(b, i):
                    with sp.Fori(0, NT // 4) as g:
                        for u in range(4):
                            page = sp.value_load(pages[0:1, ds(g * 4 + (b * NT + u), 1)], min_val=0, max_val=n_phys - 1)
                            sp.dma_start(cache[i][:, ds(g * 4 + u, 1), :].rearrange("p t c -> p (t c)"),
                                         cache_in[ds(page + l * n_phys, 1)].rearrange("o p c -> (o p) c")).then_inc(ck_loaded[i].s, DMA)

                sp.wait_ge(gn_low.s, gn_low.at(l, HR))
                sp.wait_ge(gn_high.s, gn_high.at(l, HR))
                sp.wait_ge(ret_stored.s, ret_stored.at(l, DMA))
                settle(sp)
                load_cache(0, 0)
                load_cache(1, 1)
                sp.wait_ge(at_oc.s, at_oc.at(l, HM))
                sp.wait_ge(own_stored.s, own_stored.at(l, 32))
                settle(sp)
                load_cache(2, 2)
                for b in range(3, NB):
                    sp.wait_ge(t_lat.s, t_lat.at(l, b - 2))
                    sp.wait_ge(c_ksq.s, c_ksq.at(l, b - 2))
                    settle(sp)
                    load_cache(b, b % 3)
                load_blocks(CUT_CACHE, CUT_P)
                sp.wait_ge(t_fin.s, t_fin.at(l, NB))
                sp.dma_start(p_raw[:, :, :], p_in[ds(l, 1)].rearrange("o p c n -> (o p) c n")).then_inc(p_loaded.s, DMA)
                load_blocks(CUT_P, NBLK)

            sp.wait_ge(conv_stored.s, DEPTH * 32)
            sp.wait_ge(ret_stored.s, DEPTH * DMA)
            sp.wait_ge(own_stored.s, DEPTH * 32)
            for i in range(2):
                sp.wait_ge(st_stored[i].s, DEPTH * 64)
            sp.wait_ge(x_final.s, 1)
            sp.dma_start(y_out, xT[:, :, :]).then_inc(y_stored.s, DMA)
            sp.wait_ge(y_stored.s, DMA)

        @block.gpsimd
        def _(pool):
            pool.sem_inc(w_split.s, 1)
            with pool.Fori(0, DEPTH) as l:
                def cut_low(n, r):
                    pool.wait_ge(w_high.s, w_high.at(l, n + 1))
                    pool.tensor_tensor(w_lo[r][:, :], w_raw[r][:, :], w_hi[r][:, :].bitcast(F32), ALU.subtract)\
                        .then_inc(w_split.s, 1)

                with pool.Fori(0, NBLK // RING) as j:
                    for r in range(RING):
                        cut_low(j * RING + r, r)
                for n in range(NBLK // RING * RING, NBLK):
                    cut_low(n, n % RING)

        @block.tensor
        def _(pe):
            mm = pe.matmul
            pe.wait_ge(tables_loaded.s, 4 * DMA)
            rot = tb("rot", QK, 0, slice(0, QK))

            def three(out, w, rhs, first, last):
                a = mm(out, w[0], rhs[0], start=first, stop=False)
                mm(out, w[0], rhs[1], start=False, stop=False)
                return a, mm(out, w[1], rhs[0], start=False, stop=last)

            with pe.Fori(0, DEPTH) as l:
                def chunk(c, c_static, run, rhs, M=P, wait_k=None):
                    pe.wait_ge(chunk_free.s, chunk_free.at(l, c - 3))
                    out = bank[c_static % 4][0:M, 0:T]
                    for k, (n, n_static, a) in enumerate(run):
                        s = n_static % RING
                        if a == 0:
                            pe.wait_ge(w_split.s, w_split.at(l, n + 1))
                        if wait_k is not None:
                            wait_k(k)
                        first, last = three(out, (w_hi[s][:, a:a + M], w_lo[s][:, a:a + M]),
                                            (rhs[0][:, k, :], rhs[1][:, k, :]), k == 0, k == len(run) - 1)
                        if a == 0:
                            first.then_inc(w_begun.s, 1)
                    last.then_inc(chunk_ready.s, 1)

                def group(stage, i, rhs, wait_k=None):
                    for r in range(4):
                        n, c = B0[stage] + r, C0[stage] + r
                        chunk(i * 4 + c, c, [(i * 4 + n, n, k * P) for k in range(KT)], rhs, wait_k=wait_k if r == 0 else None)

                def stream_chunk(stage, m, kt, rhs, wait_k=None):
                    t0 = m * kt
                    chunk(C0[stage] + m, C0[stage] + m,
                          [(B0[stage] + (t0 + k) // 8, B0[stage] + (t0 + k) // 8, (t0 + k) % 8 * P) for k in range(kt)],
                          rhs, wait_k=wait_k)

                h = (h_hi, h_lo)
                s_ = (s_hi, s_lo)

                def token_sums(w):
                    for k in range(KT):
                        pe.wait_ge(x_sq.s, x_sq.at(l, w * KT + k + 1))
                        mm(bank[4][:, 0:T], ones, (et if k < 4 else zt)[:, k % 4, :], start=k == 0, stop=k == KT - 1).then_inc(x_sum.s, 1)

                def h_there(w):
                    return lambda k: pe.wait_ge(h_low.s, h_low.at(l, w * KT + k + 1))

                pe.wait_ge(chunk_free.s, chunk_free.at(l, 0))
                token_sums(0)
                with pe.Fori(0, 2) as i:
                    group("glu", i, h, h_there(0))
                with pe.Fori(0, 2) as i:
                    group("qk", i, h)
                pe.wait_ge(rope_ready.s, rope_ready.at(l, 2))
                pe.wait_ge(x_root.s, x_root.at(l, 1))
                for hd in range(HR):
                    for c in range(2):
                        pe.transpose(bank[4 + c][:, hd * P:hd * P + P], qk[:, HR + hd, c * P:c * P + P], ident)
                    ins = pe.transpose(bank[6][0:NB, hd * P:hd * P + P], qk[:, HR + hd, TP:T], ident)
                ins.then_inc(k_turned.s, 1)
                pe.wait_ge(k_copied.s, k_copied.at(l, 1))
                settle(pe)
                with pe.Fori(0, 2) as i:
                    group("v", i, h)
                    pe.wait_ge(v_copied.s, v_copied.at(l, i))
                    pe.wait_ge(chunk_free.s, chunk_free.at(l, i * 4 + (C0["v"] + 4)))
                    for r in range(4):
                        for c in range(2):
                            pe.transpose(bank[4 + c][:, r * P:r * P + P], zt[:, r, c * P:c * P + P], ident)
                        ins = pe.transpose(bank[6][0:NB, r * P:r * P + P], zt[:, r, TP:T], ident)
                    ins.then_inc(v_turned.s, 1)
                with pe.Fori(0, 2) as i:
                    group("rg", i, h)
                with pe.Fori(0, 2) as i:
                    group("gate_a", i, h)

                pe.wait_ge(conv_done.s, conv_done.at(l, 1))
                pe.wait_ge(v_copied.s, v_copied.at(l, 2))
                for c in range(CT):
                    ins = mm(bank[4][:, 0:T], ones, yconv[:, c, :], start=c == 0, stop=c == CT - 1)
                ins.then_inc(cln_sum.s, 1)
                pe.wait_ge(cln_sq.s, cln_sq.at(l, 1))
                for c in range(CT):
                    ins = mm(bank[5][:, 0:T], ones, et[:, c, :], start=c == 0, stop=c == CT - 1)
                ins.then_inc(cln_sum.s, 1)

                def ret_scores(hd):
                    b = bank[4 + hd % 2]
                    if hd >= 2:
                        pe.wait_ge(ret_sd.s, ret_sd.at(l, hd - 1))
                    mm(b[:, 0:TP], qk[:, HR + hd, 0:P], qk[:, hd, 0:TP], start=True, stop=True)
                    mm(b[:, TP:TP + P], qk[:, HR + hd, P:TP], qk[:, hd, P:TP], start=True, stop=True).then_inc(ret_s.s, 1)

                pe.wait_ge(cln_root.s, cln_root.at(l, 1))
                ret_scores(0)
                ret_scores(1)
                for hd in range(HR):
                    pe.wait_ge(ret_sd.s, ret_sd.at(l, hd + 1))
                    if hd:
                        pe.wait_ge(ret_oc.s, ret_oc.at(l, hd))
                    for e in range(2):
                        o = bank[6][:, e * TP:e * TP + TP]
                        v0 = hd * DV + e * P
                        mm(o, v_nat[:, 0, v0:v0 + P], sT[hd % 2][:, 0:TP], start=True, stop=False)
                        ins = mm(o[:, P:TP], v_nat[:, 1, v0:v0 + P], sT[hd % 2][:, TP:TP + P], start=False, stop=True)
                    ins.then_inc(ret_o.s, 1)
                    if hd:
                        pe.wait_ge(ret_stc.s, ret_stc.at(l, hd))
                    for c in range(2):
                        ins = mm(bank[7][:, 0:DV], k_nat[:, c, hd * P:hd * P + P], v_nat[:, c, hd * DV:hd * DV + DV],
                                 start=c == 0, stop=c == 1)
                    ins.then_inc(ret_st.s, 1)
                    if hd + 2 < HR:
                        ret_scores(hd + 2)

                pe.wait_ge(ret_oc.s, ret_oc.at(l, HR))
                settle(pe)
                with pe.Fori(0, NB // 2) as j:
                    for i in range(2):
                        b = j * 2 + i
                        pe.wait_ge(st_mask.s, st_mask.at(l, b + 1))
                        for hd in range(HR):
                            ins = mm(bank[4 + hd // 2][:, hd % 2 * DV:hd % 2 * DV + DV], k_mask[i][0:NB, hd * P:hd * P + P],
                                     v_smp[0:NB, hd * DV:hd * DV + DV], start=True, stop=True)
                        ins.then_inc(st_outer.s, 1)
                        pe.wait_ge(st_new.s, st_new.at(l, b + 1))
                        for hd in range(HR):
                            for e in range(2):
                                m = 2 * hd + e
                                ins = mm(bank[6][:, m:m + 1], state[i][:, hd, e * P:e * P + P],
                                         qk[:, hd, ds(b + TP, 1)], start=True, stop=True)
                        ins.then_inc(st_o.s, 1)

                pe.wait_ge(conv_split.s, conv_split.at(l, 1))
                for m in range(KT):
                    stream_chunk("conv_out", m, CT, (cv_hi, cv_lo))

                pe.wait_ge(st_oc.s, st_oc.at(l, NB))
                pe.wait_ge(ret_stc.s, ret_stc.at(l, HR))
                for hd in range(HR):
                    for e in range(2):
                        ins = mm(bank[4 + hd][:, 0:T], ones, oT[:, 2 * hd + e, :], start=e == 0, stop=e == 1)
                    ins.then_inc(gn_sum.s, 1)
                for hd in range(HR):
                    pe.wait_ge(gn_sq.s, gn_sq.at(l, hd + 1))
                    for e in range(2):
                        ins = mm(bank[4 + hd][:, 0:T], ones, et[:, 2 * (hd % 2) + e, :], start=e == 0, stop=e == 1)
                    ins.then_inc(gn_var.s, 1)

                with pe.Fori(0, 2) as i:
                    group("gate_b", i, h)
                pe.wait_ge(gn_low.s, gn_low.at(l, HR))
                settle(pe)
                with pe.Fori(0, 2) as i:
                    group("ret_out", i, s_)

                for m in range(6):
                    n, c = B0["kvq"] + m, C0["kvq"] + m
                    chunk(c, c, [(n, n, k * P) for k in range(KT)], h)
                pe.wait_ge(kvq_act.s, kvq_act.at(l, 3))
                pe.wait_ge(gn_root.s, gn_root.at(l, HR))
                for k in range(3):
                    ins = mm(bank[4][:, 0:T], ones, sqg[:, k, :], start=k == 0, stop=k == 2)
                ins.then_inc(kvq_sum.s, 1)
                pe.wait_ge(kvq_act.s, kvq_act.at(l, 5))
                for k in range(2):
                    ins = mm(bank[5][:, 0:T], ones, sqg[:, 3 + k, :], start=k == 0, stop=k == 1)
                ins.then_inc(kvq_sum.s, 1)
                pe.wait_ge(chunk_free.s, chunk_free.at(l, C0["kvq"] + 6))
                mm(bank[6][0:QK, 0:T], rot, zt[0:QK, 1, :], start=True, stop=True).then_inc(kr_rot.s, 1)

                def head_sum(k, buf_bank):
                    pe.wait_ge(hn_sq.s, hn_sq.at(l, k + 1))
                    if k >= 2:
                        pe.wait_ge(hn_root.s, hn_root.at(l, k - 1))
                    mm(buf_bank[0:QK, 0:T], ones[0:QK, 0:QK], et[0:QK, k % 4, :], start=True, stop=True).then_inc(hn_sum.s, 1)

                pe.wait_ge(qa_low.s, qa_low.at(l, 1))
                pe.wait_ge(kvq_root.s, kvq_root.at(l, 2))
                pe.wait_ge(kpe_ready.s, kpe_ready.at(l, 1))
                for step in range(HM + 3):
                    if step < HM:
                        g = min(step // 3, 2)
                        n, c = B0["uq"] + g, C0["uq"] + step
                        chunk(c, c, [(n, n, ((step - 3 * g) * 3 + k) * QK) for k in range(3)], (qa_hi, qa_lo), M=QK)
                    hd = step - 1
                    if 0 <= hd < HM:
                        pe.wait_ge(chunk_free.s, chunk_free.at(l, C0["uq"] + hd + 1))
                        if hd >= 2:
                            pe.wait_ge(q_roped.s, q_roped.at(l, hd - 1))
                        mm(bank[4 + hd % 2][0:QK, 0:T], rot, qm[0:QK, hd, :], start=True, stop=True).then_inc(uq_rot.s, 1)
                    hd = step - 3
                    if hd >= 0:
                        head_sum(hd, bank[6 + hd % 2])
                pe.wait_ge(mla_w_loaded.s, mla_w_loaded.at(l, 32))
                pe.wait_ge(q_roped.s, q_roped.at(l, HM))
                pe.wait_ge(ckv_ready.s, ckv_ready.at(l, 1))
                for step in range(HM + 2):
                    if step < HM:
                        if step >= 2:
                            pe.wait_ge(kn_copied.s, kn_copied.at(l, step - 1))
                        for c in range(2):
                            ins = mm(bank[4 + step % 2][0:NOPE, 0:T], uk[:, c, step * NOPE:step * NOPE + NOPE], ckvT[:, c, :],
                                     start=c == 0, stop=c == 1)
                        ins.then_inc(kn_ready.s, 1)
                    if step >= 2:
                        head_sum(HM + step - 2, bank[6 + step % 2])
                pe.wait_ge(kn_copied.s, kn_copied.at(l, HM))
                for c in range(2):
                    for k in range(2):
                        ins = mm(bank[4 + c][:, :], ckvT[:, k, c * P:c * P + P], uv[:, k, :], start=k == 0, stop=k == 1)
                ins.then_inc(vm_ready.s, 1)
                pe.wait_ge(hn_root.s, hn_root.at(l, 2 * HM))
                pe.wait_ge(own_prod.s, own_prod.at(l, 1))
                mm(bank[6][:, 0:HM * NB], ones[0:QK, :], et[0:QK, 0, 0:HM * NB], start=True, stop=True).then_inc(own_sum.s, 1)
                pe.wait_ge(qg_ready.s, qg_ready.at(l, 1))
                pe.wait_ge(ukt_loaded.s, ukt_loaded.at(l, DMA))
                for hd in range(HM):
                    for c in range(2):
                        o = (c * HM + hd) * NB
                        ins = mm(bank[7][:, o:o + NB], uk_t[0:NOPE, hd, c * P:c * P + P], et[0:NOPE, 1, hd * NB:hd * NB + NB],
                                 start=True, stop=True)
                ins.then_inc(qt_ready.s, 1)

                def att_scores(hd):
                    b = bank[4 + hd % 2]
                    if hd >= 2:
                        pe.wait_ge(at_m.s, at_m.at(l, hd - 1))
                    mm(b[:, 0:P], qm[0:QK, hd, 0:P], km[0:QK, hd, 0:P], start=True, stop=True)
                    mm(b[:, P:3 * P], qm[0:QK, hd, P:TP], km[0:QK, hd, 0:TP], start=True, stop=True).then_inc(at_s.s, 1)

                pe.wait_ge(vm_copied.s, vm_copied.at(l, 1))
                pe.wait_ge(hn_done.s, hn_done.at(l, 2 * HM))
                att_scores(0)
                att_scores(1)
                pe.wait_ge(own_copied.s, own_copied.at(l, 1))
                pe.wait_ge(qt_low.s, qt_low.at(l, 1))
                for hd in range(HM):
                    pe.wait_ge(at_n.s, at_n.at(l, hd + 1))
                    if hd:
                        pe.wait_ge(at_tc.s, at_tc.at(l, hd))
                    for c in range(3):
                        ins = pe.transpose(bank[6][:, c * P:c * P + P], ap_s[hd % 2][:, c * P:c * P + P], ident)
                    ins.then_inc(at_t.s, 1)
                    if hd + 2 < HM:
                        att_scores(hd + 2)
                    pe.wait_ge(at_tc.s, at_tc.at(l, hd + 1))
                    if hd:
                        pe.wait_ge(at_oc.s, at_oc.at(l, hd))
                    r = slice(hd % 2 * VD, hd % 2 * VD + VD)
                    mm(bank[7][r, 0:TP], vm[:, 0, hd * VD:hd * VD + VD], ap_t[hd % 2][:, 0:TP], start=True, stop=False)
                    mm(bank[7][r, P:TP], vm[:, 1, hd * VD:hd * VD + VD], ap_t[hd % 2][:, TP:TP + P], start=False, stop=True)\
                        .then_inc(at_o.s, 1)



                def front(b, i, tail, turn):
                    ck = ck_loaded[i]
                    pe.wait_ge(ck.s, ck.at(l, (turn + 1) * (DMA * NT)))
                    pe.wait_ge(c_kst.s, c_kst.at(l, b + 1))
                    if tail is not None:
                        pe.wait_ge(c_lo.s, c_lo.at(l, b * 8))
                    for g in range(4):
                        ins = pe.transpose(bank[5][:, g * P:g * P + P], kpe_n[:, 4 * g:4 * g + 4, :].rearrange("p t r -> p (t r)"), ident)
                    ins.then_inc(c_kt.s, 1)

                    def turn_pair(tp):
                        if tp == 1:
                            pe.wait_ge(c_ktc.s, c_ktc.at(l, b + 1))
                        elif tp >= 2:
                            pe.wait_ge(c_lo.s, c_lo.at(l, b * 8 + (tp - 1)))
                        for u in range(2):
                            for c in range(2):
                                q = 2 * u + c
                                ins = pe.transpose(bank[4 + tp % 2][:, q * P:q * P + P], cache[i][:, 2 * tp + u, c * P:c * P + P], ident)
                        ins.then_inc(c_tr.s, 1)

                    turn_pair(0)
                    turn_pair(1)
                    for g in range(4):
                        ins = mm(bank[6][:, i * P + g * 32:i * P + g * 32 + 32], kpeT[:, g, :], q_pe[i][:, :, :].rearrange("p r h -> p (r h)"),
                                 start=True, stop=True)
                    ins.then_inc(c_pe.s, 1)
                    pe.wait_ge(c_q.s, c_q.at(l, b + 1))
                    for tp in range(NT // 2):
                        if 0 < tp < NT // 2 - 1:
                            turn_pair(tp + 1)
                        pe.wait_ge(c_lo.s, c_lo.at(l, b * 8 + (tp + 1)))
                        for u in range(2):
                            t = 2 * tp + u
                            if tail is not None or t >= 2:
                                pe.wait_ge(c_sq.s, c_sq.at(l, b * NT + (t - 1)))
                                pe.wait_ge(c_sr.s, c_sr.at(l, b * NT + (t - 1)))
                            for half, cols in enumerate((UKA, UKB)):
                                for c in range(2):
                                    q = 2 * u + c
                                    _, ins = three(bank[2 * u + half][:, 0:cols.stop - cols.start], (ct_hi[tp % 2][:, q, :], ct_lo[tp % 2][:, q, :]),
                                                   (uk_hi[:, c, cols], uk_lo[:, c, cols]), c == 0, c == 1)
                            ins.then_inc(c_kn.s, 1)
                        if tail is not None and tp in (2, 4, 6, 7):
                            tail_step(tail, (2, 4, 6, 7).index(tp))

                def tail_step(tail, step):
                    b, i = tail[0], tail[1]
                    if step == 0:
                        pe.wait_ge(t_mx.s, t_mx.at(l, b + 1))
                        pe.transpose(bank[7][0:HM, KVL:KVL + P], small[:, 0:8], ident).then_inc(t_mt.s, 1)
                    elif step == 1:
                        pe.wait_ge(t_dg.s, t_dg.at(l, b + 1))
                        mm(bank[7][:, 392:392 + HM], ones[0:HM, :], small[0:HM, 16:24], start=True, stop=True).then_inc(t_bc.s, 1)
                    elif step == 2:
                        pe.wait_ge(t_p.s, t_p.at(l, b + 1))
                        for t in range(NT):
                            mm(bank[7][0:HM, 0:KVL], pr[:, t, :], cache[i][:, t, 0:KVL], start=t == 0, stop=t == NT - 1)
                        pe.wait_ge(t_l.s, t_l.at(l, b + 1))
                        mm(bank[7][:, 400:400 + HM], ones, small[:, 48:56], start=True, stop=True).then_inc(t_lat.s, 1)
                    else:
                        pe.wait_ge(t_cp.s, t_cp.at(l, b + 1))
                        for c in range(2):
                            ins = mm(bank[7][:, 408 + c * HM:416 + c * HM], latn[0:HM, c * P:c * P + P], ident[0:HM, 0:HM], start=True, stop=True)
                        ins.then_inc(t_tr.s, 1)

                pe.wait_ge(chunk_free.s, chunk_free.at(l, C0["gate_c"]))
                pe.wait_ge(at_tc.s, at_tc.at(l, HM))
                pe.wait_ge(at_oc.s, at_oc.at(l, HM))
                pe.wait_ge(uk_low.s, uk_low.at(l, 1))
                front(0, 0, None, 0)
                with pe.Fori(0, 2) as j:
                    for u in range(3):
                        front(j * 3 + (u + 1), (u + 1) % 3, (j * 3 + u, u), j + (u + 1) // 3)
                front(NB - 1, 1, (NB - 2, 0), 2)
                for step in range(4):
                    tail_step((NB - 1, 1), step)

                pe.wait_ge(t_fin.s, t_fin.at(l, NB))
                for hd in range(HM):
                    r = slice(hd % 2 * VD, hd % 2 * VD + VD)
                    o = hd // 2 * NB
                    for c in range(2):
                        ins = mm(bank[4][r, o:o + NB], uv[:, c, hd * VD:hd * VD + VD], lat[:, c, hd, :], start=c == 0, stop=c == 1)
                ins.then_inc(uvs_ready.s, 1)

                with pe.Fori(0, 2) as i:
                    group("gate_c", i, h)
                pe.wait_ge(mla_split.s, mla_split.at(l, 1))
                for m in range(KT):
                    stream_chunk("mla_out", m, 4, (s_hi[:, 4:8, :], s_lo[:, 4:8, :]))
                with pe.Fori(0, 2) as i:
                    group("w_out", i, s_, lambda k: pe.wait_ge(mix_low.s, mix_low.at(l, k + 1)))

                token_sums(1)
                with pe.Fori(0, 2 * FT // 4) as i:
                    group("ffn_in", i, h, h_there(1))
                for m in range(KT):
                    stream_chunk("ffn_out", m, FT, (a_hi, a_lo), (lambda k: pe.wait_ge(ffn_low.s, ffn_low.at(l, k + 1))) if m == 0 else None)

                token_sums(2)
                with pe.Fori(0, 2) as i:
                    group("ple_gate", i, h, h_there(2))
                pe.wait_ge(p_low.s, p_low.at(l, 1))
                for m in range(KT):
                    stream_chunk("ple_proj", m, 2, (p_hi, p_lo))

        @block.scalar
        def _(act):
            A = act.activation

            def copy(out, in_, **kw):
                return A(out, in_, ACT.Copy, **kw)

            asteps = Steps()

            def asteps_restart():
                if asteps.n:
                    act.wait_ge(act_step.s, asteps.n)
                    act.sem_clear(act_step.s)
                    asteps.n = 0

            def sigmoid(out, tmp, z):
                A(tmp, z, ACT.Exp, scale=-1.0).then_inc(act_step.s, asteps.one())
                act.wait_ge(act_step.s, asteps.n)
                A(tmp, tmp, ACT.Ln, bias=1.0).then_inc(act_step.s, asteps.one())
                act.wait_ge(act_step.s, asteps.n)
                return A(out, tmp, ACT.Exp, scale=-1.0)

            def rsqrt_mean(out, total, width):
                A(out, total, ACT.Ln, scale=1.0 / width, bias=EPS).then_inc(act_step.s, asteps.one())
                act.wait_ge(act_step.s, asteps.n)
                return A(out, out, ACT.Exp, scale=-0.5)

            act.preload_act_table_set("natural_log_exp_and_others")
            act.sem_inc(v_copied.s, 1)
            act.wait_ge(tables_loaded.s, 4 * DMA)
            act.wait_ge(q_pe_zeroed.s, 1)
            with act.Fori(0, DEPTH) as l:
                def cut(j, n_static):
                    r = n_static % RING
                    if n_static >= RING:
                        act.wait_ge(w_begun.s, w_begun.at(l, j * RING + (n_static - RING + 2)))
                    ld = w_loaded[r]
                    act.wait_ge(ld.s, ld.at(l, j * DMA + (n_static // RING + 1) * DMA))
                    copy(w_hi[r][:, :], w_raw[r][:, :]).then_inc(w_high.s, 1)

                def split_x(w, gain, there):
                    for k in range(KT):
                        there(k)
                        copy(h_hi[:, k, :], xT[:, k, :], scale=col(gain, k)).then_inc(h_high.s, 1)
                        A((et if k < 4 else zt)[:, k % 4, :], xT[:, k, :], ACT.Square).then_inc(x_sq.s, 1)
                    act.wait_ge(x_sum.s, x_sum.at(l, (w + 1) * KT))
                    rsqrt_mean(rstd[:, :], bank[4][:, 0:T], D).then_inc(x_root.s, 1)

                def exps(stage, i, slots):
                    for r in slots:
                        cut(i, B0[stage] + r + 3)
                        act.wait_ge(chunk_free.s, chunk_free.at(l, i * 4 + (C0[stage] + r + 1)))
                        out = gate[:, ds(i * 4 + r, 1), :].rearrange("p o t -> p (o t)") if stage in GATES else et[:, r, :]
                        sigmoid(out, et[:, r, :], zt[:, r, :]).then_inc(exp_ready.s, 1)

                act.wait_ge(vec_ready.s, vec_ready.at(l, 1))
                act.wait_ge(chunk_free.s, chunk_free.at(l, 0))
                split_x(0, "g_mix", lambda k: cut(0, k) if k < 3 else None)
                act.wait_ge(conv_state_loaded.s, conv_state_loaded.at(l, DMA))
                copy(u_smp[:, :, :, 0:30], conv_stage[:, :, :, :]).then_inc(conv_state_placed.s, 1)
                for c in range(CT):
                    ins = A(yconv[:, c, :], tb("rope_c", T), ACT.Identity, scale=0.0, bias=col("b_dw", c))
                ins.then_inc(conv_biased.s, 1)
                asteps_restart()
                with act.Fori(0, 2) as i:
                    for r in (1, 3):
                        cut(i, B0["glu"] + r + 2)
                        exps("glu", i, (r,))
                    asteps_restart()
                act.wait_ge(u_ready.s, u_ready.at(l, 1))
                copy(conv_new[:, :, :, :], u_smp[:, :, :, 1:31]).then_inc(conv_new_ready.s, 1)
                act.wait_ge(conv_new_ready.s, conv_new_ready.at(l, 1))
                act.dma_start(conv_sample_out[ds(l, 1)].rearrange("o p c b w -> (o p) c b w"), conv_new[:, :, :, :]).then_inc(conv_stored.s, DMA)
                act.dma_start(conv_prompt_out[ds(l, 1)].rearrange("o p c w -> (o p) c w"), u_ext[:, :, TP:TP + 30]).then_inc(conv_stored.s, DMA)

                with act.Fori(0, 2) as i:
                    for r in range(4):
                        cut(i, B0["qk"] + r + 3)

                act.wait_ge(k_turned.s, k_turned.at(l, 1))
                for hd in range(HR):
                    for c in range(2):
                        copy(k_nat[:, c, hd * P:hd * P + P], bank[4 + c][:, hd * P:hd * P + P], scale=tb("kdec", 1, c * HR + hd))
                copy(k_smp[0:NB, :], bank[6][0:NB, :]).then_inc(k_copied.s, 1)
                with act.Fori(0, 2) as i:
                    for r in range(4):
                        cut(i, B0["v"] + r + 3)
                    act.wait_ge(v_turned.s, v_turned.at(l, i + 1))
                    for c in range(2):
                        copy(v_nat[:, c, ds(i * 512, 512)], bank[4 + c][:, :])
                    copy(v_smp[0:NB, ds(i * 512, 512)], bank[6][0:NB, :]).then_inc(v_copied.s, 1)
                asteps_restart()
                with act.Fori(0, 2) as i:
                    exps("rg", i, range(4))
                    asteps_restart()

                asteps_restart()
                with act.Fori(0, 2) as i:
                    exps("gate_a", i, range(4))
                    asteps_restart()


                act.wait_ge(exp_ready.s, exp_ready.at(l, E0["gate_a"] + KT))
                act.wait_ge(cln_centred.s, cln_centred.at(l, 1))
                A(et[:, :, :], yconv[:, :, :], ACT.Square).then_inc(cln_sq.s, 1)
                act.wait_ge(cln_sum.s, cln_sum.at(l, 2))
                rsqrt_mean(rsb[:, 0, :], bank[5][:, 0:T], CONV).then_inc(cln_root.s, 1)
                act.wait_ge(cln_y.s, cln_y.at(l, 1))
                sigmoid(et[:, :, :], et[:, :, :], yconv[:, :, :]).then_inc(cln_exp.s, 1)
                act.wait_ge(conv_act.s, conv_act.at(l, 1))
                copy(cv_hi[:, 0:CT, :], yconv[:, :, :]).then_inc(conv_high.s, 1)

                act.wait_ge(conv_stored.s, conv_stored.at(l, 32))
                for hd in range(HR):
                    act.wait_ge(ret_o.s, ret_o.at(l, hd + 1))
                    copy(oT[:, 2 * hd:2 * hd + 2, 0:TP], bank[6][:, :].rearrange("p (e t) -> p e t", e=2)).then_inc(ret_oc.s, 1)
                    act.wait_ge(ret_st.s, ret_st.at(l, hd + 1))
                    copy(ret_stage[:, hd, :], bank[7][:, 0:DV]).then_inc(ret_stc.s, 1)
                act.wait_ge(ret_stc.s, ret_stc.at(l, HR))
                act.dma_start(ret_prompt_out[ds(l, 1)].rearrange("o h d e -> d (o h) e"), ret_stage[:, :, :]).then_inc(ret_stored.s, DMA)

                for n in range(B0["conv_out"], B0["gate_b"]):
                    cut(0, n + 3)

                def gn_square(hd):
                    act.wait_ge(gn_c.s, gn_c.at(l, hd + 1))
                    if hd >= 2:
                        act.wait_ge(gn_var.s, gn_var.at(l, hd - 1))
                    e = 2 * (hd % 2)
                    A(et[:, e:e + 2, :], oT[:, 2 * hd:2 * hd + 2, :], ACT.Square).then_inc(gn_sq.s, 1)

                def gn_rt(hd):
                    act.wait_ge(gn_var.s, gn_var.at(l, hd + 1))
                    if hd >= 2:
                        act.wait_ge(gn_y.s, gn_y.at(l, hd - 1))
                    rsqrt_mean(rsb[:, hd % 2, :], bank[4 + hd][:, 0:T], DV).then_inc(gn_root.s, 1)

                def gn_hi(hd):
                    act.wait_ge(gn_y.s, gn_y.at(l, hd + 1))
                    copy(s_hi[:, 2 * hd:2 * hd + 2, :], oT[:, 2 * hd:2 * hd + 2, :]).then_inc(gn_high.s, 1)

                gn_square(0)
                gn_square(1)
                gn_rt(0)
                gn_square(2)
                gn_rt(1)
                gn_hi(0)
                gn_square(3)
                gn_rt(2)
                gn_hi(1)
                gn_rt(3)
                gn_hi(2)
                gn_hi(3)
                asteps_restart()
                with act.Fori(0, 2) as i:
                    exps("gate_b", i, range(4))
                    asteps_restart()


                with act.Fori(0, 2) as i:
                    for r in range(4):
                        cut(i, B0["ret_out"] + r + 3)

                for m in range(5):
                    cut(0, B0["kvq"] + m + 3)
                    act.wait_ge(chunk_free.s, chunk_free.at(l, C0["kvq"] + m + 1))
                    z = zt[:, (0, 1, 2, 3, 0)[m], :]
                    ins = A(sqg[:, m, :], z, ACT.Square)
                    if m < 3:
                        ins = copy(qa_hi[:, m, :], z, scale=col("g_qa", m))
                    ins.then_inc(kvq_act.s, 1)
                cut(0, B0["kvq"] + 5 + 3)
                for n, width in enumerate((QL, KVL)):
                    act.wait_ge(kvq_sum.s, kvq_sum.at(l, n + 1))
                    rsqrt_mean(rsb[:, n, :], bank[4 + n][:, 0:T], width).then_inc(kvq_root.s, 1)

                def head_square(k, buf):
                    if k >= 4:
                        act.wait_ge(hn_done.s, hn_done.at(l, k - 3))
                    A(et[0:QK, k % 4, :], buf, ACT.Square).then_inc(hn_sq.s, 1)

                def head_root(k):
                    act.wait_ge(hn_sum.s, hn_sum.at(l, k + 1))
                    rsqrt_mean(et[0:QK, k % 4, :], bank[6 + k % 2][0:QK, 0:T], QK).then_inc(hn_root.s, 1)

                for step in range(HM + 2):
                    if step in (0, 3, 6):
                        cut(0, B0["uq"] + step // 3 + 3)
                    if step < HM:
                        act.wait_ge(q_roped.s, q_roped.at(l, step + 1))
                        head_square(step, qm[0:QK, step, :])
                    if step >= 2:
                        head_root(step - 2)
                act.wait_ge(ckv_ready.s, ckv_ready.at(l, 1))
                act.dma_start(ckv_out[ds(l, 1)].rearrange("o p c t -> (o p) c t"), ckvT[:, :, :]).then_inc(own_stored.s, DMA)
                act.dma_start(kpe_out[ds(l, 1)].rearrange("o p t -> (o p) t"), kpe_own[NOPE:QK, :]).then_inc(own_stored.s, DMA)
                for step in range(HM + 2):
                    if step < HM:
                        copy(km[NOPE:QK, step, :], kpe_own[NOPE:QK, :])
                        act.wait_ge(kn_ready.s, kn_ready.at(l, step + 1))
                        copy(km[0:NOPE, step, :], bank[4 + step % 2][0:NOPE, 0:T]).then_inc(kn_copied.s, 1)
                        act.wait_ge(kn_copied.s, kn_copied.at(l, step + 1))
                        head_square(HM + step, km[0:QK, step, :])
                    if step >= 2:
                        head_root(HM + step - 2)
                act.wait_ge(vm_ready.s, vm_ready.at(l, 1))
                for c in range(2):
                    ins = copy(vm[:, c, :], bank[4 + c][:, :])
                ins.then_inc(vm_copied.s, 1)
                act.wait_ge(own_sum.s, own_sum.at(l, 1))
                copy(own[:, :, :].rearrange("p b h -> p (b h)"), bank[6][:, 0:HM * NB]).then_inc(own_copied.s, 1)
                act.wait_ge(qt_ready.s, qt_ready.at(l, 1))
                for c in range(2):
                    ins = copy(qt_hi[:, :, c, :], bank[7][:, c * 64:c * 64 + 64].rearrange("p (h b) -> p b h", h=HM))
                ins.then_inc(qt_high.s, 1)

                def att_exp(hd):
                    i = hd % 2
                    act.wait_ge(at_m.s, at_m.at(l, hd + 1))
                    A(ap_s[i][:, 0:P], ap_s[i][:, 0:P], ACT.Exp, scale=ATT_SCALE, bias=small[:, 4 + 2 * i:5 + 2 * i],
                      accum_out=small[:, 8 + 2 * i:9 + 2 * i])
                    A(ap_s[i][:, P:3 * P], ap_s[i][:, P:3 * P], ACT.Exp, scale=ATT_SCALE, bias=small[:, 5 + 2 * i:6 + 2 * i],
                      accum_out=small[:, 9 + 2 * i:10 + 2 * i]).then_inc(at_p.s, 1)

                att_exp(0)
                for hd in range(HM):
                    if hd + 1 < HM:
                        att_exp(hd + 1)
                    act.wait_ge(at_t.s, at_t.at(l, hd + 1))
                    copy(ap_t[hd % 2][:, :], bank[6][:, 0:3 * P]).then_inc(at_tc.s, 1)
                    act.wait_ge(at_o.s, at_o.at(l, hd + 1))
                    r = slice(hd % 2 * VD, hd % 2 * VD + VD)
                    copy(oM[r, hd // 2, 0:TP], bank[7][r, 0:TP]).then_inc(at_oc.s, 1)
                act.wait_ge(own_stored.s, own_stored.at(l, 32))
                copy(uk_hi[:, :, 0:256], uk[:, :, 0:256])
                copy(uk_hi[:, :, UKB], uk[:, :, 256:512]).then_inc(uk_high.s, 1)

                def gather_rope(b, i, turn):
                    ck = ck_loaded[i]
                    act.wait_ge(ck.s, ck.at(l, (turn + 1) * (DMA * NT)))
                    if not isinstance(b, int) or b:
                        act.wait_ge(c_ksq.s, c_ksq.at(l, b))
                    for r in range(4):
                        rows = slice(r * ROPE, r * ROPE + ROPE)
                        copy(q_pe[i][rows, r, :], qpe4[rows, ds(b, 1), :].rearrange("p o h -> p (o h)"))
                    copy(kpe_n[:, :, :], cache[i][:, :, KVL:KV]).then_inc(c_kst.s, 1)

                def next_q(b):
                    copy(uk_hi[:, :, 256:256 + HM], qt_hi[:, ds(b, 1)].rearrange("p o c h -> p (o c) h").bitcast(F32))
                    copy(uk_lo[:, :, 256:256 + HM], qt_lo[:, ds(b, 1)].rearrange("p o c h -> p (o c) h").bitcast(F32)).then_inc(c_q.s, 1)

                def front(b, i, tail, follows):
                    if tail is not None:
                        act.wait_ge(c_ss.s, c_ss.at(l, b * NT - 1))
                    act.wait_ge(c_kst.s, c_kst.at(l, b + 1))
                    A(sq[0][:, :, :].rearrange("p h n -> p (h n)"), kpe_n[:, :, :].rearrange("p t r -> p (t r)"), ACT.Square).then_inc(c_ksq.s, 1)
                    act.wait_ge(c_kt.s, c_kt.at(l, b + 1))
                    copy(kpeT[:, :, :], bank[5][:, :].rearrange("p (g k) -> p g k", g=4)).then_inc(c_ktc.s, 1)

                    def high(tp):
                        act.wait_ge(c_tr.s, c_tr.at(l, b * 8 + (tp + 1)))
                        copy(ct_hi[tp % 2][:, :, :], bank[4 + tp % 2][:, :].rearrange("p (q k) -> p q k", q=4)).then_inc(c_hi.s, 1)

                    high(0)
                    for tp in range(NT // 2):
                        if tp + 1 < NT // 2:
                            high(tp + 1)
                        for u in range(2):
                            t = 2 * tp + u
                            act.wait_ge(c_kn.s, c_kn.at(l, b * NT + (t + 1)))
                            if t == 0:
                                act.wait_ge(c_kss.s, c_kss.at(l, b + 1))
                            elif t >= 2 or tail is not None:
                                act.wait_ge(c_ss.s, c_ss.at(l, b * NT + (t - 1)))
                            if t == NT - 1 and follows is not None:
                                next_q(b + 1)
                            for half in range(2):
                                ins = A(sq[u][:, 4 * half:4 * half + 4, :], bank[2 * u + half][:, 0:256].rearrange("p (h n) -> p h n", h=4), ACT.Square)
                            ins.then_inc(c_sq.s, 1)
                            copy(scores[i][:, t, :], bank[2 * u][:, 256:256 + HM]).then_inc(c_sr.s, 1)
                        if tp == 4 and follows is not None:
                            gather_rope(b + 1, (i + 1) % 3, follows)
                        if tail is not None and tp == 0:
                            tail_root(tail)
                        if tail is not None and tp == 5:
                            tail_exp(tail)
                        if tail is not None and tp == 6:
                            tail_copy(tail)

                def tail_root(b):
                    act.wait_ge(t_tot.s, t_tot.at(l, b + 1))
                    rsqrt_mean(kn_r[:, :, :], kn_r[:, :, :], QK).then_inc(t_root.s, 1)

                def tail_copy(b):
                    act.wait_ge(t_lat.s, t_lat.at(l, b + 1))
                    copy(latn[0:HM, :], bank[7][0:HM, 0:KVL]).then_inc(t_cp.s, 1)

                def tail_exp(b):
                    act.wait_ge(t_shift.s, t_shift.at(l, b + 1))
                    A(pr[:, :, :], sc[:, :, :], ACT.Exp, scale=ATT_SCALE)
                    A(small[:, 40:48], small[:, 32:40], ACT.Exp, scale=ATT_SCALE).then_inc(t_p.s, 1)

                act.wait_ge(qt_low.s, qt_low.at(l, 1))
                gather_rope(0, 0, 0)
                next_q(0)
                front(0, 0, None, 0)
                asteps_restart()
                with act.Fori(0, 2) as j:
                    for u in range(3):
                        front(j * 3 + (u + 1), (u + 1) % 3, j * 3 + u, j + (u + 2) // 3)
                    asteps_restart()
                front(NB - 1, 1, NB - 2, None)
                tail_root(NB - 1)
                tail_exp(NB - 1)
                tail_copy(NB - 1)

                act.wait_ge(uvs_ready.s, uvs_ready.at(l, 1))
                copy(oM[:, :, TP:T], bank[4][:, 0:4 * NB].rearrange("p (q b) -> p q b", q=4)).then_inc(uvs_copied.s, 1)
                act.wait_ge(uvs_copied.s, uvs_copied.at(l, 1))
                copy(s_hi[:, 4:8, :], oM[:, :, :]).then_inc(mla_high.s, 1)
                asteps_restart()
                with act.Fori(0, 2) as i:
                    exps("gate_c", i, range(4))
                    asteps_restart()

                for k in range(KT):
                    if k % 2 == 0:
                        cut(0, B0["mla_out"] + k // 2 + 3)
                    act.wait_ge(mix_done.s, mix_done.at(l, k + 1 if k < 4 else KT))
                    copy(s_hi[:, k, :], mix[:, k, :]).then_inc(mix_high.s, 1)

                def out_there(k):
                    cut(0, B0["w_out"] + k + 3)
                    act.wait_ge(chunk_free.s, chunk_free.at(l, C0["w_out"] + k + 1))

                split_x(1, "g_ffn", out_there)
                asteps_restart()
                with act.Fori(0, 2 * FT // 4) as i:
                    exps("ffn_in", i, (0,))
                    for u in range(2):
                        cut(i, B0["ffn_in"] + 2 * u + 1 + 3)
                        act.wait_ge(ffn_a.s, ffn_a.at(l, i * 2 + (u + 1)))
                        copy(a_hi[:, ds(i * 2 + u, 1), :].rearrange("p o t -> p (o t)"), zt[:, 2 * u, :]).then_inc(ffn_high.s, 1)
                        if u == 0:
                            exps("ffn_in", i, (2,))
                    asteps_restart()
                def down_there(m):
                    for n in range(-(-m * FT // 8), -(-(m + 1) * FT // 8)):
                        cut(0, B0["ffn_out"] + n + 3)
                    act.wait_ge(chunk_free.s, chunk_free.at(l, C0["ffn_out"] + m + 1))

                split_x(2, "g_ple", down_there)
                act.wait_ge(p_loaded.s, p_loaded.at(l, DMA))
                copy(p_hi[:, :, :], p_raw[:, :, :]).then_inc(p_high.s, 1)
                for r in range(KT):
                    n = B0["ple_gate"] + r + 3
                    if n < NBLK:
                        cut(0, n)
                    act.wait_ge(chunk_free.s, chunk_free.at(l, C0["ple_gate"] + r + 1))
                    sigmoid(gate[:, r, :], et[:, r % 4, :], zt[:, r % 4, :]).then_inc(exp_ready.s, 1)
                asteps_restart()

        @block.vector
        def _(v):
            steps = Steps()

            def steps_restart():
                if steps.n:
                    v.wait_ge(dve_step.s, steps.n)
                    v.sem_clear(dve_step.s)
                    steps.n = 0

            tt, stt = v.tensor_tensor, v.scalar_tensor_tensor

            def flat(ap):
                return ap.rearrange("p o t -> p (o t)")

            v.wait_ge(tables_loaded.s, 4 * DMA)
            v.sem_inc(chunk_free.s, 4)
            for i in range(3):
                ins = v.memset(q_pe[i][:, :, :], 0.0)
            ins.then_inc(q_pe_zeroed.s, 1)
            with v.Fori(0, DEPTH) as l:
                def split_x(w, gain):
                    for k in range(KT):
                        v.wait_ge(h_high.s, h_high.at(l, w * KT + k + 1))
                        stt(h_lo[:, k, :], xT[:, k, :], col(gain, k), h_hi[:, k, :].bitcast(F32), ALU.mult, ALU.subtract)\
                            .then_inc(h_low.s, 1)
                    v.wait_ge(x_root.s, x_root.at(l, w + 1))


                def take(stage, i, r, out=None, rows=P, rs=rstd[:, :], s=None):
                    c = C0[stage] + r
                    v.wait_ge(chunk_ready.s, chunk_ready.at(l, i * 4 + (c + 1)))
                    out = zt[:, r % 4, :] if out is None else out
                    tt(out, bank[c % 4][0:rows, 0:T], rs[0:rows, :], ALU.mult).then_inc(chunk_free.s, 1)

                def taken(stage, i, r):
                    v.wait_ge(chunk_free.s, chunk_free.at(l, i * 4 + (C0[stage] + r + 1)))

                def sigmoid_there(n):
                    v.wait_ge(exp_ready.s, exp_ready.at(l, n + 1))

                def taps(ct, i, r):
                    for j in range(4):
                        w = 4 * r + j
                        stt(yconv[:, ct, 0:TP], u_ext[:, ct, ds(i * 16 + w, TP)],
                               vec[:, ds(i * 16 + (VEC["w_dw"] + ct * 32 + w), 1)], yconv[:, ct, 0:TP], ALU.mult, ALU.add).then_inc(dve_step.s, steps.one())
                        v.wait_ge(dve_step.s, steps.n)

                def gates(stage, ct=None):
                    with v.Fori(0, 2) as i:
                        for r in range(4):
                            sigmoid_there(i * 4 + (E0[stage] + r - 4))
                            take(stage, i, r)
                            if ct is not None:
                                taps(ct, i, r)
                        steps_restart()

                def gated_sum(stage, done=None, first=False):
                    with v.Fori(0, 2) as i:
                        for r in range(4):
                            c = C0[stage] + r
                            m = i * 4 + r
                            v.wait_ge(chunk_ready.s, chunk_ready.at(l, i * 4 + (c + 1)))
                            g, x = flat(gate[:, ds(m, 1), :]), flat(mix[:, ds(m, 1), :])
                            sigmoid_there(E0[GATE_OF[stage]] + KT - 1)
                            if first:
                                tt(x, bank[c % 4][:, 0:T], g, ALU.mult).then_inc(chunk_free.s, 1)
                                continue
                            tt(zt[:, r, :], bank[c % 4][:, 0:T], g, ALU.mult).then_inc(chunk_free.s, 1)
                            taken(stage, i, r)
                            ins = tt(x, x, zt[:, r, :], ALU.add)
                            if done is not None:
                                ins.then_inc(done.s, 1)
                            else:
                                ins.then_inc(dve_step.s, steps.one())
                        steps_restart()

                def add_to_x(stage):
                    with v.Fori(0, 2) as i:
                        for r in range(4):
                            c = C0[stage] + r
                            x = flat(xT[:, ds(i * 4 + r, 1), :])
                            v.wait_ge(chunk_ready.s, chunk_ready.at(l, i * 4 + (c + 1)))
                            tt(x, bank[c % 4][:, 0:T], x, ALU.add).then_inc(chunk_free.s, 1)

                v.tensor_copy(vec[:, :], flat(vecs[:, ds(l, 1), :])).then_inc(vec_ready.s, 1)
                v.wait_ge(vec_ready.s, vec_ready.at(l, 1))
                split_x(0, "g_mix")
                v.memset(u_ext[:, :, 0:30], 0.0).then_inc(dve_step.s, steps.one())
                v.memset(u_ext[:, :, 30 + TP:288], 0.0).then_inc(dve_step.s, steps.one())
                steps_restart()
                with v.Fori(0, 2) as i:
                    for r in range(4):
                        take("glu", i, r)
                        if r % 2:
                            sigmoid_there(i * 2 + r // 2)
                            taken("glu", i, r - 1)
                            m = i * 2 + r // 2
                            tt(flat(u_ext[:, ds(m, 1), 30:30 + TP]), zt[:, r - 1, 0:TP], et[:, r, 0:TP], ALU.mult).then_inc(dve_step.s, steps.one())
                            tt(u_smp[:, ds(m, 1), :, 30:31].rearrange("p o b w -> p (o b w)"), zt[:, r - 1, TP:T], et[:, r, TP:T], ALU.mult).then_inc(dve_step.s, steps.one())
                    steps_restart()
                v.wait_ge(conv_state_placed.s, conv_state_placed.at(l, 1))
                v.wait_ge(conv_biased.s, conv_biased.at(l, 1))
                taps_w = vec[:, VEC["w_dw"]:VEC["w_dw"] + CT * 32].rearrange("p (c w) -> p c w", c=CT)[:, :, 0:31]
                tt(conv_prod[:, :, :, :], u_smp[:, :, :, :], taps_w.unsqueeze(2).broadcast_to([P, CT, NB, 31]), ALU.mult)\
                    .then_inc(u_ready.s, 1)
                v.wait_ge(u_ready.s, u_ready.at(l, 1))
                v.tensor_reduce(small[:, 0:CT * NB], conv_prod[:, :, :, :].rearrange("p c b w -> p (c b) w"), AX.X, ALU.add).then_inc(dve_step.s, steps.one())
                v.wait_ge(dve_step.s, steps.n)
                steps_restart()

                with v.Fori(0, 2) as i:
                    for r in range(4):
                        take("qk", i, r)
                        taken("qk", i, r)
                        cos = tab[:, ds(i * T + TAB["rope_c"], T)]
                        o = flat(qk[:, ds(i * 4 + r, 1), :])
                        lo, hi = (slice(0, 64), slice(64, P))
                        tt(et[:, r, :], zt[:, r, :], cos, ALU.mult).then_inc(dve_step.s, steps.one())
                        tt(qk[lo, ds(i * 4 + r, 1), :].rearrange("p o t -> p (o t)"), zt[hi, r, :], tab[hi, ds(i * T + TAB["rope_s"], T)], ALU.mult).then_inc(dve_step.s, steps.one())
                        tt(qk[hi, ds(i * 4 + r, 1), :].rearrange("p o t -> p (o t)"), zt[lo, r, :], tab[lo, ds(i * T + TAB["rope_s"], T)], ALU.mult).then_inc(dve_step.s, steps.one())
                        v.wait_ge(dve_step.s, steps.n)
                        ins = tt(o, o, et[:, r, :], ALU.add)
                        if r == 3:
                            ins.then_inc(rope_ready.s, 1)
                        else:
                            ins.then_inc(dve_step.s, steps.one())
                        taps(0, i, r)
                    steps_restart()
                with v.Fori(0, 2) as i:
                    v.wait_ge(v_copied.s, v_copied.at(l, i))
                    for r in range(4):
                        take("v", i, r)
                        taps(1, i, r)
                    steps_restart()
                v.wait_ge(conv_stored.s, conv_stored.at(l, 32))
                v.wait_ge(v_copied.s, v_copied.at(l, 2))
                settle(v)
                with v.Fori(0, 2) as i:
                    for r in range(5):
                        if r < 4:
                            take("rg", i, r)
                        if r:
                            q = r - 1
                            sigmoid_there(i * 4 + (E0["rg"] + q))
                            tt(flat(rgs[:, ds(i * 4 + q, 1), :]), zt[:, q, :], et[:, q, :], ALU.mult).then_inc(dve_step.s, steps.one())
                            taps(2, i, q)
                    steps_restart()
                gates("gate_a", 3)
                ys = yconv[:, :, TP:T]
                tt(ys, ys, small[:, 0:CT * NB].rearrange("p (c b) -> p c b", c=CT), ALU.add).then_inc(conv_done.s, 1)

                v.wait_ge(cln_sum.s, cln_sum.at(l, 1))
                for c in range(CT):
                    ins = stt(yconv[:, c, :], bank[4][:, 0:T], -1.0 / CONV, yconv[:, c, :], ALU.mult, ALU.add)
                ins.then_inc(cln_centred.s, 1)
                v.wait_ge(cln_root.s, cln_root.at(l, 1))

                for c in range(CT):
                    stt(yconv[:, c, :], yconv[:, c, :], col("g_cln", c), rsb[:, 0, :], ALU.mult, ALU.mult).then_inc(dve_step.s, steps.one())
                v.wait_ge(dve_step.s, steps.n)
                for c in range(CT):
                    ins = v.tensor_scalar(yconv[:, c, :], yconv[:, c, :], col("b_cln", c), None, ALU.add)
                ins.then_inc(cln_y.s, 1)
                v.wait_ge(cln_exp.s, cln_exp.at(l, 1))
                tt(yconv[:, :, :], yconv[:, :, :], et[:, :, :], ALU.mult).then_inc(conv_act.s, 1)
                v.wait_ge(conv_high.s, conv_high.at(l, 1))
                tt(cv_lo[:, 0:CT, :], yconv[:, :, :], cv_hi[:, 0:CT, :].bitcast(F32), ALU.subtract).then_inc(conv_split.s, 1)

                for hd in range(HR):
                    v.wait_ge(ret_s.s, ret_s.at(l, hd + 1))
                    tt(sT[hd % 2][:, :], bank[4 + hd % 2][:, 0:384], tb("decay", 384, 384 * hd), ALU.mult).then_inc(ret_sd.s, 1)
                steps_restart()
                with v.Fori(0, NB // 2) as j:
                    for i in range(2):
                        b = j * 2 + i
                        v.tensor_scalar(k_mask[i][0:NB, :], k_smp[0:NB, :], tab[0:NB, ds(b + TAB["ident"], 1)], None, ALU.mult)\
                            .then_inc(st_mask.s, 1)
                        v.wait_ge(st_outer.s, st_outer.at(l, b + 1))
                        sl = st_loaded[i]
                        v.wait_ge(sl.s, j * DMA + sl.at(l, DMA))
                        for hd in range(HR):
                            s = state[i][:, hd, :]
                            ins = stt(s, s, GAMMA[hd], bank[4 + hd // 2][:, hd % 2 * DV:hd % 2 * DV + DV], ALU.mult, ALU.add)
                        ins.then_inc(st_new.s, 1)
                        v.wait_ge(st_o.s, st_o.at(l, b + 1))
                        v.tensor_copy(oT[:, :, ds(b + TP, 1)].rearrange("p m o -> p (m o)"), bank[6][:, 0:KT]).then_inc(st_oc.s, 1)
                gated_sum("conv_out", first=True)

                for hd in range(HR):
                    v.wait_ge(gn_sum.s, gn_sum.at(l, hd + 1))
                    o = oT[:, 2 * hd:2 * hd + 2, :]
                    stt(o, bank[4 + hd][:, 0:T].unsqueeze(1).broadcast_to([P, 2, T]), -1.0 / DV, o, ALU.mult, ALU.add).then_inc(gn_c.s, 1)
                for hd in range(HR):
                    v.wait_ge(gn_root.s, gn_root.at(l, hd + 1))
                    r = rsb[:, hd % 2, :]
                    o = oT[:, 2 * hd:2 * hd + 2, :]

                    tt(o, o, r.unsqueeze(1).broadcast_to([P, 2, T]), ALU.mult).then_inc(dve_step.s, steps.one())
                    v.wait_ge(dve_step.s, steps.n)
                    for m in (2 * hd, 2 * hd + 1):
                        ins = stt(oT[:, m, :], oT[:, m, :], col("g_rgn", m), rgs[:, m, :], ALU.mult, ALU.mult)
                    ins.then_inc(gn_y.s, 1)
                    v.wait_ge(gn_high.s, gn_high.at(l, hd + 1))
                    tt(s_lo[:, 2 * hd:2 * hd + 2, :], o, s_hi[:, 2 * hd:2 * hd + 2, :].bitcast(F32), ALU.subtract).then_inc(gn_low.s, 1)
                steps_restart()
                v.wait_ge(ret_stored.s, ret_stored.at(l, DMA))
                settle(v)
                gates("gate_b")
                gated_sum("ret_out")

                def kvq(m):
                    v.wait_ge(chunk_ready.s, chunk_ready.at(l, C0["kvq"] + m + 1))
                    tt(zt[:, m % 4, :], bank[(C0["kvq"] + m) % 4][:, 0:T], rstd[:, :], ALU.mult).then_inc(chunk_free.s, 1)

                for m in range(4):
                    kvq(m)
                for m in range(3):
                    v.wait_ge(kvq_act.s, kvq_act.at(l, m + 1))
                    ins = stt(qa_lo[:, m, :], zt[:, m, :], col("g_qa", m), qa_hi[:, m, :].bitcast(F32), ALU.mult, ALU.subtract)
                ins.then_inc(qa_low.s, 1)
                v.wait_ge(qa_low.s, qa_low.at(l, 1))
                kvq(4)
                kvq(5)
                for n in range(2):
                    v.wait_ge(kvq_root.s, kvq_root.at(l, n + 1))

                v.wait_ge(dve_step.s, steps.n)
                for c in range(2):
                    ins = stt(ckvT[:, c, :], zt[:, 3 if c == 0 else 0, :], col("g_kva", c), rsb[:, 1, :], ALU.mult, ALU.mult)
                ins.then_inc(ckv_ready.s, 1)
                pe_rows = slice(NOPE, QK)
                m_cos, m_sin = tb("mla_c", T, 0, pe_rows), tb("mla_s", T, 0, pe_rows)
                v.wait_ge(kr_rot.s, kr_rot.at(l, 1))
                tt(kpe_own[pe_rows, :], bank[6][pe_rows, 0:T], m_sin, ALU.mult).then_inc(dve_step.s, steps.one())
                tt(zt[pe_rows, 1, :], zt[pe_rows, 1, :], m_cos, ALU.mult).then_inc(dve_step.s, steps.one())
                v.wait_ge(dve_step.s, steps.n)
                tt(kpe_own[pe_rows, :], kpe_own[pe_rows, :], zt[pe_rows, 1, :], ALU.add).then_inc(kpe_ready.s, 1)

                def head_norm(k, buf, gain):
                    v.wait_ge(hn_root.s, hn_root.at(l, k + 1))
                    r = et[0:QK, k % 4, :]

                    stt(buf, buf, col(gain)[0:QK, :], r, ALU.mult, ALU.mult).then_inc(hn_done.s, 1)

                for step in range(HM + 4):
                    if step < HM:
                        c = C0["uq"] + step
                        v.wait_ge(chunk_ready.s, chunk_ready.at(l, c + 1))
                        tt(qm[0:QK, step, :], bank[c % 4][0:QK, 0:T], rsb[0:QK, 0, :], ALU.mult).then_inc(chunk_free.s, 1)
                    hd = step - 1
                    if 0 <= hd < HM:
                        v.wait_ge(uq_rot.s, uq_rot.at(l, hd + 1))
                        q = qm[pe_rows, hd, :]
                        tt(zt[pe_rows, hd % 4, :], bank[4 + hd % 2][pe_rows, 0:T], m_sin, ALU.mult).then_inc(dve_step.s, steps.one())
                        tt(q, q, m_cos, ALU.mult).then_inc(dve_step.s, steps.one())
                        v.wait_ge(dve_step.s, steps.n)
                        tt(q, q, zt[pe_rows, hd % 4, :], ALU.add).then_inc(q_roped.s, 1)
                    if step >= 4:
                        head_norm(step - 4, qm[0:QK, step - 4, :], "g_qn")
                for hd in range(HM):
                    head_norm(HM + hd, km[0:QK, hd, :], "g_kn")
                v.wait_ge(hn_done.s, hn_done.at(l, 2 * HM))
                qs = qm[0:QK, :, TP:T]
                tt(et[0:QK, 0, 0:64].rearrange("p (b h) -> p b h", b=NB), qs.rearrange("p h b -> p b h"),
                   km[0:QK, :, TP:T].rearrange("p h b -> p b h"), ALU.mult).then_inc(own_prod.s, 1)
                v.tensor_scalar(et[0:QK, 1, 0:64].rearrange("p (h b) -> p h b", h=HM), qs, col("g_kn")[0:QK, :], None, ALU.mult)\
                    .then_inc(qg_ready.s, 1)
                v.wait_ge(qg_ready.s, qg_ready.at(l, 1))
                for q in range(4):
                    v.tensor_copy(qpe4[32 * q:32 * q + 32, :, :], et[pe_rows, 1, 0:64].rearrange("p (h b) -> p b h", h=HM)).then_inc(dve_step.s, steps.one())
                v.tensor_copy(ckv_own[:, :, :], ckvT[:, :, TP:T]).then_inc(dve_step.s, steps.one())
                v.wait_ge(dve_step.s, steps.n)
                v.wait_ge(qt_high.s, qt_high.at(l, 1))
                for c in range(2):
                    ins = tt(qt_lo[:, :, c, :], bank[7][:, c * 64:c * 64 + 64].rearrange("p (h b) -> p b h", h=HM),
                             qt_hi[:, :, c, :].bitcast(F32), ALU.subtract)
                ins.then_inc(qt_low.s, 1)

                def att_max(hd):
                    i = hd % 2
                    v.wait_ge(at_s.s, at_s.at(l, hd + 1))
                    tt(ap_s[i][:, :], bank[4 + i][:, 0:384], tb("mask", 384), ALU.add).then_inc(dve_step.s, steps.one())
                    v.wait_ge(dve_step.s, steps.n)
                    v.tensor_reduce(small[:, 0:1], ap_s[i][:, 0:P], AX.X, ALU.max).then_inc(dve_step.s, steps.one())
                    v.tensor_reduce(small[:, 1:2], ap_s[i][:, P:3 * P], AX.X, ALU.max).then_inc(dve_step.s, steps.one())
                    v.wait_ge(dve_step.s, steps.n)
                    v.tensor_scalar(small[:, 4 + 2 * i:6 + 2 * i], small[:, 0:2], -ATT_SCALE, None, ALU.mult).then_inc(at_m.s, 1)

                def att_div(hd):
                    i = hd % 2
                    v.wait_ge(at_p.s, at_p.at(l, hd + 1))
                    v.reciprocal(small[:, 8 + 2 * i:10 + 2 * i], small[:, 8 + 2 * i:10 + 2 * i]).then_inc(dve_step.s, steps.one())
                    v.wait_ge(dve_step.s, steps.n)
                    v.tensor_scalar(ap_s[i][:, 0:P], ap_s[i][:, 0:P], small[:, 8 + 2 * i:9 + 2 * i], None, ALU.mult)
                    v.tensor_scalar(ap_s[i][:, P:3 * P], ap_s[i][:, P:3 * P], small[:, 9 + 2 * i:10 + 2 * i], None, ALU.mult)\
                        .then_inc(at_n.s, 1)

                att_max(0)
                for hd in range(HM):
                    if hd + 1 < HM:
                        att_max(hd + 1)
                    att_div(hd)
                v.wait_ge(uk_high.s, uk_high.at(l, 1))
                tt(uk_lo[:, :, 0:256], uk[:, :, 0:256], uk_hi[:, :, 0:256].bitcast(F32), ALU.subtract)
                tt(uk_lo[:, :, UKB], uk[:, :, 256:512], uk_hi[:, :, UKB].bitcast(F32), ALU.subtract).then_inc(uk_low.s, 1)

                def front(b, i, tail):
                    v.wait_ge(c_ksq.s, c_ksq.at(l, b + 1))
                    v.tensor_reduce(sspe[i][:, :], sq[0][:, :, :].rearrange("p h (a r) -> p (h a) r", r=ROPE), AX.X, ALU.add).then_inc(c_kss.s, 1)

                    def low(tp):
                        v.wait_ge(c_hi.s, c_hi.at(l, b * 8 + (tp + 1)))
                        tt(ct_lo[tp % 2][:, :, :], bank[4 + tp % 2][:, :].rearrange("p (q k) -> p q k", q=4),
                           ct_hi[tp % 2][:, :, :].bitcast(F32), ALU.subtract).then_inc(c_lo.s, 1)

                    low(0)
                    for tp in range(NT // 2):
                        if tp + 1 < NT // 2:
                            low(tp + 1)
                        for u in range(2):
                            t = 2 * tp + u
                            if t == 0:
                                v.wait_ge(c_pe.s, c_pe.at(l, b + 1))
                                v.tensor_copy(scores_pe[i][:, :, :].rearrange("p t h -> p (t h)"), bank[6][:, i * P:i * P + P]).then_inc(c_pec.s, 1)
                            v.wait_ge(c_sq.s, c_sq.at(l, b * NT + (t + 1)))
                            v.tensor_reduce(ssq[i][:, t, :], sq[u][:, :, :], AX.X, ALU.add).then_inc(c_ss.s, 1)
                        if tail is not None and tp in (0, 1, 3, 5, 6, 7):
                            tail_step(tail, (0, 1, 3, 5, 6, 7).index(tp))

                def tail_step(tail, step):
                    b, i = tail
                    if step == 0:
                        v.wait_ge(c_ss.s, c_ss.at(l, b * NT + NT))
                        v.wait_ge(c_kss.s, c_kss.at(l, b + 1))
                        tt(kn_r[:, :, :], ssq[i][:, :, :], sspe[i][:, :].unsqueeze(2).broadcast_to([P, NT, HM]), ALU.add)\
                            .then_inc(t_tot.s, 1)
                    elif step == 1:
                        v.wait_ge(t_root.s, t_root.at(l, b + 1))

                        v.wait_ge(c_sr.s, c_sr.at(l, b * NT + NT))
                        v.wait_ge(c_pec.s, c_pec.at(l, b + 1))
                        tt(scores[i][:, :, :], scores[i][:, :, :], scores_pe[i][:, :, :], ALU.add).then_inc(dve_step.s, steps.one())
                        v.wait_ge(dve_step.s, steps.n)
                        tt(sc[:, :, :], scores[i][:, :, :], kn_r[:, :, :], ALU.mult).then_inc(dve_step.s, steps.one())
                        v.wait_ge(dve_step.s, steps.n)
                        v.tensor_reduce(small[:, 0:8], sc[:, :, :].rearrange("p t h -> p h t"), AX.X, ALU.max).then_inc(t_mx.s, 1)
                    elif step == 2:
                        v.wait_ge(t_mt.s, t_mt.at(l, b + 1))
                        v.tensor_reduce(small[0:HM, 8:9], bank[7][0:HM, KVL:KVL + P], AX.X, ALU.max).then_inc(dve_step.s, steps.one())
                        v.wait_ge(dve_step.s, steps.n)
                        v.tensor_scalar(small[0:HM, 16:24], ident[0:HM, 0:HM], small[0:HM, 8:9], None, ALU.mult).then_inc(t_dg.s, 1)
                    elif step == 3:
                        v.wait_ge(t_bc.s, t_bc.at(l, b + 1))
                        o = flat(own[:, ds(b, 1), :])
                        m = small[:, 24:32]
                        tt(m, bank[7][:, 392:392 + HM], o, ALU.max).then_inc(dve_step.s, steps.one())
                        v.wait_ge(dve_step.s, steps.n)
                        tt(sc[:, :, :], sc[:, :, :], m.unsqueeze(1).broadcast_to([P, NT, HM]), ALU.subtract).then_inc(dve_step.s, steps.one())
                        tt(small[:, 32:40], o, m, ALU.subtract).then_inc(t_shift.s, 1)
                    elif step == 4:
                        v.wait_ge(t_p.s, t_p.at(l, b + 1))
                        v.tensor_reduce(small[:, 48:56], pr[:, :, :].rearrange("p t h -> p h t"), AX.X, ALU.add).then_inc(t_l.s, 1)
                    else:
                        v.wait_ge(t_tr.s, t_tr.at(l, b + 1))
                        tt(small[:, 56:64], bank[7][:, 400:400 + HM], small[:, 40:48], ALU.add).then_inc(dve_step.s, steps.one())
                        v.wait_ge(dve_step.s, steps.n)
                        v.reciprocal(small[:, 56:64], small[:, 56:64]).then_inc(dve_step.s, steps.one())
                        v.wait_ge(dve_step.s, steps.n)
                        for c in range(2):
                            stt(small[:, 64 + 8 * c:72 + 8 * c], small[:, 40:48], ckv_own[:, c, ds(b, 1)], bank[7][:, 408 + c * HM:416 + c * HM],
                                      ALU.mult, ALU.add).then_inc(dve_step.s, steps.one())
                        v.wait_ge(dve_step.s, steps.n)
                        for c in range(2):
                            ins = tt(lat[:, c, :, ds(b, 1)].rearrange("p h o -> p (h o)"), small[:, 64 + 8 * c:72 + 8 * c], small[:, 56:64], ALU.mult)
                        ins.then_inc(t_fin.s, 1)

                steps_restart()
                front(0, 0, None)
                steps_restart()
                with v.Fori(0, 2) as j:
                    for u in range(3):
                        front(j * 3 + (u + 1), (u + 1) % 3, (j * 3 + u, u))
                    steps_restart()
                front(NB - 1, 1, (NB - 2, 0))
                for step in range(6):
                    tail_step((NB - 1, 1), step)
                v.wait_ge(mla_high.s, mla_high.at(l, 1))
                tt(s_lo[:, 4:8, :], oM[:, :, :], s_hi[:, 4:8, :].bitcast(F32), ALU.subtract).then_inc(mla_split.s, 1)
                steps_restart()
                v.wait_ge(mla_split.s, mla_split.at(l, 1))
                settle(v)
                gates("gate_c")
                gated_sum("mla_out", mix_done)
                for k in range(KT):
                    v.wait_ge(mix_high.s, mix_high.at(l, k + 1))
                    tt(s_lo[:, k, :], mix[:, k, :], s_hi[:, k, :].bitcast(F32), ALU.subtract).then_inc(mix_low.s, 1)
                add_to_x("w_out")

                split_x(1, "g_ffn")
                settle(v)
                steps_restart()
                with v.Fori(0, 2 * FT // 4) as i:
                    def low(u):
                        v.wait_ge(ffn_high.s, ffn_high.at(l, i * 2 + (u + 1)))
                        tt(flat(a_lo[:, ds(i * 2 + u, 1), :]), zt[:, 2 * u, :], flat(a_hi[:, ds(i * 2 + u, 1), :]).bitcast(F32), ALU.subtract)\
                            .then_inc(ffn_low.s, 1)

                    for u in range(2):
                        g, up = 2 * u, 2 * u + 1
                        take("ffn_in", i, g)
                        take("ffn_in", i, up)
                        if u:
                            low(0)
                        sigmoid_there(i * 2 + (E0["ffn_in"] + u))
                        tt(zt[:, g, :], zt[:, g, :], et[:, g, :], ALU.mult).then_inc(dve_step.s, steps.one())
                        v.wait_ge(dve_step.s, steps.n)
                        taken("ffn_in", i, up)
                        tt(zt[:, g, :], zt[:, g, :], zt[:, up, :], ALU.mult).then_inc(ffn_a.s, 1)
                    low(1)
                    steps_restart()
                add_to_x("ffn_out")

                split_x(2, "g_ple")
                v.wait_ge(p_high.s, p_high.at(l, 1))
                tt(p_lo[:, :, :], p_raw[:, :, :], p_hi[:, :, :].bitcast(F32), ALU.subtract).then_inc(p_low.s, 1)
                gates("ple_gate")
                with v.Fori(0, 2) as i:
                    for r in range(4):
                        sigmoid_there(E0["ple_gate"] + KT - 1)
                        c = C0["ple_proj"] + r
                        x = flat(xT[:, ds(i * 4 + r, 1), :])
                        v.wait_ge(chunk_ready.s, chunk_ready.at(l, i * 4 + (c + 1)))
                        tt(zt[:, r, :], bank[c % 4][:, 0:T], flat(gate[:, ds(i * 4 + r, 1), :]), ALU.mult).then_inc(chunk_free.s, 1)
                        taken("ple_proj", i, r)
                        tt(x, x, zt[:, r, :], ALU.add).then_inc(dve_step.s, steps.one())
                    steps_restart()
            v.sem_inc(x_final.s, 1)


def constants():
    f = np.float32
    tab = np.zeros((P, NTAB), f)
    pos = np.concatenate([np.arange(TP), np.full(NB, PAST)]).astype(f)

    def angles(half):
        inv = np.power(f(10000.0), -np.arange(half, dtype=f) / f(half)).astype(f)
        ang = (inv[:, None] * pos[None, :]).astype(f)
        return np.cos(ang.astype(np.float64)), np.sin(ang.astype(np.float64))

    def put(name, a, rows=slice(0, P), off=0):
        tab[rows, TAB[name] + off:TAB[name] + off + a.shape[1]] = a

    c, s = angles(DK // 2)
    for i, factor in enumerate((1.0, DK ** -0.5)):
        put("rope_c", np.concatenate([c, c]) * factor, off=i * T)
        put("rope_s", np.concatenate([s, -s]) * factor, off=i * T)
    lg = np.log(1.0 - 2.0 ** (-5.0 - np.arange(HR, dtype=np.float64)))
    j, i = np.arange(P)[:, None], np.arange(P)[None, :]
    for h in range(HR):
        diag = np.where(i >= j, np.exp((i - j) * lg[h]), 0.0)
        put("decay", np.concatenate([diag, np.exp((i + P - j) * lg[h]), diag], 1), off=384 * h)
        for ch in range(2):
            put("kdec", np.exp((TP - 1 - (ch * P + np.arange(P))) * lg[h])[:, None], off=ch * HR + h)
    q, k = np.arange(P)[:, None], np.arange(P)[None, :]
    causal = np.where(k <= q, 0.0, -1e30)
    put("mask", np.concatenate([causal, np.zeros((P, P)), causal], 1))
    c, s = angles(ROPE // 2)
    put("mla_c", np.concatenate([np.ones((NOPE, T)), c, c]), slice(0, QK))
    put("mla_s", np.concatenate([np.zeros((NOPE, T)), s, s]), slice(0, QK))
    put("ident", np.eye(P))
    put("ones", np.ones((P, P)))
    rot = np.zeros((QK, QK))
    half = ROPE // 2
    for a in range(half):
        rot[NOPE + half + a, NOPE + a] = -1.0
        rot[NOPE + a, NOPE + half + a] = 1.0
    put("rot", rot, slice(0, QK))
    return tab


def kernel(x_prompt, x_sample, p_prompt, p_sample, cache_ckv, cache_kpe, state_ret, state_conv, page_table,
           g_mix, w_in, w_dw, b_dw, g_cln, b_cln, w_conv_out, g_rgn, w_ret_out, g_qa, w_uq, g_qn, g_kva,
           w_uk, w_uv, g_kn, w_mla_out, w_out, g_ffn, w_gate, w_up, w_down, g_ple, w_ple_gate, w_ple_proj):
    import concourse.bacc as bacc
    from concourse.bass_utils import run_bass_kernel_spmd

    A = np.asarray

    def tiles(w):
        w = A(w)
        k, m = w.shape
        return w.reshape(k // P, P, m // P, P).transpose(2, 0, 1, 3)

    def blocks(t):
        t = t.reshape(-1, 8, P, P)
        return t.transpose(0, 2, 1, 3).reshape(-1, P, 8 * P)

    def paired(a, b):
        return np.stack([tiles(a), tiles(b)], 1).reshape(-1, KT, P, P)

    def layer_stream(l):
        w = A(w_in[l])
        c = np.cumsum([0, CONV, CONV, HR * DK, HR * DK, HR * DV, HR * DV, QL, KVL, ROPE, D, D, D])
        part = [w[:, c[i]:c[i + 1]] for i in range(len(c) - 1)]
        glu_a, glu_g, rq, rk, rv, rg, q_a, kv_a, _, ga, gb, gc = part
        kr = w[:, c[8] - NOPE:c[8] - NOPE + P]
        uq = A(w_uq[l]).reshape(3, P, HM, QK).transpose(1, 2, 0, 3).reshape(P, HM, 3 * QK)
        uq_blocks = []
        h = 0
        for n in UQ_HEADS:
            b = uq[:, h:h + n].reshape(P, n * 3 * QK)
            uq_blocks.append(np.concatenate([b, np.zeros((P, 8 * P - b.shape[1]), b.dtype)], 1))
            h += n
        return np.concatenate([
            blocks(paired(glu_a, glu_g)), blocks(tiles(rq)), blocks(tiles(rk)), blocks(tiles(rv)), blocks(tiles(rg)),
            blocks(tiles(ga)), blocks(tiles(w_conv_out[l])), blocks(tiles(gb)), blocks(tiles(w_ret_out[l])),
            blocks(tiles(q_a)), blocks(tiles(kv_a)), blocks(tiles(kr)), np.stack(uq_blocks),
            blocks(tiles(gc)), blocks(tiles(w_mla_out[l])), blocks(tiles(w_out[l])),
            blocks(paired(w_gate[l], w_up[l])), blocks(tiles(w_down[l])), blocks(tiles(w_ple_gate[l])), blocks(tiles(w_ple_proj[l])),
        ])

    def channel_major(prompt, sample, width):
        x = np.concatenate([A(prompt).reshape(TP, width), A(sample).reshape(NB, width)])
        return x.T.reshape(width // P, P, T).transpose(1, 0, 2)

    def vectors(l):
        def cols(g, n):
            g = A(g)
            if g.shape[0] < P:
                return np.concatenate([g, np.zeros(P - g.shape[0], g.dtype)]).reshape(P, 1)
            return g.reshape(n, P).T

        taps = A(w_dw[l]).T.reshape(CT, P, TAPS)
        taps = np.concatenate([taps, np.zeros((CT, P, 1), taps.dtype)], 2).transpose(1, 0, 2).reshape(P, CT * 32)
        return np.concatenate([cols(g_mix[l], KT), cols(g_ffn[l], KT), cols(g_ple[l], KT), taps, cols(b_dw[l], CT),
                               cols(g_cln[l], CT), cols(b_cln[l], CT), cols(g_rgn[l], KT), cols(g_qa[l], 3),
                               cols(g_kva[l], 2), cols(g_qn[l], 1), cols(g_kn[l], 1)], 1)

    L = range(DEPTH)
    n_phys = cache_ckv.shape[1]
    arrays = {
        "x": channel_major(x_prompt, x_sample, D),
        "p": np.stack([channel_major(p_prompt[l], p_sample[l], PLE) for l in L]),
        "stream": np.concatenate([layer_stream(l) for l in L]),
        "uk": np.stack([A(w_uk[l]).reshape(2, P, 512).transpose(1, 0, 2) for l in L]),
        "uv": np.stack([A(w_uv[l]).reshape(2, P, 512).transpose(1, 0, 2) for l in L]),
        "ukt": np.stack([A(w_uk[l]).reshape(KVL, HM, NOPE).transpose(2, 1, 0) for l in L]),
        "vec": np.stack([vectors(l) for l in L]).transpose(1, 0, 2),
        "tab": constants(),
        "cache": np.concatenate([A(cache_ckv), A(cache_kpe)], 3).reshape(DEPTH * n_phys, PAGE, KVL + ROPE),
        "pages": A(page_table).reshape(1, NB * NT),
        "state": A(state_ret).reshape(DEPTH * NB, HR, DK, DV),
        "conv": A(state_conv).reshape(DEPTH, NB, TAPS - 1, CT, P).transpose(0, 4, 3, 1, 2),
    }
    outs = {"y": (P, KT, T), "ckv_o": (DEPTH, P, 2, T), "kpe_o": (DEPTH, ROPE, T), "ret_p": (DEPTH, HR, DK, DV),
            "ret_s": (DEPTH * NB, HR, DK, DV), "conv_p": (DEPTH, P, CT, TAPS - 1), "conv_s": (DEPTH, P, CT, NB, TAPS - 1)}
    nc = bacc.Bacc("TRN2", target_bir_lowering=False, num_devices=1)
    arrays = {f"in_{k}": np.ascontiguousarray(a) for k, a in arrays.items()}
    args = [nc.dram_tensor(n, a.shape, mybir.dt.from_np(a.dtype), kind="ExternalInput").ap() for n, a in arrays.items()]
    args += [nc.dram_tensor(f"out_{n}", s, F32, kind="ExternalOutput").ap() for n, s in outs.items()]
    build(nc, *args)
    r = run_bass_kernel_spmd(nc, [arrays], core_ids=[0]).results[0]

    y = r["out_y"].transpose(2, 1, 0).reshape(T, D)
    ckv_o = r["out_ckv_o"].transpose(0, 3, 2, 1).reshape(DEPTH, T, KVL)
    kpe_o = r["out_kpe_o"].transpose(0, 2, 1)
    conv_p = r["out_conv_p"].transpose(0, 3, 2, 1).reshape(DEPTH, 1, TAPS - 1, CONV)
    conv_s = r["out_conv_s"].transpose(0, 3, 4, 2, 1).reshape(DEPTH, NB, TAPS - 1, CONV)
    return (y[:TP].reshape(1, TP, D), y[TP:].reshape(NB, 1, D),
            ckv_o[:, :TP].reshape(DEPTH, 1, TP, KVL), kpe_o[:, :TP].reshape(DEPTH, 1, TP, ROPE),
            ckv_o[:, TP:].reshape(DEPTH, NB, 1, KVL), kpe_o[:, TP:].reshape(DEPTH, NB, 1, ROPE),
            r["out_ret_p"].reshape(DEPTH, 1, HR, DK, DV), r["out_ret_s"].reshape(DEPTH, NB, HR, DK, DV), conv_p, conv_s)
```

```python
from contextlib import ExitStack

import numpy as np
import concourse.bass as bass
from concourse import mybir

F32 = mybir.dt.float32
F32R = mybir.dt.float32r
I32 = mybir.dt.int32
ALU = mybir.AluOpType
ACT = mybir.ActivationFunctionType
AX = mybir.AxisListType
ds = bass.ds

P = 128
DEPTH, D, TP, NB = 2, 1024, 256, 8
T = TP + NB
KT = D // P
EPS = 1e-6
CONV, TAPS = 512, 31
CT = CONV // P
HR, DK, DV = 4, 128, 256
HM, NOPE, ROPE, VD = 8, 64, 32, 64
QK = NOPE + ROPE
QL, KVL = 384, 256
PAST, PAGE = 2048, 128
NT = PAST // PAGE
FF = 2816
FT = FF // P
PLE = 256
ATT_SCALE = QK ** -0.5

STAGES = [("glu", 8, 8), ("qk", 8, 8), ("v", 8, 8), ("rg", 8, 8), ("gate_a", 8, 8), ("conv_out", 4, 8),
          ("gate_b", 8, 8), ("ret_out", 8, 8), ("kvq", 6, 6), ("uq", 3, 8), ("gate_c", 8, 8), ("mla_out", 4, 8),
          ("w_out", 8, 8), ("ffn_in", 2 * FT, 2 * FT), ("ffn_out", FT, 8), ("ple_gate", 8, 8), ("ple_proj", 2, 8)]
B0, C0 = {}, {}
NBLK = NCHUNK = 0
for _name, _b, _c in STAGES:
    B0[_name], C0[_name] = NBLK, NCHUNK
    NBLK += _b
    NCHUNK += _c
RING = 4
UQ_HEADS = (3, 3, 2)

TAB = {}
_n = 0
for _name, _w in (("rope_c", 2 * T), ("rope_s", 2 * T), ("decay", HR * 384), ("mask", 384), ("mla_c", T), ("mla_s", T),
                  ("ident", P), ("ones", P), ("rot", QK), ("kdec", 2 * HR),
                  ("pick3", NB), ("pick", NB * NB)):
    TAB[_name] = _n
    _n += _w
NTAB = _n
VEC = {}
_n = 0
for _name, _w in (("g_mix", KT), ("g_ffn", KT), ("g_ple", KT), ("w_dw", CT * 32), ("b_dw", CT), ("g_cln", CT),
                  ("b_cln", CT), ("g_rgn", KT), ("g_qa", 3), ("g_kva", 2), ("g_qn", 1), ("g_kn", 1)):
    VEC[_name] = _n
    _n += _w
NVEC = _n

GAMMA = [1.0 - 2.0 ** (-5.0 - h) for h in range(HR)]


def build(nc, x_in, p_in, stream, uk_in, uv_in, ukt_in, vec_in, tab_in, cache_in, pages_in, state_in, conv_in,
          y_out, ckv_out, kpe_out, ret_prompt_out, ret_sample_out, conv_prompt_out, conv_sample_out):
    ctx = ExitStack()
    with ctx:
        base = -(-nc.sbuf_base // 32) * 32
        top = [0]
        names = {}

        def at_offset(name, cols, offset, dt=F32, shape=None):
            names[name] = (offset, cols * 4)
            return nc.alloc_sbuf_tensor_at(name, [P] + (shape or [cols]), dt, offset=base + offset)

        def place(name, shape, dt=F32):
            cols = int(np.prod(shape))
            off = top[0]
            top[0] += -(-cols * 4 // 32) * 32
            return at_offset(name, cols, off, dt, list(shape))

        xT = place("xT", [KT, T])
        h_hi = place("h_hi", [KT, T], F32R)
        h_lo = place("h_lo", [KT, T], F32R)
        w_raw = [place(f"w_raw{r}", [8 * P]) for r in range(RING)]
        w_hi = [place(f"w_hi{r}", [8 * P], F32R) for r in range(RING)]
        w_lo = [place(f"w_lo{r}", [8 * P], F32R) for r in range(RING)]
        tab = place("tab", [NTAB])
        vecs = place("vecs", [DEPTH, NVEC])
        vec = place("vec", [NVEC])
        pages = place("pages", [NB * NT], I32)
        uk = place("uk", [2, 512])
        uv = place("uv", [2, 512])
        off_ukh = top[0]
        UKW = 512 + HM
        UKA, UKB = slice(0, 256 + HM), slice(256 + HM, UKW)
        uk_hi = place("uk_hi", [2, UKW], F32R)
        uk_lo = place("uk_lo", [2, UKW], F32R)
        off_ukt = top[0]
        uk_t = place("uk_t", [HM, 256])
        zt = place("zt", [4, T])
        et = place("et", [4, T])
        rstd = place("rstd", [T])
        rsb = place("rsb", [2, T])

        kpe_own = place("kpe_own", [T])
        ckv_own = place("ckv_own", [2, NB])
        own = place("own", [HM, NB])
        qt_hi = place("qt_hi", [NB, 2, HM], F32R)
        qt_lo = place("qt_lo", [NB, 2, HM], F32R)
        q_pick = place("q_pick", [NB, HR, NB])
        qpe4 = place("qpe4", [NB, HM])
        lat = place("lat", [2, HM, NB])
        small = place("small", [96])
        q_pe = [place(f"q_pe{i}", [4, HM]) for i in range(3)]
        off_mix = top[0]
        mix = place("mix", [KT, T])
        off_g = top[0]
        gate = place("gate", [KT, T])
        off_s = top[0]
        s_hi = place("s_hi", [KT, T], F32R)
        s_lo = place("s_lo", [KT, T], F32R)
        off_u = top[0]
        a_hi = at_offset("a_hi", FT * T, off_g, F32R, [FT, T])
        a_lo = at_offset("a_lo", FT * T, off_g + FT * T * 4, F32R, [FT, T])
        p_raw = at_offset("p_raw", 2 * T, -(-(off_g + 2 * FT * T * 4) // 32) * 32, F32, [2, T])
        p_hi = at_offset("p_hi", 2 * T, off_s, F32R, [2, T])
        p_lo = at_offset("p_lo", 2 * T, off_s + 2 * T * 4, F32R, [2, T])
        yconv = at_offset("yconv", CT * T, off_mix, F32, [CT, T])
        o = off_u
        u_ext = at_offset("u_ext", CT * 288, o, F32, [CT, 288])
        u_smp = at_offset("u_smp", CT * NB * 31, o + CT * 288 * 4, F32, [CT, NB, 31])
        oT = at_offset("oT", KT * T, o, F32, [KT, T])
        o += CT * 288 * 4 + CT * NB * 31 * 4
        qk = at_offset("qk", KT * T, o, F32, [KT, T]); o += KT * T * 4
        v_nat = at_offset("v_nat", 2 * 1024, o, F32, [2, 1024]); o += 8192
        v3 = at_offset("v3", 1024, o, F32R, [1024])
        conv_stage = at_offset("conv_stage", CT * NB * 30, o, F32, [CT, NB, 30]); o += 4096
        k_nat = at_offset("k_nat", 2 * 512, o, F32, [2, 512]); o += 4096
        k3 = at_offset("k3", 512, o, F32R, [512]); o += 2048
        k_smp = at_offset("k_smp", 512, off_s, F32, [512])
        v_smp = at_offset("v_smp", 1024, off_s + KT * T * 4, F32, [1024])
        o_row = at_offset("o_row", 1024, names["v_nat"][0], F32, [1024])
        rgs = at_offset("rgs", KT * T, o, F32, [KT, T])
        conv_prod = at_offset("conv_prod", CT * NB * 31, o, F32, [CT, NB, 31])
        conv_new = at_offset("conv_new", CT * NB * 30, o + CT * NB * 31 * 4, F32, [CT, NB, 30]); o += KT * T * 4
        end1 = o
        state = [at_offset(f"state{i}", 1024, a, F32, [HR, DV])
                 for i, a in enumerate((off_ukt, off_ukt + 4096, off_s + 4 * T * 4, off_s + 12 * T * 4))]
        sT = [at_offset(f"sT{i}", 384, off_ukh + 1536 * i, F32, [384]) for i in range(2)]
        k_mask = [at_offset(f"k_mask{i}", 512, off_ukh + 3072 + 2048 * i, F32R, [512]) for i in range(2)]
        ret_stage = at_offset("ret_stage", 1024, names["zt"][0], F32, [HR, DV])
        KV = KVL + ROPE
        cache = [at_offset(f"cache{i}", NT * KV, (off_u, off_u + NT * KV * 4, off_g)[i], F32, [NT, KV]) for i in range(3)]
        o = off_u + 2 * NT * KV * 4
        vm = at_offset("vm", 2 * 512, o, F32, [2, 512])
        sq = [at_offset(f"sq{i}", 512, names["et"][0] + 2048 * i, F32, [HM, 64]) for i in range(2)]
        o += 4096
        ssq = [at_offset(f"ssq{i}", NT * HM, o + 512 * i, F32, [NT, HM]) for i in range(3)]
        sspe = [at_offset(f"sspe{i}", NT, o + 1536 + 64 * i, F32, [NT]) for i in range(3)]
        kn_r = at_offset("kn_r", NT * HM, o + 1728, F32, [NT, HM])
        sc = at_offset("sc", NT * HM, o + 2240, F32, [NT, HM])
        pr = at_offset("pr", NT * HM, o + 2752, F32, [NT, HM])
        scores = [at_offset(f"scores{i}", NT * HM, off_g + NT * KV * 4 + 1536 + 512 * i, F32, [NT, HM]) for i in range(3)]
        scores_pe = [at_offset(f"scores_pe{i}", NT * HM, off_g + NT * KV * 4 + 512 * i, F32, [NT, HM]) for i in range(3)]
        latn = at_offset("latn", KVL, names["rsb"][0])
        kpeT = at_offset("kpeT", 512, o - 4096, F32, [4, P])
        kpe_n = at_offset("kpe_n", 512, o - 2048, F32, [NT, ROPE])
        end2 = o + 3264
        qm = at_offset("qm", HM * T, off_g, F32, [HM, T])
        sqg = at_offset("sqg", 5 * T, off_g, F32, [5, T])
        qa_hi = at_offset("qa_hi", 3 * T, off_s, F32R, [3, T])
        qa_lo = at_offset("qa_lo", 3 * T, off_s + 3 * T * 4, F32R, [3, T])
        ckvT = at_offset("ckvT", 2 * T, off_s + 6 * T * 4, F32, [2, T])
        km = at_offset("km", HM * T, off_s + 8 * T * 4, F32, [HM, T])
        ap_s = [at_offset(f"ap_s{i}", 384, off_ukh + 1536 * i, F32, [384]) for i in range(3)]
        ap_t = [at_offset(f"ap_t{i}", 384, off_ukh + 4608 + 1536 * i, F32, [384]) for i in range(2)]
        oM = at_offset("oM", 4 * T, names["zt"][0], F32, [4, T])
        ct_hi = [at_offset(f"ct_hi{i}", 512, off_ukt + 4096 * i, F32R, [4, P]) for i in range(2)]
        ct_lo = [at_offset(f"ct_lo{i}", 512, off_ukt + 4096 * i + 2048, F32R, [4, P]) for i in range(2)]
        cv_hi, cv_lo = s_hi, s_lo
        a_end = off_g + 2 * FT * T * 4
        total = max(end1, end2, a_end)
        assert base + total <= nc.sbuf_usable_end, (base, total, end1, end2, a_end, nc.sbuf_usable_end)
        ctx.enter_context(nc.sbuf_tensor("arena", [P, (base + total - nc.sbuf_base) // 4 + 1], F32))

        bank = [ctx.enter_context(nc.psum_tensor(f"bank{i}", [P, 512], F32)) for i in range(8)]

        DMA = 16

        class Sem:

            def __init__(self, name, per=1, credit=0):
                self.s = ctx.enter_context(nc.semaphore(name))
                self.per, self.credit = per, credit

            def at(self, l, n):
                return l * self.per + (n + self.credit)

        settled = {e: Sem(f"settled_{i}") for i, e in enumerate((nc.sync.engine, nc.tensor.engine, nc.vector.engine))}

        def settle(eng):
            eng.sem_inc(settled[eng.engine].s, 1)

        class Steps:

            def __init__(self):
                self.n = 0

            def one(self):
                self.n += 1
                return 1

        def col(name, k=0):
            return vec[:, VEC[name] + k:VEC[name] + k + 1]

        def tb(name, w, a=0, rows=slice(0, P)):
            return tab[rows, TAB[name] + a:TAB[name] + a + w]

        ident = tb("ident", P)
        ones = tb("ones", P)

        x_loaded = Sem("x_loaded")
        consts_loaded = Sem("consts_loaded")
        tables_loaded = Sem("tables_loaded")
        w_loaded = [Sem(f"w_loaded{r}", 16 * ((NBLK - r + RING - 1) // RING)) for r in range(RING)]
        w_split = Sem("w_split", NBLK, 1)
        w_high = Sem("w_high", NBLK)
        w_begun = Sem("w_begun", NBLK)
        chunk_ready = Sem("chunk_ready", NCHUNK)
        chunk_free = Sem("chunk_free", NCHUNK, 4)
        h_high = Sem("h_high", 3 * KT)
        h_low = Sem("h_low", 3 * KT)
        x_sq = Sem("x_sq", 3 * KT)
        x_sum = Sem("x_sum", 3 * KT)
        x_root = Sem("x_root", 3)

        NEXP = 4 + 8 + 24 + FT + 8
        exp_ready = Sem("exp_ready", NEXP)
        E0 = {"glu": 0, "rg": 4, "gate_a": 12, "gate_b": 20, "gate_c": 28, "ffn_in": 36, "ple_gate": 36 + FT}
        vec_ready = Sem("vec_ready")
        conv_state_loaded = Sem("conv_state_loaded", 16)
        conv_state_placed = Sem("conv_state_placed")
        conv_biased = Sem("conv_biased")
        u_ready = Sem("u_ready")
        conv_new_ready = Sem("conv_new_ready")
        conv_stored = Sem("conv_stored", 32)
        rope_ready = Sem("rope_ready", 2)
        k_turned = Sem("k_turned")
        k_copied = Sem("k_copied")
        v_turned = Sem("v_turned", 2)
        v_copied = Sem("v_copied", 2, 1)
        conv_done = Sem("conv_done")
        cln_sum = Sem("cln_sum", 2)
        cln_centred = Sem("cln_centred")
        cln_sq = Sem("cln_sq")
        cln_root = Sem("cln_root")
        cln_y = Sem("cln_y")
        cln_exp = Sem("cln_exp")
        conv_act = Sem("conv_act")
        conv_high = Sem("conv_high")
        conv_split = Sem("conv_split")
        ret_s = Sem("ret_s", HR)
        ret_sd = Sem("ret_sd", HR)
        ret_o = Sem("ret_o", HR)
        ret_oc = Sem("ret_oc", HR)
        ret_st = Sem("ret_st", HR)
        ret_stc = Sem("ret_stc", HR)
        ret_stored = Sem("ret_stored", 16)
        st_loaded = [Sem(f"st_loaded{i}", 32) for i in range(4)]
        st_stored = [Sem(f"st_stored{i}", 32) for i in range(4)]
        st_mask = Sem("st_mask", NB)
        st_outer = Sem("st_outer", NB)
        st_new = Sem("st_new", NB)
        st_o = Sem("st_o", NB)
        st_row = Sem("st_row")
        st_turned = Sem("st_turned")
        st_oc = Sem("st_oc")
        gn_sum = Sem("gn_sum", HR)
        gn_c = Sem("gn_c", HR)
        gn_sq = Sem("gn_sq", HR)
        gn_var = Sem("gn_var", HR)
        gn_root = Sem("gn_root", HR)
        gn_y = Sem("gn_y", HR)
        gn_high = Sem("gn_high", HR)
        gn_low = Sem("gn_low", HR)
        mla_w_loaded = Sem("mla_w_loaded", 32)
        p_loaded = Sem("p_loaded", 16)
        ukt_loaded = Sem("ukt_loaded", 16)
        kvq_act = Sem("kvq_act", 5)
        qa_low = Sem("qa_low")
        kvq_sum = Sem("kvq_sum", 2)
        kvq_root = Sem("kvq_root", 2)
        ckv_ready = Sem("ckv_ready")
        kr_rot = Sem("kr_rot")
        kpe_ready = Sem("kpe_ready")
        own_stored = Sem("own_stored", 32)
        uq_rot = Sem("uq_rot", HM)
        q_roped = Sem("q_roped", HM)
        hn_sq = Sem("hn_sq", 2 * HM)
        hn_sum = Sem("hn_sum", 2 * HM)
        hn_root = Sem("hn_root", 2 * HM)
        hn_done = Sem("hn_done", 2 * HM)
        kn_ready = Sem("kn_ready", HM)
        kn_copied = Sem("kn_copied", HM)
        vm_ready = Sem("vm_ready")
        vm_copied = Sem("vm_copied")
        qs_ready = Sem("qs_ready", 2)
        own_sum = Sem("own_sum")
        own_copied = Sem("own_copied")
        qt_ready = Sem("qt_ready")
        qt_high = Sem("qt_high")
        qt_low = Sem("qt_low")
        at_s = Sem("at_s", HM)
        at_m = Sem("at_m", HM)
        at_p = Sem("at_p", HM)
        at_n = Sem("at_n", HM)
        at_t = Sem("at_t", HM)
        at_tc = Sem("at_tc", HM)
        at_o = Sem("at_o", HM)
        at_oc = Sem("at_oc", HM)
        uk_high = Sem("uk_high")
        uk_low = Sem("uk_low")
        ck_loaded = [Sem(f"ck_loaded{i}", 16 * NT * ((NB - i + 2) // 3)) for i in range(3)]
        c_kst = Sem("c_kst", NB)
        c_kt = Sem("c_kt", NB)
        c_ktc = Sem("c_ktc", NB)
        c_ksq = Sem("c_ksq", NB)
        c_kss = Sem("c_kss", NB)
        c_q = Sem("c_q", NB)

        c_tr = Sem("c_tr", NB * 8)
        c_hi = Sem("c_hi", NB * 8)
        c_lo = Sem("c_lo", NB * 8)
        c_kn = Sem("c_kn", NB * NT)
        c_sq = Sem("c_sq", NB * NT)
        c_ss = Sem("c_ss", NB * NT)
        c_sr = Sem("c_sr", NB * NT)
        c_pe = Sem("c_pe", NB)
        c_pec = Sem("c_pec", NB)
        t_cp = Sem("t_cp", NB)
        t_tr = Sem("t_tr", NB)
        t_tot = Sem("t_tot", NB)
        t_root = Sem("t_root", NB)
        t_mx = Sem("t_mx", NB)
        t_mt = Sem("t_mt", NB)
        t_dg = Sem("t_dg", NB)
        t_bc = Sem("t_bc", NB)
        t_shift = Sem("t_shift", NB)
        t_p = Sem("t_p", NB)
        t_l = Sem("t_l", NB)
        t_lat = Sem("t_lat", NB)
        t_fin = Sem("t_fin", NB)
        uvs_ready = Sem("uvs_ready")
        uvs_copied = Sem("uvs_copied")
        mla_high = Sem("mla_high")
        mla_split = Sem("mla_split")
        mix_done = Sem("mix_done", KT)
        mix_high = Sem("mix_high", KT)
        mix_low = Sem("mix_low", KT)
        ffn_a = Sem("ffn_a", FT)
        ffn_high = Sem("ffn_high", FT)
        ffn_low = Sem("ffn_low", FT)
        p_high = Sem("p_high")
        p_low = Sem("p_low")
        x_final = Sem("x_final")
        act_step = Sem("act_step")
        dve_step = Sem("dve_step")
        y_stored = Sem("y_stored", 16)

        O_BANK = (6, 7, 2, 3)
        GATES = ("gate_a", "gate_b", "gate_c", "ple_gate")
        GATE_OF = {"conv_out": "gate_a", "ret_out": "gate_b", "mla_out": "gate_c"}
        block = ctx.enter_context(nc.Block())
        CUT_RET = (B0["conv_out"] + RING) // RING * RING
        CUT_CACHE = (B0["gate_c"] + RING) // RING * RING

        CUT_P = B0["ffn_in"] // RING * RING + RING

        @block.sync
        def _(sp):
            sp.dma_start(xT[:, :, :], x_in).then_inc(x_loaded.s, DMA)
            sp.dma_start(vecs[:, :, :], vec_in).then_inc(x_loaded.s, DMA)
            first = TAB["ident"]
            sp.dma_start(tab[:, first:], tab_in[:, first:]).then_inc(consts_loaded.s, DMA)
            sp.dma_start(pages[0:1, :], pages_in).then_inc(consts_loaded.s, DMA)
            sp.dma_start(tab[:, 0:first], tab_in[:, 0:first]).then_inc(tables_loaded.s, DMA)
            sp.wait_ge(consts_loaded.s, 2 * DMA)

            with sp.Fori(0, DEPTH) as l:
                def load_block(n, r, reuse):
                    sp.wait_ge(w_split.s, w_split.at(l, reuse))
                    sp.dma_start(w_raw[r][:, :], stream[ds(l * NBLK + n, 1)].rearrange("o p c -> (o p) c"))\
                        .then_inc(w_loaded[r].s, DMA)

                def load_blocks(a, b):
                    whole = (b - a) // RING
                    if whole > 0:
                        with sp.Fori(0, whole) as j:
                            for r in range(RING):
                                load_block(j * RING + (a + r), r, j * RING + (a + r - RING + 1))
                    for n in range(a + whole * RING, b):
                        load_block(n, n % RING, n - RING + 1)

                sp.wait_ge(w_split.s, w_split.at(l, 0))
                sp.dma_start(conv_stage[:, :, :, :], conv_in[ds(l, 1)].rearrange("o p c b w -> (o p) c b w"))\
                    .then_inc(conv_state_loaded.s, DMA)
                for r in range(RING):
                    load_block(r, r, 0)
                load_blocks(RING, CUT_RET)
                sp.dma_start(uk[:, :, :], uk_in[ds(l, 1)].rearrange("o p c n -> (o p) c n")).then_inc(mla_w_loaded.s, DMA)
                sp.dma_start(uv[:, :, :], uv_in[ds(l, 1)].rearrange("o p c n -> (o p) c n")).then_inc(mla_w_loaded.s, DMA)

                def load_state(b, i):
                    sp.dma_start(state[i][:, :, :], state_in[ds(l * NB + b, 1)].rearrange("o h d e -> d (o h) e"))\
                        .then_inc(st_loaded[i].s, DMA)

                def store_state(b, i):
                    sp.wait_ge(st_new.s, st_new.at(l, b + 1))
                    sp.dma_start(ret_sample_out[ds(l * NB + b, 1)].rearrange("o h d e -> d (o h) e"), state[i][:, :, :])\
                        .then_inc(st_stored[i].s, DMA)

                for i in range(4):
                    load_state(i, i)
                for b in range(NB):
                    store_state(b, b % 4)
                    if b >= 1 and b + 3 < NB:
                        st = st_stored[(b - 1) % 4]
                        sp.wait_ge(st.s, st.at(l, DMA))
                        sp.wait_ge(st_o.s, st_o.at(l, b))
                        load_state(b + 3, (b - 1) % 4)
                for i in range(2):
                    sp.wait_ge(st_stored[i].s, st_stored[i].at(l, 2 * DMA))
                sp.wait_ge(st_o.s, st_o.at(l, NB))
                sp.dma_start(uk_t[0:NOPE, :, :], ukt_in[ds(l, 1)].rearrange("o p c n -> (o p) c n")).then_inc(ukt_loaded.s, DMA)
                load_blocks(CUT_RET, CUT_CACHE)

                n_phys = cache_in.shape[0] // DEPTH
                def load_cache(b, i):
                    with sp.Fori(0, NT // 4) as g:
                        for u in range(4):
                            page = sp.value_load(pages[0:1, ds(g * 4 + (b * NT + u), 1)], min_val=0, max_val=n_phys - 1)
                            sp.dma_start(cache[i][:, ds(g * 4 + u, 1), :].rearrange("p t c -> p (t c)"),
                                         cache_in[ds(page + l * n_phys, 1)].rearrange("o p c -> (o p) c")).then_inc(ck_loaded[i].s, DMA)

                sp.wait_ge(gn_low.s, gn_low.at(l, HR))
                sp.wait_ge(gn_high.s, gn_high.at(l, HR))
                sp.wait_ge(ret_stored.s, ret_stored.at(l, DMA))
                settle(sp)
                load_cache(0, 0)
                load_cache(1, 1)
                sp.wait_ge(at_oc.s, at_oc.at(l, HM))
                sp.wait_ge(own_stored.s, own_stored.at(l, 32))
                settle(sp)
                load_cache(2, 2)
                for b in range(3, NB):
                    sp.wait_ge(t_lat.s, t_lat.at(l, b - 2))
                    sp.wait_ge(c_ksq.s, c_ksq.at(l, b - 2))
                    settle(sp)
                    load_cache(b, b % 3)
                load_blocks(CUT_CACHE, CUT_P)
                sp.wait_ge(t_fin.s, t_fin.at(l, NB))
                sp.dma_start(p_raw[:, :, :], p_in[ds(l, 1)].rearrange("o p c n -> (o p) c n")).then_inc(p_loaded.s, DMA)
                load_blocks(CUT_P, NBLK)

            sp.wait_ge(conv_stored.s, DEPTH * 32)
            sp.wait_ge(ret_stored.s, DEPTH * DMA)
            sp.wait_ge(own_stored.s, DEPTH * 32)
            for i in range(4):
                sp.wait_ge(st_stored[i].s, DEPTH * 32)
            sp.wait_ge(x_final.s, 1)
            sp.dma_start(y_out, xT[:, :, :]).then_inc(y_stored.s, DMA)
            sp.wait_ge(y_stored.s, DMA)

        @block.gpsimd
        def _(pool):
            pool.sem_inc(w_split.s, 1)
            with pool.Fori(0, DEPTH) as l:
                def cut_low(n, r):
                    pool.wait_ge(w_high.s, w_high.at(l, n + 1))
                    pool.tensor_tensor(w_lo[r][:, :], w_raw[r][:, :], w_hi[r][:, :].bitcast(F32), ALU.subtract)\
                        .then_inc(w_split.s, 1)

                with pool.Fori(0, NBLK // RING) as j:
                    for r in range(RING):
                        cut_low(j * RING + r, r)
                for n in range(NBLK // RING * RING, NBLK):
                    cut_low(n, n % RING)

        @block.tensor
        def _(pe):
            mm = pe.matmul
            pe.wait_ge(consts_loaded.s, 2 * DMA)
            rot = tb("rot", QK, 0, slice(0, QK))

            def three(out, w, rhs, first, last):
                a = mm(out, w[0], rhs[0], start=first, stop=False)
                mm(out, w[0], rhs[1], start=False, stop=False)
                return a, mm(out, w[1], rhs[0], start=False, stop=last)

            with pe.Fori(0, DEPTH) as l:
                def chunk(c, c_static, run, rhs, M=P, wait_k=None):
                    pe.wait_ge(chunk_free.s, chunk_free.at(l, c - 3))
                    out = bank[c_static % 4][0:M, 0:T]
                    for k, (n, n_static, a) in enumerate(run):
                        s = n_static % RING
                        if a == 0:
                            pe.wait_ge(w_split.s, w_split.at(l, n + 1))
                        if wait_k is not None:
                            wait_k(k)
                        first, last = three(out, (w_hi[s][:, a:a + M], w_lo[s][:, a:a + M]),
                                            (rhs[0][:, k, :], rhs[1][:, k, :]), k == 0, k == len(run) - 1)
                        if a == 0:
                            first.then_inc(w_begun.s, 1)
                    last.then_inc(chunk_ready.s, 1)

                def group(stage, i, rhs, wait_k=None):
                    for r in range(4):
                        n, c = B0[stage] + r, C0[stage] + r
                        chunk(i * 4 + c, c, [(i * 4 + n, n, k * P) for k in range(KT)], rhs, wait_k=wait_k if r == 0 else None)

                def stream_chunk(stage, m, kt, rhs, wait_k=None):
                    t0 = m * kt
                    chunk(C0[stage] + m, C0[stage] + m,
                          [(B0[stage] + (t0 + k) // 8, B0[stage] + (t0 + k) // 8, (t0 + k) % 8 * P) for k in range(kt)],
                          rhs, wait_k=wait_k)

                h = (h_hi, h_lo)
                s_ = (s_hi, s_lo)

                def token_sums(w):
                    for k in range(KT):
                        pe.wait_ge(x_sq.s, x_sq.at(l, w * KT + k + 1))
                        mm(bank[4][:, 0:T], ones, (et if k < 4 else zt)[:, k % 4, :], start=k == 0, stop=k == KT - 1).then_inc(x_sum.s, 1)

                def h_there(w):
                    return lambda k: pe.wait_ge(h_low.s, h_low.at(l, w * KT + k + 1))

                pe.wait_ge(chunk_free.s, chunk_free.at(l, 0))
                token_sums(0)
                with pe.Fori(0, 2) as i:
                    group("glu", i, h, h_there(0))
                with pe.Fori(0, 2) as i:
                    group("qk", i, h)
                with pe.Fori(0, 2) as i:
                    group("v", i, h)
                    pe.wait_ge(x_root.s, x_root.at(l, 1))
                    pe.wait_ge(v_copied.s, v_copied.at(l, i))
                    pe.wait_ge(chunk_free.s, chunk_free.at(l, i * 4 + (C0["v"] + 4)))
                    for r in range(4):
                        for c in range(2):
                            pe.transpose(bank[4 + c][:, r * P:r * P + P], zt[:, r, c * P:c * P + P], ident)
                        ins = pe.transpose(bank[6][0:NB, r * P:r * P + P], zt[:, r, TP:T], ident)
                    ins.then_inc(v_turned.s, 1)
                pe.wait_ge(v_copied.s, v_copied.at(l, 2))
                for hd in range(HR):
                    for c in range(2):
                        pe.transpose(bank[4 + c][:, hd * P:hd * P + P], qk[:, HR + hd, c * P:c * P + P], ident)
                    ins = pe.transpose(bank[6][0:NB, hd * P:hd * P + P], qk[:, HR + hd, TP:T], ident)
                ins.then_inc(k_turned.s, 1)
                with pe.Fori(0, 2) as i:
                    group("rg", i, h)
                with pe.Fori(0, 2) as i:
                    group("gate_a", i, h)

                pe.wait_ge(conv_done.s, conv_done.at(l, 1))
                pe.wait_ge(chunk_free.s, chunk_free.at(l, C0["conv_out"]))
                for c in range(CT):
                    ins = mm(bank[0][:, 0:T], ones, yconv[:, c, :], start=c == 0, stop=c == CT - 1)
                ins.then_inc(cln_sum.s, 1)

                def ret_scores(hd):
                    b = bank[4 + hd % 2]
                    if hd >= 2:
                        pe.wait_ge(ret_sd.s, ret_sd.at(l, hd - 1))
                    mm(b[:, 0:TP], qk[:, HR + hd, 0:P], qk[:, hd, 0:TP], start=True, stop=True)
                    mm(b[:, TP:TP + P], qk[:, HR + hd, P:TP], qk[:, hd, P:TP], start=True, stop=True).then_inc(ret_s.s, 1)

                pe.wait_ge(k_copied.s, k_copied.at(l, 1))
                ret_scores(0)
                ret_scores(1)
                pe.wait_ge(cln_sq.s, cln_sq.at(l, 1))
                for c in range(CT):
                    ins = mm(bank[1][:, 0:T], ones, et[:, c, :], start=c == 0, stop=c == CT - 1)
                ins.then_inc(cln_sum.s, 1)
                for hd in range(HR):
                    pe.wait_ge(ret_sd.s, ret_sd.at(l, hd + 1))
                    if hd:
                        pe.wait_ge(ret_oc.s, ret_oc.at(l, hd))
                    for e in range(2):
                        o = bank[6][:, e * TP:e * TP + TP]
                        v0 = hd * DV + e * P
                        mm(o, v_nat[:, 0, v0:v0 + P], sT[hd % 2][:, 0:TP], start=True, stop=False)
                        ins = mm(o[:, P:TP], v_nat[:, 1, v0:v0 + P], sT[hd % 2][:, TP:TP + P], start=False, stop=True)
                    ins.then_inc(ret_o.s, 1)
                    if hd:
                        pe.wait_ge(ret_stc.s, ret_stc.at(l, hd))
                    for c in range(2):
                        ins = mm(bank[7][:, 0:DV], k_nat[:, c, hd * P:hd * P + P], v_nat[:, c, hd * DV:hd * DV + DV],
                                 start=c == 0, stop=c == 1)
                    ins.then_inc(ret_st.s, 1)
                    if hd + 2 < HR:
                        ret_scores(hd + 2)

                def outer(b):
                    pe.wait_ge(st_mask.s, st_mask.at(l, b + 1))
                    if b >= 2:
                        pe.wait_ge(st_new.s, st_new.at(l, b - 1))
                    for hd in range(HR):
                        ins = mm(bank[(4, 0)[b % 2] + hd // 2][:, hd % 2 * DV:hd % 2 * DV + DV], k_mask[b % 2][0:72, hd * P:hd * P + P],
                                 v3[0:72, hd * DV:hd * DV + DV], start=True, stop=True)
                    ins.then_inc(st_outer.s, 1)

                pe.wait_ge(ret_oc.s, ret_oc.at(l, HR))
                pe.wait_ge(ret_stc.s, ret_stc.at(l, HR))
                pe.wait_ge(cln_root.s, cln_root.at(l, 1))
                outer(0)
                outer(1)
                for b in range(NB):
                    pe.wait_ge(st_new.s, st_new.at(l, b + 1))
                    for hd in range(HR):
                        ins = mm(bank[O_BANK[hd]][0:NB, 0:DV], q_pick[:, b, hd, :], state[b % 4][:, hd, :],
                                 start=b == 0, stop=b == NB - 1)
                    ins.then_inc(st_o.s, 1)
                    if b + 2 < NB:
                        outer(b + 2)

                pe.wait_ge(conv_split.s, conv_split.at(l, 1))
                for m in range(KT):
                    if m == 2:
                        pe.wait_ge(st_row.s, st_row.at(l, 1))
                        for k in range(KT):
                            ins = mm(bank[4][:, k * NB:k * NB + NB], o_row[0:NB, k * P:k * P + P], ident[0:NB, 0:NB], start=True, stop=True)
                        ins.then_inc(st_turned.s, 1)
                    stream_chunk("conv_out", m, CT, (cv_hi, cv_lo))

                pe.wait_ge(st_oc.s, st_oc.at(l, 1))
                pe.wait_ge(ret_stc.s, ret_stc.at(l, HR))
                for hd in range(HR):
                    for e in range(2):
                        ins = mm(bank[4 + hd][:, 0:T], ones, oT[:, 2 * hd + e, :], start=e == 0, stop=e == 1)
                    ins.then_inc(gn_sum.s, 1)
                for hd in range(HR):
                    pe.wait_ge(gn_sq.s, gn_sq.at(l, hd + 1))
                    for e in range(2):
                        ins = mm(bank[4 + hd][:, 0:T], ones, et[:, 2 * (hd % 2) + e, :], start=e == 0, stop=e == 1)
                    ins.then_inc(gn_var.s, 1)

                with pe.Fori(0, 2) as i:
                    group("gate_b", i, h)
                pe.wait_ge(gn_low.s, gn_low.at(l, HR))
                settle(pe)
                with pe.Fori(0, 2) as i:
                    group("ret_out", i, s_)

                for m in range(6):
                    n, c = B0["kvq"] + m, C0["kvq"] + m
                    chunk(c, c, [(n, n, k * P) for k in range(KT)], h)
                pe.wait_ge(kvq_act.s, kvq_act.at(l, 3))
                pe.wait_ge(gn_root.s, gn_root.at(l, HR))
                for k in range(3):
                    ins = mm(bank[4][:, 0:T], ones, sqg[:, k, :], start=k == 0, stop=k == 2)
                ins.then_inc(kvq_sum.s, 1)
                pe.wait_ge(kvq_act.s, kvq_act.at(l, 5))
                for k in range(2):
                    ins = mm(bank[5][:, 0:T], ones, sqg[:, 3 + k, :], start=k == 0, stop=k == 1)
                ins.then_inc(kvq_sum.s, 1)
                pe.wait_ge(chunk_free.s, chunk_free.at(l, C0["kvq"] + 6))
                mm(bank[6][0:QK, 0:T], rot, zt[0:QK, 1, :], start=True, stop=True).then_inc(kr_rot.s, 1)

                def head_sum(k, buf_bank):
                    pe.wait_ge(hn_sq.s, hn_sq.at(l, k + 1))
                    if k >= 2:
                        pe.wait_ge(hn_root.s, hn_root.at(l, k - 1))
                    mm(buf_bank[0:QK, 0:T], ones[0:QK, 0:QK], et[0:QK, k % 4, :], start=True, stop=True).then_inc(hn_sum.s, 1)

                pe.wait_ge(qa_low.s, qa_low.at(l, 1))
                pe.wait_ge(kvq_root.s, kvq_root.at(l, 2))
                pe.wait_ge(kpe_ready.s, kpe_ready.at(l, 1))
                for step in range(HM + 3):
                    if step < HM:
                        g = min(step // 3, 2)
                        n, c = B0["uq"] + g, C0["uq"] + step
                        chunk(c, c, [(n, n, ((step - 3 * g) * 3 + k) * QK) for k in range(3)], (qa_hi, qa_lo), M=QK)
                    hd = step - 1
                    if 0 <= hd < HM:
                        pe.wait_ge(chunk_free.s, chunk_free.at(l, C0["uq"] + hd + 1))
                        if hd >= 2:
                            pe.wait_ge(q_roped.s, q_roped.at(l, hd - 1))
                        mm(bank[4 + hd % 2][0:QK, 0:T], rot, qm[0:QK, hd, :], start=True, stop=True).then_inc(uq_rot.s, 1)
                    hd = step - 3
                    if hd >= 0:
                        head_sum(hd, bank[6 + hd % 2])
                pe.wait_ge(mla_w_loaded.s, mla_w_loaded.at(l, 32))
                pe.wait_ge(q_roped.s, q_roped.at(l, HM))
                pe.wait_ge(ckv_ready.s, ckv_ready.at(l, 1))
                for step in range(HM + 2):
                    if step < HM:
                        if step >= 2:
                            pe.wait_ge(kn_copied.s, kn_copied.at(l, step - 1))
                        for c in range(2):
                            ins = mm(bank[4 + step % 2][0:NOPE, 0:T], uk[:, c, step * NOPE:step * NOPE + NOPE], ckvT[:, c, :],
                                     start=c == 0, stop=c == 1)
                        ins.then_inc(kn_ready.s, 1)
                    if step >= 2:
                        head_sum(HM + step - 2, bank[6 + step % 2])
                pe.wait_ge(kn_copied.s, kn_copied.at(l, HM))
                for c in range(2):
                    for k in range(2):
                        ins = mm(bank[4 + c][:, :], ckvT[:, k, c * P:c * P + P], uv[:, k, :], start=k == 0, stop=k == 1)
                ins.then_inc(vm_ready.s, 1)
                pe.wait_ge(hn_root.s, hn_root.at(l, 2 * HM))
                pe.wait_ge(qs_ready.s, qs_ready.at(l, 1))
                mm(bank[6][:, 0:HM * NB], ones[0:QK, :], et[0:QK, 0, 0:HM * NB], start=True, stop=True).then_inc(own_sum.s, 1)
                pe.wait_ge(qs_ready.s, qs_ready.at(l, 2))
                pe.wait_ge(ukt_loaded.s, ukt_loaded.at(l, DMA))
                for hd in range(HM):
                    for c in range(2):
                        o = (c * HM + hd) * NB
                        ins = mm(bank[7][:, o:o + NB], uk_t[0:NOPE, hd, c * P:c * P + P], et[0:NOPE, 1, hd * NB:hd * NB + NB],
                                 start=True, stop=True)
                ins.then_inc(qt_ready.s, 1)

                def att_scores(hd):
                    b = bank[4 + hd % 2]
                    if hd >= 2:
                        pe.wait_ge(at_m.s, at_m.at(l, hd - 1))
                    mm(b[:, 0:P], qm[0:QK, hd, 0:P], km[0:QK, hd, 0:P], start=True, stop=True)
                    mm(b[:, P:3 * P], qm[0:QK, hd, P:TP], km[0:QK, hd, 0:TP], start=True, stop=True).then_inc(at_s.s, 1)

                pe.wait_ge(vm_copied.s, vm_copied.at(l, 1))
                pe.wait_ge(hn_done.s, hn_done.at(l, 2 * HM))
                att_scores(0)
                att_scores(1)
                pe.wait_ge(own_copied.s, own_copied.at(l, 1))
                pe.wait_ge(qt_low.s, qt_low.at(l, 1))
                for hd in range(HM + 1):
                    if hd + 2 < HM:
                        att_scores(hd + 2)
                    if hd < HM:
                        pe.wait_ge(at_n.s, at_n.at(l, hd + 1))
                        if hd:
                            pe.wait_ge(at_tc.s, at_tc.at(l, hd))
                        for c in range(3):
                            ins = pe.transpose(bank[6][:, c * P:c * P + P], ap_s[hd % 3][:, c * P:c * P + P], ident)
                        ins.then_inc(at_t.s, 1)
                    if hd:
                        e = hd - 1
                        pe.wait_ge(at_tc.s, at_tc.at(l, e + 1))
                        if e:
                            pe.wait_ge(at_oc.s, at_oc.at(l, e))
                        r = slice(e % 2 * VD, e % 2 * VD + VD)
                        mm(bank[7][r, 0:TP], vm[:, 0, e * VD:e * VD + VD], ap_t[e % 2][:, 0:TP], start=True, stop=False)
                        mm(bank[7][r, P:TP], vm[:, 1, e * VD:e * VD + VD], ap_t[e % 2][:, TP:TP + P], start=False, stop=True)\
                            .then_inc(at_o.s, 1)

                def rope_turn(b):
                    pe.wait_ge(c_kst.s, c_kst.at(l, b + 1))
                    if not isinstance(b, int) or b:
                        pe.wait_ge(c_pec.s, c_pec.at(l, b))
                    for g in range(4):
                        ins = pe.transpose(bank[6][:, g * P:g * P + P], kpe_n[:, 4 * g:4 * g + 4, :].rearrange("p t r -> p (t r)"), ident)
                    ins.then_inc(c_kt.s, 1)

                def rope_scores(b, i):
                    pe.wait_ge(c_ktc.s, c_ktc.at(l, b + 1))
                    for g in range(4):
                        ins = mm(bank[6][:, i * P + g * 32:i * P + g * 32 + 32], kpeT[:, g, :], q_pe[i][:, :, :].rearrange("p r h -> p (r h)"),
                                 start=True, stop=True)
                    ins.then_inc(c_pe.s, 1)

                def turn_pair(b, i, tp, turn):
                    if turn is not None:
                        ck = ck_loaded[i]
                        pe.wait_ge(ck.s, ck.at(l, (turn + 1) * (DMA * NT)))
                    if not (isinstance(b, int) and b * 8 + tp < 2):
                        pe.wait_ge(c_lo.s, c_lo.at(l, b * 8 + (tp - 1)))
                    for u in range(2):
                        for c in range(2):
                            q = 2 * u + c
                            ins = pe.transpose(bank[4 + tp % 2][:, q * P:q * P + P], cache[i][:, 2 * tp + u, c * P:c * P + P], ident)
                    ins.then_inc(c_tr.s, 1)

                def front(b, i, tail, follows):
                    pe.wait_ge(c_q.s, c_q.at(l, b + 1))
                    for tp in range(NT // 2):
                        if tp < NT // 2 - 1:
                            turn_pair(b, i, tp + 1, None)
                        elif follows is not None:
                            turn_pair(b + 1, (i + 1) % 3, 0, follows)
                            rope_scores(b + 1, (i + 1) % 3)
                        pe.wait_ge(c_lo.s, c_lo.at(l, b * 8 + (tp + 1)))
                        for u in range(2):
                            t = 2 * tp + u
                            if tail is not None or t >= 2:
                                pe.wait_ge(c_sq.s, c_sq.at(l, b * NT + (t - 1)))
                                pe.wait_ge(c_sr.s, c_sr.at(l, b * NT + (t - 1)))
                            for half, cols in enumerate((UKA, UKB)):
                                for c in range(2):
                                    q = 2 * u + c
                                    _, ins = three(bank[2 * u + half][:, 0:cols.stop - cols.start], (ct_hi[tp % 2][:, q, :], ct_lo[tp % 2][:, q, :]),
                                                   (uk_hi[:, c, cols], uk_lo[:, c, cols]), c == 0, c == 1)
                            ins.then_inc(c_kn.s, 1)
                        if tail is not None and tp in (2, 4, 6, 7):
                            tail_step(tail, (2, 4, 6, 7).index(tp))
                        if tp == 5 and follows is not None:
                            rope_turn(b + 1)

                def tail_step(tail, step):
                    b, i = tail[0], tail[1]
                    if step == 0:
                        pe.wait_ge(t_mx.s, t_mx.at(l, b + 1))
                        pe.transpose(bank[7][0:HM, KVL:KVL + P], small[:, 0:8], ident).then_inc(t_mt.s, 1)
                    elif step == 1:
                        pe.wait_ge(t_dg.s, t_dg.at(l, b + 1))
                        mm(bank[7][:, 392:392 + HM], ones[0:HM, :], small[0:HM, 16:24], start=True, stop=True).then_inc(t_bc.s, 1)
                    elif step == 2:
                        pe.wait_ge(t_p.s, t_p.at(l, b + 1))
                        for t in range(NT):
                            mm(bank[7][0:HM, 0:KVL], pr[:, t, :], cache[i][:, t, 0:KVL], start=t == 0, stop=t == NT - 1)
                        pe.wait_ge(t_l.s, t_l.at(l, b + 1))
                        mm(bank[7][:, 400:400 + HM], ones, small[:, 48:56], start=True, stop=True).then_inc(t_lat.s, 1)
                    else:
                        pe.wait_ge(t_cp.s, t_cp.at(l, b + 1))
                        for c in range(2):
                            ins = mm(bank[7][:, 408 + c * HM:416 + c * HM], latn[0:HM, c * P:c * P + P], ident[0:HM, 0:HM], start=True, stop=True)
                        ins.then_inc(t_tr.s, 1)

                pe.wait_ge(chunk_free.s, chunk_free.at(l, C0["gate_c"]))
                pe.wait_ge(at_tc.s, at_tc.at(l, HM))
                pe.wait_ge(at_oc.s, at_oc.at(l, HM))
                pe.wait_ge(uk_low.s, uk_low.at(l, 1))
                rope_turn(0)
                turn_pair(0, 0, 0, 0)
                rope_scores(0, 0)
                front(0, 0, None, 0)
                with pe.Fori(0, 2) as j:
                    for u in range(3):
                        front(j * 3 + (u + 1), (u + 1) % 3, (j * 3 + u, u), j + (u + 2) // 3)
                front(NB - 1, 1, (NB - 2, 0), None)
                for step in range(4):
                    tail_step((NB - 1, 1), step)

                pe.wait_ge(t_fin.s, t_fin.at(l, NB))
                for hd in range(HM):
                    r = slice(hd % 2 * VD, hd % 2 * VD + VD)
                    o = hd // 2 * NB
                    for c in range(2):
                        ins = mm(bank[4][r, o:o + NB], uv[:, c, hd * VD:hd * VD + VD], lat[:, c, hd, :], start=c == 0, stop=c == 1)
                ins.then_inc(uvs_ready.s, 1)

                with pe.Fori(0, 2) as i:
                    group("gate_c", i, h)
                pe.wait_ge(mla_split.s, mla_split.at(l, 1))
                for m in range(KT):
                    stream_chunk("mla_out", m, 4, (s_hi[:, 4:8, :], s_lo[:, 4:8, :]))
                with pe.Fori(0, 2) as i:
                    group("w_out", i, s_, lambda k: pe.wait_ge(mix_low.s, mix_low.at(l, k + 1)))

                token_sums(1)
                with pe.Fori(0, 2 * FT // 4) as i:
                    group("ffn_in", i, h, h_there(1))
                for m in range(KT):
                    stream_chunk("ffn_out", m, FT, (a_hi, a_lo), (lambda k: pe.wait_ge(ffn_low.s, ffn_low.at(l, k + 1))) if m == 0 else None)

                token_sums(2)
                with pe.Fori(0, 2) as i:
                    group("ple_gate", i, h, h_there(2))
                pe.wait_ge(p_low.s, p_low.at(l, 1))
                for m in range(KT):
                    stream_chunk("ple_proj", m, 2, (p_hi, p_lo))

        @block.scalar
        def _(act):
            A = act.activation

            def copy(out, in_, **kw):
                return A(out, in_, ACT.Copy, **kw)

            asteps = Steps()

            def asteps_restart():
                if asteps.n:
                    act.wait_ge(act_step.s, asteps.n)
                    act.sem_clear(act_step.s)
                    asteps.n = 0

            def sigmoid(out, tmp, z):
                A(tmp, z, ACT.Exp, scale=-1.0).then_inc(act_step.s, asteps.one())
                act.wait_ge(act_step.s, asteps.n)
                A(tmp, tmp, ACT.Ln, bias=1.0).then_inc(act_step.s, asteps.one())
                act.wait_ge(act_step.s, asteps.n)
                return A(out, tmp, ACT.Exp, scale=-1.0)

            def rsqrt_mean(out, total, width):
                A(out, total, ACT.Ln, scale=1.0 / width, bias=EPS).then_inc(act_step.s, asteps.one())
                act.wait_ge(act_step.s, asteps.n)
                return A(out, out, ACT.Exp, scale=-0.5)

            act.preload_act_table_set("natural_log_exp_and_others")
            act.sem_inc(v_copied.s, 1)
            act.wait_ge(x_loaded.s, 2 * DMA)
            act.wait_ge(consts_loaded.s, 2 * DMA)
            act.wait_ge(chunk_free.s, 4)
            with act.Fori(0, DEPTH) as l:
                def cut(j, n_static):
                    r = n_static % RING
                    if n_static >= RING:
                        act.wait_ge(w_begun.s, w_begun.at(l, j * RING + (n_static - RING + 2)))
                    ld = w_loaded[r]
                    act.wait_ge(ld.s, ld.at(l, j * DMA + (n_static // RING + 1) * DMA))
                    copy(w_hi[r][:, :], w_raw[r][:, :]).then_inc(w_high.s, 1)

                def split_x(w, gain, there):
                    for k in range(KT):
                        there(k)
                        copy(h_hi[:, k, :], xT[:, k, :], scale=col(gain, k)).then_inc(h_high.s, 1)
                        A((et if k < 4 else zt)[:, k % 4, :], xT[:, k, :], ACT.Square).then_inc(x_sq.s, 1)
                    act.wait_ge(x_sum.s, x_sum.at(l, (w + 1) * KT))
                    rsqrt_mean(rstd[:, :], bank[4][:, 0:T], D).then_inc(x_root.s, 1)

                def exps(stage, i, slots):
                    for r in slots:
                        cut(i, B0[stage] + r + 3)
                        act.wait_ge(chunk_free.s, chunk_free.at(l, i * 4 + (C0[stage] + r + 1)))
                        out = gate[:, ds(i * 4 + r, 1), :].rearrange("p o t -> p (o t)") if stage in GATES else et[:, r, :]
                        sigmoid(out, et[:, r, :], zt[:, r, :]).then_inc(exp_ready.s, 1)

                act.wait_ge(vec_ready.s, vec_ready.at(l, 1))
                act.wait_ge(chunk_free.s, chunk_free.at(l, 0))
                split_x(0, "g_mix", lambda k: cut(0, k) if k < 3 else None)
                act.wait_ge(conv_state_loaded.s, conv_state_loaded.at(l, DMA))
                copy(u_smp[:, :, :, 0:30], conv_stage[:, :, :, :]).then_inc(conv_state_placed.s, 1)
                for c in range(CT):
                    ins = A(yconv[:, c, :], tb("ident", T), ACT.Identity, scale=0.0, bias=col("b_dw", c))
                ins.then_inc(conv_biased.s, 1)
                asteps_restart()
                with act.Fori(0, 2) as i:
                    for r in (1, 3):
                        cut(i, B0["glu"] + r + 2)
                        exps("glu", i, (r,))
                    asteps_restart()
                act.wait_ge(u_ready.s, u_ready.at(l, 1))
                copy(conv_new[:, :, :, :], u_smp[:, :, :, 1:31]).then_inc(conv_new_ready.s, 1)
                act.wait_ge(conv_new_ready.s, conv_new_ready.at(l, 1))
                act.dma_start(conv_sample_out[ds(l, 1)].rearrange("o p c b w -> (o p) c b w"), conv_new[:, :, :, :]).then_inc(conv_stored.s, DMA)
                act.dma_start(conv_prompt_out[ds(l, 1)].rearrange("o p c w -> (o p) c w"), u_ext[:, :, TP:TP + 30]).then_inc(conv_stored.s, DMA)

                with act.Fori(0, 2) as i:
                    for r in range(4):
                        cut(i, B0["qk"] + r + 3)

                with act.Fori(0, 2) as i:
                    for r in range(4):
                        cut(i, B0["v"] + r + 3)
                    act.wait_ge(v_turned.s, v_turned.at(l, i + 1))
                    for c in range(2):
                        copy(v_nat[:, c, ds(i * 512, 512)], bank[4 + c][:, :])
                    copy(v_smp[0:NB, ds(i * 512, 512)], bank[6][0:NB, :]).then_inc(v_copied.s, 1)
                act.wait_ge(k_turned.s, k_turned.at(l, 1))
                for hd in range(HR):
                    for c in range(2):
                        copy(k_nat[:, c, hd * P:hd * P + P], bank[4 + c][:, hd * P:hd * P + P], scale=tb("kdec", 1, c * HR + hd))
                copy(k_smp[0:NB, :], bank[6][0:NB, :]).then_inc(k_copied.s, 1)
                asteps_restart()
                with act.Fori(0, 2) as i:
                    exps("rg", i, range(4))
                    asteps_restart()

                asteps_restart()
                with act.Fori(0, 2) as i:
                    exps("gate_a", i, range(4))
                    asteps_restart()


                act.wait_ge(exp_ready.s, exp_ready.at(l, E0["gate_a"] + KT))
                act.wait_ge(cln_centred.s, cln_centred.at(l, 1))
                A(et[:, :, :], yconv[:, :, :], ACT.Square).then_inc(cln_sq.s, 1)
                act.wait_ge(cln_sum.s, cln_sum.at(l, 2))
                rsqrt_mean(rsb[:, 0, :], bank[1][:, 0:T], CONV).then_inc(cln_root.s, 1)

                def ret_out(hd):
                    act.wait_ge(ret_o.s, ret_o.at(l, hd + 1))
                    copy(oT[:, 2 * hd:2 * hd + 2, 0:TP], bank[6][:, :].rearrange("p (e t) -> p e t", e=2)).then_inc(ret_oc.s, 1)
                    act.wait_ge(ret_st.s, ret_st.at(l, hd + 1))
                    copy(ret_stage[:, hd, :], bank[7][:, 0:DV]).then_inc(ret_stc.s, 1)

                act.wait_ge(conv_stored.s, conv_stored.at(l, 32))
                ret_out(0)
                act.wait_ge(cln_y.s, cln_y.at(l, 1))
                sigmoid(et[:, :, :], et[:, :, :], yconv[:, :, :]).then_inc(cln_exp.s, 1)
                ret_out(1)
                ret_out(2)
                act.wait_ge(conv_act.s, conv_act.at(l, 1))
                copy(cv_hi[:, 0:CT, :], yconv[:, :, :]).then_inc(conv_high.s, 1)
                ret_out(3)
                act.wait_ge(ret_stc.s, ret_stc.at(l, HR))
                act.dma_start(ret_prompt_out[ds(l, 1)].rearrange("o h d e -> d (o h) e"), ret_stage[:, :, :]).then_inc(ret_stored.s, DMA)

                act.wait_ge(st_o.s, st_o.at(l, NB))
                for hd in range(HR):
                    ins = copy(o_row[0:NB, hd * DV:hd * DV + DV], bank[O_BANK[hd]][0:NB, 0:DV])
                ins.then_inc(st_row.s, 1)
                for n in range(B0["conv_out"], B0["gate_b"]):
                    cut(0, n + 3)

                def gn_square(hd):
                    act.wait_ge(gn_c.s, gn_c.at(l, hd + 1))
                    if hd >= 2:
                        act.wait_ge(gn_var.s, gn_var.at(l, hd - 1))
                    e = 2 * (hd % 2)
                    A(et[:, e:e + 2, :], oT[:, 2 * hd:2 * hd + 2, :], ACT.Square).then_inc(gn_sq.s, 1)

                def gn_rt(hd):
                    act.wait_ge(gn_var.s, gn_var.at(l, hd + 1))
                    if hd >= 2:
                        act.wait_ge(gn_y.s, gn_y.at(l, hd - 1))
                    rsqrt_mean(rsb[:, hd % 2, :], bank[4 + hd][:, 0:T], DV).then_inc(gn_root.s, 1)

                def gn_hi(hd):
                    act.wait_ge(gn_y.s, gn_y.at(l, hd + 1))
                    copy(s_hi[:, 2 * hd:2 * hd + 2, :], oT[:, 2 * hd:2 * hd + 2, :]).then_inc(gn_high.s, 1)

                gn_square(0)
                gn_square(1)
                gn_rt(0)
                gn_square(2)
                gn_rt(1)
                gn_hi(0)
                gn_square(3)
                gn_rt(2)
                gn_hi(1)
                gn_rt(3)
                for i in (2, 3):
                    act.wait_ge(st_stored[i].s, st_stored[i].at(l, 2 * DMA))
                gn_hi(2)
                gn_hi(3)
                asteps_restart()
                with act.Fori(0, 2) as i:
                    exps("gate_b", i, range(4))
                    asteps_restart()


                with act.Fori(0, 2) as i:
                    for r in range(4):
                        cut(i, B0["ret_out"] + r + 3)

                for m in range(5):
                    cut(0, B0["kvq"] + m + 3)
                    act.wait_ge(chunk_free.s, chunk_free.at(l, C0["kvq"] + m + 1))
                    z = zt[:, (0, 1, 2, 3, 0)[m], :]
                    ins = A(sqg[:, m, :], z, ACT.Square)
                    if m < 3:
                        ins = copy(qa_hi[:, m, :], z, scale=col("g_qa", m))
                    ins.then_inc(kvq_act.s, 1)
                cut(0, B0["kvq"] + 5 + 3)
                for n, width in enumerate((QL, KVL)):
                    act.wait_ge(kvq_sum.s, kvq_sum.at(l, n + 1))
                    rsqrt_mean(rsb[:, n, :], bank[4 + n][:, 0:T], width).then_inc(kvq_root.s, 1)

                def head_square(k, buf):
                    if k >= 4:
                        act.wait_ge(hn_done.s, hn_done.at(l, k - 3))
                    A(et[0:QK, k % 4, :], buf, ACT.Square).then_inc(hn_sq.s, 1)

                def head_root(k):
                    act.wait_ge(hn_sum.s, hn_sum.at(l, k + 1))
                    rsqrt_mean(et[0:QK, k % 4, :], bank[6 + k % 2][0:QK, 0:T], QK).then_inc(hn_root.s, 1)

                for step in range(HM + 2):
                    if step in (0, 3, 6):
                        cut(0, B0["uq"] + step // 3 + 3)
                    if step < HM:
                        act.wait_ge(q_roped.s, q_roped.at(l, step + 1))
                        head_square(step, qm[0:QK, step, :])
                    if step >= 2:
                        head_root(step - 2)
                act.wait_ge(ckv_ready.s, ckv_ready.at(l, 1))
                act.dma_start(ckv_out[ds(l, 1)].rearrange("o p c t -> (o p) c t"), ckvT[:, :, :]).then_inc(own_stored.s, DMA)
                act.dma_start(kpe_out[ds(l, 1)].rearrange("o p t -> (o p) t"), kpe_own[NOPE:QK, :]).then_inc(own_stored.s, DMA)
                for step in range(HM + 2):
                    if step < HM:
                        copy(km[NOPE:QK, step, :], kpe_own[NOPE:QK, :])
                        act.wait_ge(kn_ready.s, kn_ready.at(l, step + 1))
                        copy(km[0:NOPE, step, :], bank[4 + step % 2][0:NOPE, 0:T]).then_inc(kn_copied.s, 1)
                        act.wait_ge(kn_copied.s, kn_copied.at(l, step + 1))
                        head_square(HM + step, km[0:QK, step, :])
                    if step >= 2:
                        head_root(HM + step - 2)
                act.wait_ge(vm_ready.s, vm_ready.at(l, 1))
                for c in range(2):
                    ins = copy(vm[:, c, :], bank[4 + c][:, :])
                ins.then_inc(vm_copied.s, 1)
                act.wait_ge(own_sum.s, own_sum.at(l, 1))
                copy(own[:, :, :].rearrange("p b h -> p (b h)"), bank[6][:, 0:HM * NB]).then_inc(own_copied.s, 1)
                act.wait_ge(qt_ready.s, qt_ready.at(l, 1))
                for c in range(2):
                    ins = copy(qt_hi[:, :, c, :], bank[7][:, c * 64:c * 64 + 64].rearrange("p (h b) -> p b h", h=HM))
                ins.then_inc(qt_high.s, 1)

                def att_exp(hd):
                    i = hd % 3
                    act.wait_ge(at_m.s, at_m.at(l, hd + 1))
                    A(ap_s[i][:, 0:P], ap_s[i][:, 0:P], ACT.Exp, scale=ATT_SCALE, bias=small[:, 4 + 2 * i:5 + 2 * i],
                      accum_out=small[:, 12 + 2 * i:13 + 2 * i])
                    A(ap_s[i][:, P:3 * P], ap_s[i][:, P:3 * P], ACT.Exp, scale=ATT_SCALE, bias=small[:, 5 + 2 * i:6 + 2 * i],
                      accum_out=small[:, 13 + 2 * i:14 + 2 * i]).then_inc(at_p.s, 1)

                att_exp(0)
                att_exp(1)
                for hd in range(HM + 1):
                    if hd + 2 < HM:
                        att_exp(hd + 2)
                    if hd < HM:
                        act.wait_ge(at_t.s, at_t.at(l, hd + 1))
                        if hd >= 2:
                            act.wait_ge(at_o.s, at_o.at(l, hd - 1))
                        copy(ap_t[hd % 2][:, :], bank[6][:, 0:3 * P]).then_inc(at_tc.s, 1)
                    if hd:
                        e = hd - 1
                        act.wait_ge(at_o.s, at_o.at(l, e + 1))
                        r = slice(e % 2 * VD, e % 2 * VD + VD)
                        copy(oM[r, e // 2, 0:TP], bank[7][r, 0:TP]).then_inc(at_oc.s, 1)
                act.wait_ge(own_stored.s, own_stored.at(l, 32))
                copy(uk_hi[:, :, 0:256], uk[:, :, 0:256])
                copy(uk_hi[:, :, UKB], uk[:, :, 256:512]).then_inc(uk_high.s, 1)

                def gather_rope(b, i, turn):
                    ck = ck_loaded[i]
                    act.wait_ge(ck.s, ck.at(l, (turn + 1) * (DMA * NT)))
                    if not isinstance(b, int) or b:
                        act.wait_ge(c_ksq.s, c_ksq.at(l, b))
                    for r in range(4):
                        rows = slice(r * ROPE, r * ROPE + ROPE)
                        copy(q_pe[i][rows, r, :], qpe4[rows, ds(b, 1), :].rearrange("p o h -> p (o h)"))
                    copy(kpe_n[:, :, :], cache[i][:, :, KVL:KV]).then_inc(c_kst.s, 1)

                def next_q(b):
                    copy(uk_hi[:, :, 256:256 + HM], qt_hi[:, ds(b, 1)].rearrange("p o c h -> p (o c) h").bitcast(F32))
                    copy(uk_lo[:, :, 256:256 + HM], qt_lo[:, ds(b, 1)].rearrange("p o c h -> p (o c) h").bitcast(F32)).then_inc(c_q.s, 1)

                def rope_copy(b):
                    act.wait_ge(c_kt.s, c_kt.at(l, b + 1))
                    copy(kpeT[:, :, :], bank[6][:, :].rearrange("p (g k) -> p g k", g=4)).then_inc(c_ktc.s, 1)

                def high(b, tp):
                    act.wait_ge(c_tr.s, c_tr.at(l, b * 8 + (tp + 1)))
                    copy(ct_hi[tp % 2][:, :, :], bank[4 + tp % 2][:, :].rearrange("p (q k) -> p q k", q=4)).then_inc(c_hi.s, 1)

                def front(b, i, tail, follows):
                    if tail is not None:
                        act.wait_ge(c_ss.s, c_ss.at(l, b * NT - 1))
                    act.wait_ge(c_kst.s, c_kst.at(l, b + 1))
                    A(sq[0][:, :, :].rearrange("p h n -> p (h n)"), kpe_n[:, :, :].rearrange("p t r -> p (t r)"), ACT.Square).then_inc(c_ksq.s, 1)
                    for tp in range(NT // 2):
                        if tp < NT // 2 - 1:
                            high(b, tp + 1)
                        elif follows is not None:
                            high(b + 1, 0)
                        for u in range(2):
                            t = 2 * tp + u
                            act.wait_ge(c_kn.s, c_kn.at(l, b * NT + (t + 1)))
                            if t == 0:
                                act.wait_ge(c_kss.s, c_kss.at(l, b + 1))
                            elif t >= 2 or tail is not None:
                                act.wait_ge(c_ss.s, c_ss.at(l, b * NT + (t - 1)))
                            if t == NT - 1 and follows is not None:
                                next_q(b + 1)
                            for half in range(2):
                                ins = A(sq[u][:, 4 * half:4 * half + 4, :], bank[2 * u + half][:, 0:256].rearrange("p (h n) -> p h n", h=4), ACT.Square)
                            ins.then_inc(c_sq.s, 1)
                            copy(scores[i][:, t, :], bank[2 * u][:, 256:256 + HM]).then_inc(c_sr.s, 1)
                        if tp == 4 and follows is not None:
                            gather_rope(b + 1, (i + 1) % 3, follows)
                        if tp == 6 and follows is not None:
                            rope_copy(b + 1)
                        if tail is not None and tp == 0:
                            tail_root(tail)
                        if tail is not None and tp == 5:
                            tail_exp(tail)
                        if tail is not None and tp == 6:
                            tail_copy(tail)

                def tail_root(b):
                    act.wait_ge(t_tot.s, t_tot.at(l, b + 1))
                    rsqrt_mean(kn_r[:, :, :], kn_r[:, :, :], QK).then_inc(t_root.s, 1)

                def tail_copy(b):
                    act.wait_ge(t_lat.s, t_lat.at(l, b + 1))
                    copy(latn[0:HM, :], bank[7][0:HM, 0:KVL]).then_inc(t_cp.s, 1)

                def tail_exp(b):
                    act.wait_ge(t_shift.s, t_shift.at(l, b + 1))
                    A(pr[:, :, :], sc[:, :, :], ACT.Exp, scale=ATT_SCALE)
                    A(small[:, 40:48], small[:, 32:40], ACT.Exp, scale=ATT_SCALE).then_inc(t_p.s, 1)

                act.wait_ge(qt_low.s, qt_low.at(l, 1))
                gather_rope(0, 0, 0)
                next_q(0)
                rope_copy(0)
                high(0, 0)
                front(0, 0, None, 0)
                asteps_restart()
                with act.Fori(0, 2) as j:
                    for u in range(3):
                        front(j * 3 + (u + 1), (u + 1) % 3, j * 3 + u, j + (u + 2) // 3)
                    asteps_restart()
                front(NB - 1, 1, NB - 2, None)
                tail_root(NB - 1)
                tail_exp(NB - 1)
                tail_copy(NB - 1)

                act.wait_ge(uvs_ready.s, uvs_ready.at(l, 1))
                copy(oM[:, :, TP:T], bank[4][:, 0:4 * NB].rearrange("p (q b) -> p q b", q=4)).then_inc(uvs_copied.s, 1)
                act.wait_ge(uvs_copied.s, uvs_copied.at(l, 1))
                copy(s_hi[:, 4:8, :], oM[:, :, :]).then_inc(mla_high.s, 1)
                asteps_restart()
                with act.Fori(0, 2) as i:
                    exps("gate_c", i, range(4))
                    asteps_restart()

                for k in range(KT):
                    if k % 2 == 0:
                        cut(0, B0["mla_out"] + k // 2 + 3)
                    act.wait_ge(mix_done.s, mix_done.at(l, k + 1 if k < 4 else KT))
                    copy(s_hi[:, k, :], mix[:, k, :]).then_inc(mix_high.s, 1)

                def out_there(k):
                    cut(0, B0["w_out"] + k + 3)
                    act.wait_ge(chunk_free.s, chunk_free.at(l, C0["w_out"] + k + 1))

                split_x(1, "g_ffn", out_there)
                asteps_restart()
                with act.Fori(0, 2 * FT // 4) as i:
                    exps("ffn_in", i, (0,))
                    for u in range(2):
                        cut(i, B0["ffn_in"] + 2 * u + 1 + 3)
                        act.wait_ge(ffn_a.s, ffn_a.at(l, i * 2 + (u + 1)))
                        copy(a_hi[:, ds(i * 2 + u, 1), :].rearrange("p o t -> p (o t)"), zt[:, 2 * u, :]).then_inc(ffn_high.s, 1)
                        if u == 0:
                            exps("ffn_in", i, (2,))
                    asteps_restart()
                def down_there(m):
                    for n in range(-(-m * FT // 8), -(-(m + 1) * FT // 8)):
                        cut(0, B0["ffn_out"] + n + 3)
                    act.wait_ge(chunk_free.s, chunk_free.at(l, C0["ffn_out"] + m + 1))

                split_x(2, "g_ple", down_there)
                act.wait_ge(p_loaded.s, p_loaded.at(l, DMA))
                copy(p_hi[:, :, :], p_raw[:, :, :]).then_inc(p_high.s, 1)
                for r in range(KT):
                    n = B0["ple_gate"] + r + 3
                    if n < NBLK:
                        cut(0, n)
                    act.wait_ge(chunk_free.s, chunk_free.at(l, C0["ple_gate"] + r + 1))
                    sigmoid(gate[:, r, :], et[:, r % 4, :], zt[:, r % 4, :]).then_inc(exp_ready.s, 1)
                asteps_restart()

        @block.vector
        def _(v):
            steps = Steps()

            tap_done = {}

            def steps_restart():
                tap_done.clear()
                if steps.n:
                    v.wait_ge(dve_step.s, steps.n)
                    v.sem_clear(dve_step.s)
                    steps.n = 0

            tt, stt = v.tensor_tensor, v.scalar_tensor_tensor

            def flat(ap):
                return ap.rearrange("p o t -> p (o t)")

            v.wait_ge(x_loaded.s, 2 * DMA)
            v.wait_ge(consts_loaded.s, 2 * DMA)
            v.sem_inc(chunk_free.s, 3)
            for i in range(3):
                ins = v.memset(q_pe[i][:, :, :], 0.0)
            ins.then_inc(chunk_free.s, 1)
            with v.Fori(0, DEPTH) as l:
                def split_x(w, gain):
                    for k in range(KT):
                        v.wait_ge(h_high.s, h_high.at(l, w * KT + k + 1))
                        stt(h_lo[:, k, :], xT[:, k, :], col(gain, k), h_hi[:, k, :].bitcast(F32), ALU.mult, ALU.subtract)\
                            .then_inc(h_low.s, 1)
                    v.wait_ge(x_root.s, x_root.at(l, w + 1))


                def take(stage, i, r, out=None, rows=P, rs=rstd[:, :], s=None):
                    c = C0[stage] + r
                    v.wait_ge(chunk_ready.s, chunk_ready.at(l, i * 4 + (c + 1)))
                    out = zt[:, r % 4, :] if out is None else out
                    tt(out, bank[c % 4][0:rows, 0:T], rs[0:rows, :], ALU.mult).then_inc(chunk_free.s, 1)

                def taken(stage, i, r):
                    v.wait_ge(chunk_free.s, chunk_free.at(l, i * 4 + (C0[stage] + r + 1)))

                def sigmoid_there(n):
                    v.wait_ge(exp_ready.s, exp_ready.at(l, n + 1))

                def taps(i, r, *runs):
                    for j in range(max(n for _, _, n in runs)):
                        for ct, first, n in runs:
                            if j < n:
                                w = first + n * r + j
                                if tap_done.get(ct):
                                    v.wait_ge(dve_step.s, tap_done[ct])
                                stt(yconv[:, ct, 0:TP], u_ext[:, ct, ds(i * (4 * n) + w, TP)],
                                    vec[:, ds(i * (4 * n) + (VEC["w_dw"] + ct * 32 + w), 1)], yconv[:, ct, 0:TP], ALU.mult, ALU.add)\
                                    .then_inc(dve_step.s, steps.one())
                                tap_done[ct] = steps.n

                def gates(stage, runs=()):
                    with v.Fori(0, 2) as i:
                        for r in range(4):
                            sigmoid_there(i * 4 + (E0[stage] + r - 4))
                            take(stage, i, r)
                            if runs:
                                taps(i, r, *runs)
                        steps_restart()

                def gated_sum(stage, done=None, first=False):
                    with v.Fori(0, 2) as i:
                        for r in range(4):
                            c = C0[stage] + r
                            m = i * 4 + r
                            v.wait_ge(chunk_ready.s, chunk_ready.at(l, i * 4 + (c + 1)))
                            g, x = flat(gate[:, ds(m, 1), :]), flat(mix[:, ds(m, 1), :])
                            sigmoid_there(E0[GATE_OF[stage]] + KT - 1)
                            if first:
                                tt(x, bank[c % 4][:, 0:T], g, ALU.mult).then_inc(chunk_free.s, 1)
                                continue
                            tt(zt[:, r, :], bank[c % 4][:, 0:T], g, ALU.mult).then_inc(chunk_free.s, 1)
                            taken(stage, i, r)
                            ins = tt(x, x, zt[:, r, :], ALU.add)
                            if done is not None:
                                ins.then_inc(done.s, 1)
                            else:
                                ins.then_inc(dve_step.s, steps.one())
                        steps_restart()

                def add_to_x(stage):
                    with v.Fori(0, 2) as i:
                        for r in range(4):
                            c = C0[stage] + r
                            x = flat(xT[:, ds(i * 4 + r, 1), :])
                            v.wait_ge(chunk_ready.s, chunk_ready.at(l, i * 4 + (c + 1)))
                            tt(x, bank[c % 4][:, 0:T], x, ALU.add).then_inc(chunk_free.s, 1)

                v.tensor_copy(vec[:, :], flat(vecs[:, ds(l, 1), :])).then_inc(vec_ready.s, 1)
                v.wait_ge(vec_ready.s, vec_ready.at(l, 1))
                split_x(0, "g_mix")
                v.memset(u_ext[:, :, 0:30], 0.0).then_inc(dve_step.s, steps.one())
                v.memset(u_ext[:, :, 30 + TP:288], 0.0).then_inc(dve_step.s, steps.one())
                steps_restart()
                with v.Fori(0, 2) as i:
                    for r in range(4):
                        take("glu", i, r)
                        if r % 2:
                            sigmoid_there(i * 2 + r // 2)
                            taken("glu", i, r - 1)
                            m = i * 2 + r // 2
                            tt(flat(u_ext[:, ds(m, 1), 30:30 + TP]), zt[:, r - 1, 0:TP], et[:, r, 0:TP], ALU.mult).then_inc(dve_step.s, steps.one())
                            tt(u_smp[:, ds(m, 1), :, 30:31].rearrange("p o b w -> p (o b w)"), zt[:, r - 1, TP:T], et[:, r, TP:T], ALU.mult).then_inc(dve_step.s, steps.one())
                    steps_restart()
                v.wait_ge(conv_state_placed.s, conv_state_placed.at(l, 1))
                v.wait_ge(conv_biased.s, conv_biased.at(l, 1))
                taps_w = vec[:, VEC["w_dw"]:VEC["w_dw"] + CT * 32].rearrange("p (c w) -> p c w", c=CT)[:, :, 0:31]
                tt(conv_prod[:, :, :, :], u_smp[:, :, :, :], taps_w.unsqueeze(2).broadcast_to([P, CT, NB, 31]), ALU.mult)\
                    .then_inc(u_ready.s, 1)
                v.wait_ge(u_ready.s, u_ready.at(l, 1))
                v.tensor_reduce(small[:, 0:CT * NB], conv_prod[:, :, :, :].rearrange("p c b w -> p (c b) w"), AX.X, ALU.add).then_inc(dve_step.s, steps.one())
                v.wait_ge(dve_step.s, steps.n)
                steps_restart()

                v.memset(k3[0:72, :].bitcast(F32), 0.0).then_inc(dve_step.s, steps.one())
                v.memset(v3[0:72, :].bitcast(F32), 0.0).then_inc(dve_step.s, steps.one())
                steps_restart()

                v.wait_ge(tables_loaded.s, DMA)
                with v.Fori(0, 2) as i:
                    for r in range(4):
                        take("qk", i, r)
                        taken("qk", i, r)
                        cos = tab[:, ds(i * T + TAB["rope_c"], T)]
                        o = flat(qk[:, ds(i * 4 + r, 1), :])
                        lo, hi = (slice(0, 64), slice(64, P))
                        tt(et[:, r, :], zt[:, r, :], cos, ALU.mult).then_inc(dve_step.s, steps.one())
                        tt(qk[lo, ds(i * 4 + r, 1), :].rearrange("p o t -> p (o t)"), zt[hi, r, :], tab[hi, ds(i * T + TAB["rope_s"], T)], ALU.mult).then_inc(dve_step.s, steps.one())
                        tt(qk[hi, ds(i * 4 + r, 1), :].rearrange("p o t -> p (o t)"), zt[lo, r, :], tab[lo, ds(i * T + TAB["rope_s"], T)], ALU.mult).then_inc(dve_step.s, steps.one())
                        v.wait_ge(dve_step.s, steps.n)
                        ins = tt(o, o, et[:, r, :], ALU.add)
                        if r == 3:
                            ins.then_inc(rope_ready.s, 1)
                        else:
                            ins.then_inc(dve_step.s, steps.one())
                        taps(i, r, (0, 0, 2), (1, 0, 1))
                    steps_restart()
                with v.Fori(0, 2) as i:
                    v.wait_ge(v_copied.s, v_copied.at(l, i))
                    for r in range(4):
                        take("v", i, r)
                        taps(i, r, (0, 16, 2), (1, 8, 3))
                    steps_restart()
                v.wait_ge(k_copied.s, k_copied.at(l, 1))
                for rows in (slice(0, NB), slice(32, 32 + NB)):
                    v.tensor_copy(k3[rows, :], k_smp[0:NB, :]).then_inc(dve_step.s, steps.one())
                for rows in (slice(0, NB), slice(64, 64 + NB)):
                    v.tensor_copy(v3[rows, :], v_smp[0:NB, :]).then_inc(dve_step.s, steps.one())
                v.wait_ge(dve_step.s, steps.n)
                tt(k3[64:64 + NB, :], k_smp[0:NB, :], k3[0:NB, :].bitcast(F32), ALU.subtract).then_inc(dve_step.s, steps.one())
                tt(v3[32:32 + NB, :], v_smp[0:NB, :], v3[0:NB, :].bitcast(F32), ALU.subtract).then_inc(dve_step.s, steps.one())
                tt(q_pick[:, :, :, :], qk[:, 0:HR, TP:T].unsqueeze(1).broadcast_to([P, NB, HR, NB]),
                   tb("pick", NB * NB).rearrange("p (b s) -> p b s", b=NB).unsqueeze(2).broadcast_to([P, NB, HR, NB]), ALU.mult)\
                    .then_inc(dve_step.s, steps.one())
                steps_restart()
                v.wait_ge(conv_stored.s, conv_stored.at(l, 32))
                v.wait_ge(v_copied.s, v_copied.at(l, 2))
                settle(v)
                with v.Fori(0, 2) as i:
                    for r in range(5):
                        if r < 4:
                            take("rg", i, r)
                        if r:
                            q = r - 1
                            sigmoid_there(i * 4 + (E0["rg"] + q))
                            tt(flat(rgs[:, ds(i * 4 + q, 1), :]), zt[:, q, :], et[:, q, :], ALU.mult).then_inc(dve_step.s, steps.one())
                            taps(i, q, (2, 0, 3), (3, 0, 1))
                    steps_restart()
                gates("gate_a", ((3, 8, 3), (2, 24, 1)))
                ys = yconv[:, :, TP:T]
                tt(ys, ys, small[:, 0:CT * NB].rearrange("p (c b) -> p c b", c=CT), ALU.add).then_inc(conv_done.s, 1)

                v.wait_ge(cln_sum.s, cln_sum.at(l, 1))
                for c in range(CT):
                    ins = stt(yconv[:, c, :], bank[0][:, 0:T], -1.0 / CONV, yconv[:, c, :], ALU.mult, ALU.add)
                ins.then_inc(cln_centred.s, 1)
                def ret_decay(hd):
                    v.wait_ge(ret_s.s, ret_s.at(l, hd + 1))
                    tt(sT[hd % 2][:, :], bank[4 + hd % 2][:, 0:384], tb("decay", 384, 384 * hd), ALU.mult).then_inc(ret_sd.s, 1)

                ret_decay(0)
                ret_decay(1)
                v.wait_ge(cln_root.s, cln_root.at(l, 1))
                for c in range(CT):
                    stt(yconv[:, c, :], yconv[:, c, :], col("g_cln", c), rsb[:, 0, :], ALU.mult, ALU.mult).then_inc(dve_step.s, steps.one())
                v.wait_ge(dve_step.s, steps.n)
                for c in range(CT):
                    ins = v.tensor_scalar(yconv[:, c, :], yconv[:, c, :], col("b_cln", c), None, ALU.add)
                ins.then_inc(cln_y.s, 1)
                ret_decay(2)
                ret_decay(3)
                v.wait_ge(cln_exp.s, cln_exp.at(l, 1))
                tt(yconv[:, :, :], yconv[:, :, :], et[:, :, :], ALU.mult).then_inc(conv_act.s, 1)
                v.wait_ge(conv_high.s, conv_high.at(l, 1))
                tt(cv_lo[:, 0:CT, :], yconv[:, :, :], cv_hi[:, 0:CT, :].bitcast(F32), ALU.subtract).then_inc(conv_split.s, 1)

                steps_restart()
                def mask(b):
                    v.tensor_scalar(k_mask[b % 2][0:72, :], k3[0:72, :].bitcast(F32), tb("pick3", 1, b, slice(0, 72)), None, ALU.mult)\
                        .then_inc(st_mask.s, 1)

                mask(0)
                mask(1)
                for b in range(NB):
                    v.wait_ge(st_outer.s, st_outer.at(l, b + 1))
                    sl = st_loaded[b % 4]
                    v.wait_ge(sl.s, sl.at(l, (b // 4 + 1) * DMA))
                    for hd in range(HR):
                        s = state[b % 4][:, hd, :]
                        ins = stt(s, s, GAMMA[hd], bank[(4, 0)[b % 2] + hd // 2][:, hd % 2 * DV:hd % 2 * DV + DV], ALU.mult, ALU.add)
                    ins.then_inc(st_new.s, 1)
                    if b + 2 < NB:
                        mask(b + 2)
                v.wait_ge(st_turned.s, st_turned.at(l, 1))
                v.tensor_copy(oT[:, :, TP:T], bank[4][:, 0:KT * NB].rearrange("p (m b) -> p m b", m=KT)).then_inc(st_oc.s, 1)
                gated_sum("conv_out", first=True)

                for hd in range(HR):
                    v.wait_ge(gn_sum.s, gn_sum.at(l, hd + 1))
                    o = oT[:, 2 * hd:2 * hd + 2, :]
                    stt(o, bank[4 + hd][:, 0:T].unsqueeze(1).broadcast_to([P, 2, T]), -1.0 / DV, o, ALU.mult, ALU.add).then_inc(gn_c.s, 1)
                for hd in range(HR):
                    v.wait_ge(gn_root.s, gn_root.at(l, hd + 1))
                    r = rsb[:, hd % 2, :]
                    o = oT[:, 2 * hd:2 * hd + 2, :]

                    tt(o, o, r.unsqueeze(1).broadcast_to([P, 2, T]), ALU.mult).then_inc(dve_step.s, steps.one())
                    v.wait_ge(dve_step.s, steps.n)
                    for m in (2 * hd, 2 * hd + 1):
                        ins = stt(oT[:, m, :], oT[:, m, :], col("g_rgn", m), rgs[:, m, :], ALU.mult, ALU.mult)
                    ins.then_inc(gn_y.s, 1)
                    v.wait_ge(gn_high.s, gn_high.at(l, hd + 1))
                    tt(s_lo[:, 2 * hd:2 * hd + 2, :], o, s_hi[:, 2 * hd:2 * hd + 2, :].bitcast(F32), ALU.subtract).then_inc(gn_low.s, 1)
                steps_restart()
                v.wait_ge(ret_stored.s, ret_stored.at(l, DMA))
                settle(v)
                gates("gate_b")
                gated_sum("ret_out")

                def kvq(m):
                    v.wait_ge(chunk_ready.s, chunk_ready.at(l, C0["kvq"] + m + 1))
                    tt(zt[:, m % 4, :], bank[(C0["kvq"] + m) % 4][:, 0:T], rstd[:, :], ALU.mult).then_inc(chunk_free.s, 1)

                for m in range(4):
                    kvq(m)
                for m in range(3):
                    v.wait_ge(kvq_act.s, kvq_act.at(l, m + 1))
                    ins = stt(qa_lo[:, m, :], zt[:, m, :], col("g_qa", m), qa_hi[:, m, :].bitcast(F32), ALU.mult, ALU.subtract)
                ins.then_inc(qa_low.s, 1)
                v.wait_ge(qa_low.s, qa_low.at(l, 1))
                kvq(4)
                kvq(5)
                for n in range(2):
                    v.wait_ge(kvq_root.s, kvq_root.at(l, n + 1))

                v.wait_ge(dve_step.s, steps.n)
                for c in range(2):
                    ins = stt(ckvT[:, c, :], zt[:, 3 if c == 0 else 0, :], col("g_kva", c), rsb[:, 1, :], ALU.mult, ALU.mult)
                ins.then_inc(ckv_ready.s, 1)
                pe_rows = slice(NOPE, QK)
                m_cos, m_sin = tb("mla_c", T, 0, pe_rows), tb("mla_s", T, 0, pe_rows)
                v.wait_ge(kr_rot.s, kr_rot.at(l, 1))
                tt(kpe_own[pe_rows, :], bank[6][pe_rows, 0:T], m_sin, ALU.mult).then_inc(dve_step.s, steps.one())
                tt(zt[pe_rows, 1, :], zt[pe_rows, 1, :], m_cos, ALU.mult).then_inc(dve_step.s, steps.one())
                v.wait_ge(dve_step.s, steps.n)
                tt(kpe_own[pe_rows, :], kpe_own[pe_rows, :], zt[pe_rows, 1, :], ALU.add).then_inc(kpe_ready.s, 1)

                def head_norm(k, buf, gain):
                    v.wait_ge(hn_root.s, hn_root.at(l, k + 1))
                    r = et[0:QK, k % 4, :]

                    stt(buf, buf, col(gain)[0:QK, :], r, ALU.mult, ALU.mult).then_inc(hn_done.s, 1)

                for step in range(HM + 4):
                    if step < HM:
                        c = C0["uq"] + step
                        v.wait_ge(chunk_ready.s, chunk_ready.at(l, c + 1))
                        tt(qm[0:QK, step, :], bank[c % 4][0:QK, 0:T], rsb[0:QK, 0, :], ALU.mult).then_inc(chunk_free.s, 1)
                    hd = step - 1
                    if 0 <= hd < HM:
                        v.wait_ge(uq_rot.s, uq_rot.at(l, hd + 1))
                        q = qm[pe_rows, hd, :]
                        tt(zt[pe_rows, hd % 4, :], bank[4 + hd % 2][pe_rows, 0:T], m_sin, ALU.mult).then_inc(dve_step.s, steps.one())
                        tt(q, q, m_cos, ALU.mult).then_inc(dve_step.s, steps.one())
                        v.wait_ge(dve_step.s, steps.n)
                        tt(q, q, zt[pe_rows, hd % 4, :], ALU.add).then_inc(q_roped.s, 1)
                    if step >= 4:
                        head_norm(step - 4, qm[0:QK, step - 4, :], "g_qn")
                for hd in range(HM):
                    head_norm(HM + hd, km[0:QK, hd, :], "g_kn")
                v.wait_ge(hn_done.s, hn_done.at(l, 2 * HM))
                qs = qm[0:QK, :, TP:T]
                tt(et[0:QK, 0, 0:64].rearrange("p (b h) -> p b h", b=NB), qs.rearrange("p h b -> p b h"),
                   km[0:QK, :, TP:T].rearrange("p h b -> p b h"), ALU.mult).then_inc(qs_ready.s, 1)
                v.tensor_scalar(et[0:QK, 1, 0:64].rearrange("p (h b) -> p h b", h=HM), qs, col("g_kn")[0:QK, :], None, ALU.mult)\
                    .then_inc(qs_ready.s, 1)
                v.wait_ge(qs_ready.s, qs_ready.at(l, 2))
                for q in range(4):
                    v.tensor_copy(qpe4[32 * q:32 * q + 32, :, :], et[pe_rows, 1, 0:64].rearrange("p (h b) -> p b h", h=HM)).then_inc(dve_step.s, steps.one())
                v.tensor_copy(ckv_own[:, :, :], ckvT[:, :, TP:T]).then_inc(dve_step.s, steps.one())
                v.wait_ge(dve_step.s, steps.n)
                v.wait_ge(qt_high.s, qt_high.at(l, 1))
                for c in range(2):
                    ins = tt(qt_lo[:, :, c, :], bank[7][:, c * 64:c * 64 + 64].rearrange("p (h b) -> p b h", h=HM),
                             qt_hi[:, :, c, :].bitcast(F32), ALU.subtract)
                ins.then_inc(qt_low.s, 1)

                def att_max(hd):
                    i = hd % 3
                    v.wait_ge(at_s.s, at_s.at(l, hd + 1))
                    if hd >= 3:
                        v.wait_ge(at_t.s, at_t.at(l, hd - 2))
                    tt(ap_s[i][:, :], bank[4 + hd % 2][:, 0:384], tb("mask", 384), ALU.add).then_inc(dve_step.s, steps.one())
                    v.wait_ge(dve_step.s, steps.n)
                    v.tensor_reduce(small[:, 0:1], ap_s[i][:, 0:P], AX.X, ALU.max).then_inc(dve_step.s, steps.one())
                    v.tensor_reduce(small[:, 1:2], ap_s[i][:, P:3 * P], AX.X, ALU.max).then_inc(dve_step.s, steps.one())
                    v.wait_ge(dve_step.s, steps.n)
                    v.tensor_scalar(small[:, 4 + 2 * i:6 + 2 * i], small[:, 0:2], -ATT_SCALE, None, ALU.mult).then_inc(at_m.s, 1)

                def att_div(hd):
                    i = hd % 3
                    sums = small[:, 12 + 2 * i:14 + 2 * i]
                    v.wait_ge(at_p.s, at_p.at(l, hd + 1))
                    v.reciprocal(sums, sums).then_inc(dve_step.s, steps.one())
                    v.wait_ge(dve_step.s, steps.n)
                    v.tensor_scalar(ap_s[i][:, 0:P], ap_s[i][:, 0:P], sums[:, 0:1], None, ALU.mult)
                    v.tensor_scalar(ap_s[i][:, P:3 * P], ap_s[i][:, P:3 * P], sums[:, 1:2], None, ALU.mult).then_inc(at_n.s, 1)

                att_max(0)
                att_max(1)
                for hd in range(HM):
                    att_div(hd)
                    if hd + 2 < HM:
                        att_max(hd + 2)
                v.wait_ge(uk_high.s, uk_high.at(l, 1))
                tt(uk_lo[:, :, 0:256], uk[:, :, 0:256], uk_hi[:, :, 0:256].bitcast(F32), ALU.subtract)
                tt(uk_lo[:, :, UKB], uk[:, :, 256:512], uk_hi[:, :, UKB].bitcast(F32), ALU.subtract).then_inc(uk_low.s, 1)

                def low(b, tp):
                    v.wait_ge(c_hi.s, c_hi.at(l, b * 8 + (tp + 1)))
                    tt(ct_lo[tp % 2][:, :, :], bank[4 + tp % 2][:, :].rearrange("p (q k) -> p q k", q=4),
                       ct_hi[tp % 2][:, :, :].bitcast(F32), ALU.subtract).then_inc(c_lo.s, 1)

                def front(b, i, tail, follows=True):
                    v.wait_ge(c_ksq.s, c_ksq.at(l, b + 1))
                    v.tensor_reduce(sspe[i][:, :], sq[0][:, :, :].rearrange("p h (a r) -> p (h a) r", r=ROPE), AX.X, ALU.add).then_inc(c_kss.s, 1)

                    for tp in range(NT // 2):
                        if tp < NT // 2 - 1:
                            low(b, tp + 1)
                        elif follows:
                            low(b + 1, 0)
                        for u in range(2):
                            t = 2 * tp + u
                            if t == 0:
                                v.wait_ge(c_pe.s, c_pe.at(l, b + 1))
                                v.tensor_copy(scores_pe[i][:, :, :].rearrange("p t h -> p (t h)"), bank[6][:, i * P:i * P + P]).then_inc(c_pec.s, 1)
                            v.wait_ge(c_sq.s, c_sq.at(l, b * NT + (t + 1)))
                            v.tensor_reduce(ssq[i][:, t, :], sq[u][:, :, :], AX.X, ALU.add).then_inc(c_ss.s, 1)
                        if tail is not None and tp in (0, 1, 3, 5, 6, 7):
                            tail_step(tail, (0, 1, 3, 5, 6, 7).index(tp))

                def tail_step(tail, step):
                    b, i = tail
                    if step == 0:
                        v.wait_ge(c_ss.s, c_ss.at(l, b * NT + NT))
                        v.wait_ge(c_kss.s, c_kss.at(l, b + 1))
                        tt(kn_r[:, :, :], ssq[i][:, :, :], sspe[i][:, :].unsqueeze(2).broadcast_to([P, NT, HM]), ALU.add)\
                            .then_inc(t_tot.s, 1)
                    elif step == 1:
                        v.wait_ge(t_root.s, t_root.at(l, b + 1))

                        v.wait_ge(c_sr.s, c_sr.at(l, b * NT + NT))
                        v.wait_ge(c_pec.s, c_pec.at(l, b + 1))
                        tt(scores[i][:, :, :], scores[i][:, :, :], scores_pe[i][:, :, :], ALU.add).then_inc(dve_step.s, steps.one())
                        v.wait_ge(dve_step.s, steps.n)
                        tt(sc[:, :, :], scores[i][:, :, :], kn_r[:, :, :], ALU.mult).then_inc(dve_step.s, steps.one())
                        v.wait_ge(dve_step.s, steps.n)
                        v.tensor_reduce(small[:, 0:8], sc[:, :, :].rearrange("p t h -> p h t"), AX.X, ALU.max).then_inc(t_mx.s, 1)
                    elif step == 2:
                        v.wait_ge(t_mt.s, t_mt.at(l, b + 1))
                        v.tensor_reduce(small[0:HM, 8:9], bank[7][0:HM, KVL:KVL + P], AX.X, ALU.max).then_inc(dve_step.s, steps.one())
                        v.wait_ge(dve_step.s, steps.n)
                        v.tensor_scalar(small[0:HM, 16:24], ident[0:HM, 0:HM], small[0:HM, 8:9], None, ALU.mult).then_inc(t_dg.s, 1)
                    elif step == 3:
                        v.wait_ge(t_bc.s, t_bc.at(l, b + 1))
                        o = flat(own[:, ds(b, 1), :])
                        m = small[:, 24:32]
                        tt(m, bank[7][:, 392:392 + HM], o, ALU.max).then_inc(dve_step.s, steps.one())
                        v.wait_ge(dve_step.s, steps.n)
                        tt(sc[:, :, :], sc[:, :, :], m.unsqueeze(1).broadcast_to([P, NT, HM]), ALU.subtract).then_inc(dve_step.s, steps.one())
                        tt(small[:, 32:40], o, m, ALU.subtract).then_inc(t_shift.s, 1)
                    elif step == 4:
                        v.wait_ge(t_p.s, t_p.at(l, b + 1))
                        v.tensor_reduce(small[:, 48:56], pr[:, :, :].rearrange("p t h -> p h t"), AX.X, ALU.add).then_inc(t_l.s, 1)
                    else:
                        v.wait_ge(t_tr.s, t_tr.at(l, b + 1))
                        tt(small[:, 56:64], bank[7][:, 400:400 + HM], small[:, 40:48], ALU.add).then_inc(dve_step.s, steps.one())
                        v.wait_ge(dve_step.s, steps.n)
                        v.reciprocal(small[:, 56:64], small[:, 56:64]).then_inc(dve_step.s, steps.one())
                        v.wait_ge(dve_step.s, steps.n)
                        for c in range(2):
                            stt(small[:, 64 + 8 * c:72 + 8 * c], small[:, 40:48], ckv_own[:, c, ds(b, 1)], bank[7][:, 408 + c * HM:416 + c * HM],
                                      ALU.mult, ALU.add).then_inc(dve_step.s, steps.one())
                        v.wait_ge(dve_step.s, steps.n)
                        for c in range(2):
                            ins = tt(lat[:, c, :, ds(b, 1)].rearrange("p h o -> p (h o)"), small[:, 64 + 8 * c:72 + 8 * c], small[:, 56:64], ALU.mult)
                        ins.then_inc(t_fin.s, 1)

                steps_restart()
                low(0, 0)
                front(0, 0, None)
                steps_restart()
                with v.Fori(0, 2) as j:
                    for u in range(3):
                        front(j * 3 + (u + 1), (u + 1) % 3, (j * 3 + u, u))
                    steps_restart()
                front(NB - 1, 1, (NB - 2, 0), follows=False)
                for step in range(6):
                    tail_step((NB - 1, 1), step)
                v.wait_ge(mla_high.s, mla_high.at(l, 1))
                tt(s_lo[:, 4:8, :], oM[:, :, :], s_hi[:, 4:8, :].bitcast(F32), ALU.subtract).then_inc(mla_split.s, 1)
                steps_restart()
                v.wait_ge(mla_split.s, mla_split.at(l, 1))
                settle(v)
                gates("gate_c")
                gated_sum("mla_out", mix_done)
                for k in range(KT):
                    v.wait_ge(mix_high.s, mix_high.at(l, k + 1))
                    tt(s_lo[:, k, :], mix[:, k, :], s_hi[:, k, :].bitcast(F32), ALU.subtract).then_inc(mix_low.s, 1)
                add_to_x("w_out")

                split_x(1, "g_ffn")
                settle(v)
                steps_restart()
                with v.Fori(0, 2 * FT // 4) as i:
                    def low(u):
                        v.wait_ge(ffn_high.s, ffn_high.at(l, i * 2 + (u + 1)))
                        tt(flat(a_lo[:, ds(i * 2 + u, 1), :]), zt[:, 2 * u, :], flat(a_hi[:, ds(i * 2 + u, 1), :]).bitcast(F32), ALU.subtract)\
                            .then_inc(ffn_low.s, 1)

                    for u in range(2):
                        g, up = 2 * u, 2 * u + 1
                        take("ffn_in", i, g)
                        take("ffn_in", i, up)
                        if u:
                            low(0)
                        sigmoid_there(i * 2 + (E0["ffn_in"] + u))
                        tt(zt[:, g, :], zt[:, g, :], et[:, g, :], ALU.mult).then_inc(dve_step.s, steps.one())
                        v.wait_ge(dve_step.s, steps.n)
                        taken("ffn_in", i, up)
                        tt(zt[:, g, :], zt[:, g, :], zt[:, up, :], ALU.mult).then_inc(ffn_a.s, 1)
                    low(1)
                    steps_restart()
                add_to_x("ffn_out")

                split_x(2, "g_ple")
                v.wait_ge(p_high.s, p_high.at(l, 1))
                tt(p_lo[:, :, :], p_raw[:, :, :], p_hi[:, :, :].bitcast(F32), ALU.subtract).then_inc(p_low.s, 1)
                gates("ple_gate")
                with v.Fori(0, 2) as i:
                    for r in range(4):
                        sigmoid_there(E0["ple_gate"] + KT - 1)
                        c = C0["ple_proj"] + r
                        x = flat(xT[:, ds(i * 4 + r, 1), :])
                        v.wait_ge(chunk_ready.s, chunk_ready.at(l, i * 4 + (c + 1)))
                        tt(zt[:, r, :], bank[c % 4][:, 0:T], flat(gate[:, ds(i * 4 + r, 1), :]), ALU.mult).then_inc(chunk_free.s, 1)
                        taken("ple_proj", i, r)
                        tt(x, x, zt[:, r, :], ALU.add).then_inc(dve_step.s, steps.one())
                    steps_restart()
            v.sem_inc(x_final.s, 1)


def constants():
    f = np.float32
    tab = np.zeros((P, NTAB), f)
    pos = np.concatenate([np.arange(TP), np.full(NB, PAST)]).astype(f)

    def angles(half):
        inv = np.power(f(10000.0), -np.arange(half, dtype=f) / f(half)).astype(f)
        ang = (inv[:, None] * pos[None, :]).astype(f)
        return np.cos(ang.astype(np.float64)), np.sin(ang.astype(np.float64))

    def put(name, a, rows=slice(0, P), off=0):
        tab[rows, TAB[name] + off:TAB[name] + off + a.shape[1]] = a

    c, s = angles(DK // 2)
    for i, factor in enumerate((1.0, DK ** -0.5)):
        put("rope_c", np.concatenate([c, c]) * factor, off=i * T)
        put("rope_s", np.concatenate([s, -s]) * factor, off=i * T)
    lg = np.log(1.0 - 2.0 ** (-5.0 - np.arange(HR, dtype=np.float64)))
    j, i = np.arange(P)[:, None], np.arange(P)[None, :]
    for h in range(HR):
        diag = np.where(i >= j, np.exp((i - j) * lg[h]), 0.0)
        put("decay", np.concatenate([diag, np.exp((i + P - j) * lg[h]), diag], 1), off=384 * h)
        for ch in range(2):
            put("kdec", np.exp((TP - 1 - (ch * P + np.arange(P))) * lg[h])[:, None], off=ch * HR + h)
    q, k = np.arange(P)[:, None], np.arange(P)[None, :]
    causal = np.where(k <= q, 0.0, -1e30)
    put("mask", np.concatenate([causal, np.zeros((P, P)), causal], 1))
    c, s = angles(ROPE // 2)
    put("mla_c", np.concatenate([np.ones((NOPE, T)), c, c]), slice(0, QK))
    put("mla_s", np.concatenate([np.zeros((NOPE, T)), s, s]), slice(0, QK))
    put("ident", np.eye(P))
    for r in range(3):
        put("pick3", np.eye(NB), slice(32 * r, 32 * r + NB))
    put("pick", np.tile(np.eye(NB).reshape(1, NB * NB), (P, 1)))
    put("ones", np.ones((P, P)))
    rot = np.zeros((QK, QK))
    half = ROPE // 2
    for a in range(half):
        rot[NOPE + half + a, NOPE + a] = -1.0
        rot[NOPE + a, NOPE + half + a] = 1.0
    put("rot", rot, slice(0, QK))
    return tab


def kernel(x_prompt, x_sample, p_prompt, p_sample, cache_ckv, cache_kpe, state_ret, state_conv, page_table,
           g_mix, w_in, w_dw, b_dw, g_cln, b_cln, w_conv_out, g_rgn, w_ret_out, g_qa, w_uq, g_qn, g_kva,
           w_uk, w_uv, g_kn, w_mla_out, w_out, g_ffn, w_gate, w_up, w_down, g_ple, w_ple_gate, w_ple_proj):
    import concourse.bacc as bacc
    from concourse.bass_utils import run_bass_kernel_spmd

    A = np.asarray

    def tiles(w):
        w = A(w)
        k, m = w.shape
        return w.reshape(k // P, P, m // P, P).transpose(2, 0, 1, 3)

    def blocks(t):
        t = t.reshape(-1, 8, P, P)
        return t.transpose(0, 2, 1, 3).reshape(-1, P, 8 * P)

    def paired(a, b):
        return np.stack([tiles(a), tiles(b)], 1).reshape(-1, KT, P, P)

    def layer_stream(l):
        w = A(w_in[l])
        c = np.cumsum([0, CONV, CONV, HR * DK, HR * DK, HR * DV, HR * DV, QL, KVL, ROPE, D, D, D])
        part = [w[:, c[i]:c[i + 1]] for i in range(len(c) - 1)]
        glu_a, glu_g, rq, rk, rv, rg, q_a, kv_a, _, ga, gb, gc = part
        kr = w[:, c[8] - NOPE:c[8] - NOPE + P]
        uq = A(w_uq[l]).reshape(3, P, HM, QK).transpose(1, 2, 0, 3).reshape(P, HM, 3 * QK)
        uq_blocks = []
        h = 0
        for n in UQ_HEADS:
            b = uq[:, h:h + n].reshape(P, n * 3 * QK)
            uq_blocks.append(np.concatenate([b, np.zeros((P, 8 * P - b.shape[1]), b.dtype)], 1))
            h += n
        return np.concatenate([
            blocks(paired(glu_a, glu_g)), blocks(tiles(rq)), blocks(tiles(rk)), blocks(tiles(rv)), blocks(tiles(rg)),
            blocks(tiles(ga)), blocks(tiles(w_conv_out[l])), blocks(tiles(gb)), blocks(tiles(w_ret_out[l])),
            blocks(tiles(q_a)), blocks(tiles(kv_a)), blocks(tiles(kr)), np.stack(uq_blocks),
            blocks(tiles(gc)), blocks(tiles(w_mla_out[l])), blocks(tiles(w_out[l])),
            blocks(paired(w_gate[l], w_up[l])), blocks(tiles(w_down[l])), blocks(tiles(w_ple_gate[l])), blocks(tiles(w_ple_proj[l])),
        ])

    def channel_major(prompt, sample, width):
        x = np.concatenate([A(prompt).reshape(TP, width), A(sample).reshape(NB, width)])
        return x.T.reshape(width // P, P, T).transpose(1, 0, 2)

    def vectors(l):
        def cols(g, n):
            g = A(g)
            if g.shape[0] < P:
                return np.concatenate([g, np.zeros(P - g.shape[0], g.dtype)]).reshape(P, 1)
            return g.reshape(n, P).T

        taps = A(w_dw[l]).T.reshape(CT, P, TAPS)
        taps = np.concatenate([taps, np.zeros((CT, P, 1), taps.dtype)], 2).transpose(1, 0, 2).reshape(P, CT * 32)
        return np.concatenate([cols(g_mix[l], KT), cols(g_ffn[l], KT), cols(g_ple[l], KT), taps, cols(b_dw[l], CT),
                               cols(g_cln[l], CT), cols(b_cln[l], CT), cols(g_rgn[l], KT), cols(g_qa[l], 3),
                               cols(g_kva[l], 2), cols(g_qn[l], 1), cols(g_kn[l], 1)], 1)

    L = range(DEPTH)
    n_phys = cache_ckv.shape[1]
    arrays = {
        "x": channel_major(x_prompt, x_sample, D),
        "p": np.stack([channel_major(p_prompt[l], p_sample[l], PLE) for l in L]),
        "stream": np.concatenate([layer_stream(l) for l in L]),
        "uk": np.stack([A(w_uk[l]).reshape(2, P, 512).transpose(1, 0, 2) for l in L]),
        "uv": np.stack([A(w_uv[l]).reshape(2, P, 512).transpose(1, 0, 2) for l in L]),
        "ukt": np.stack([A(w_uk[l]).reshape(KVL, HM, NOPE).transpose(2, 1, 0) for l in L]),
        "vec": np.stack([vectors(l) for l in L]).transpose(1, 0, 2),
        "tab": constants(),
        "cache": np.concatenate([A(cache_ckv), A(cache_kpe)], 3).reshape(DEPTH * n_phys, PAGE, KVL + ROPE),
        "pages": A(page_table).reshape(1, NB * NT),
        "state": A(state_ret).reshape(DEPTH * NB, HR, DK, DV),
        "conv": A(state_conv).reshape(DEPTH, NB, TAPS - 1, CT, P).transpose(0, 4, 3, 1, 2),
    }
    outs = {"y": (P, KT, T), "ckv_o": (DEPTH, P, 2, T), "kpe_o": (DEPTH, ROPE, T), "ret_p": (DEPTH, HR, DK, DV),
            "ret_s": (DEPTH * NB, HR, DK, DV), "conv_p": (DEPTH, P, CT, TAPS - 1), "conv_s": (DEPTH, P, CT, NB, TAPS - 1)}
    nc = bacc.Bacc("TRN2", target_bir_lowering=False, num_devices=1)
    arrays = {f"in_{k}": np.ascontiguousarray(a) for k, a in arrays.items()}
    args = [nc.dram_tensor(n, a.shape, mybir.dt.from_np(a.dtype), kind="ExternalInput").ap() for n, a in arrays.items()]
    args += [nc.dram_tensor(f"out_{n}", s, F32, kind="ExternalOutput").ap() for n, s in outs.items()]
    build(nc, *args)
    r = run_bass_kernel_spmd(nc, [arrays], core_ids=[0]).results[0]

    y = r["out_y"].transpose(2, 1, 0).reshape(T, D)
    ckv_o = r["out_ckv_o"].transpose(0, 3, 2, 1).reshape(DEPTH, T, KVL)
    kpe_o = r["out_kpe_o"].transpose(0, 2, 1)
    conv_p = r["out_conv_p"].transpose(0, 3, 2, 1).reshape(DEPTH, 1, TAPS - 1, CONV)
    conv_s = r["out_conv_s"].transpose(0, 3, 4, 2, 1).reshape(DEPTH, NB, TAPS - 1, CONV)
    return (y[:TP].reshape(1, TP, D), y[TP:].reshape(NB, 1, D),
            ckv_o[:, :TP].reshape(DEPTH, 1, TP, KVL), kpe_o[:, :TP].reshape(DEPTH, 1, TP, ROPE),
            ckv_o[:, TP:].reshape(DEPTH, NB, 1, KVL), kpe_o[:, TP:].reshape(DEPTH, NB, 1, ROPE),
            r["out_ret_p"].reshape(DEPTH, 1, HR, DK, DV), r["out_ret_s"].reshape(DEPTH, NB, HR, DK, DV), conv_p, conv_s)
```
